# Optimizing a Trainium2 kernel written in Bass

```python
import jax, jax.numpy as jnp
from jax import lax
import numpy as np

D_MODEL = 1024
BATCH = 1
SEQ = 128
DEPTH = 1
DEC_BATCH = 1
DEC_SEQ = 512
PAST_LEN = 256

GRID_W = 64
NA_HEADS = 8
HEAD_DIM = 64
NA_WIDTH = NA_HEADS * HEAD_DIM
WIN_ROWS = 8
WIN_COLS = 16
POOL_WINDOWS = (2, 4, 8, 16)
N_POOL_GROUPS = 4
POOL_GROUP_DIM = 128
POOL_WIDTH = N_POOL_GROUPS * POOL_GROUP_DIM
POOL_OUT_DIM = D_MODEL // N_POOL_GROUPS
N_EXPERTS = 16
CAPACITY_FACTOR = 2
D_EXPERT = 2752
N_MOD = 6
Q_BLOCK = 128
IN_WIDTH = 3 * NA_WIDTH + POOL_WIDTH + 2 * D_MODEL
EPS = 1e-6
NEG_INF = -1e30

kernel_name = "hybrid_na_pool_ecmoe_diffusion_step"

def rms_norm(x, g):
    x32 = x.astype(jnp.float32)
    y = x32 * lax.rsqrt(jnp.mean(x32 * x32, axis=-1, keepdims=True) + EPS)
    return (y * g.astype(jnp.float32)).astype(x.dtype)

def ada_mod(cond, w_ada, b_ada):
    m = jax.nn.silu(cond) @ w_ada + b_ada
    return jnp.split(m[:, None, :], N_MOD, axis=-1)

def mixer_projections(h, w_in, q_g, k_g):
    B, L, _ = h.shape
    p = h @ w_in
    cuts = [NA_WIDTH, 2 * NA_WIDTH, 3 * NA_WIDTH, 3 * NA_WIDTH + POOL_WIDTH,
            3 * NA_WIDTH + POOL_WIDTH + D_MODEL]
    q, k, v, u, ga, gb = jnp.split(p, cuts, axis=-1)
    q = rms_norm(q.reshape(B, L, NA_HEADS, HEAD_DIM), q_g)
    k = rms_norm(k.reshape(B, L, NA_HEADS, HEAD_DIM), k_g)
    v = v.reshape(B, L, NA_HEADS, HEAD_DIM)
    return q, k, v, u, ga, gb

def context_attention(q, k, v):
    B, L, H, dh = q.shape
    nblk = L // Q_BLOCK
    qb = q.reshape(B, nblk, Q_BLOCK, H, dh).transpose(1, 0, 2, 3, 4)

    def one_block(qblk):
        s = jnp.einsum('bqhd,bkhd->bhqk', qblk, k).astype(jnp.float32) * (HEAD_DIM ** -0.5)
        p = jax.nn.softmax(s, axis=-1)
        return jnp.einsum('bhqk,bkhd->bqhd', p.astype(v.dtype), v)

    o = lax.map(one_block, qb)
    return o.transpose(1, 0, 2, 3, 4).reshape(B, L, H * dh)

def latent_neighbourhood_attention(q, k, v, k_ctx, v_ctx, rpb):
    B, L, H, dh = q.shape
    rows = L // GRID_W
    kr = min(WIN_ROWS, rows)
    r = jnp.arange(rows)
    row_start = jnp.clip(r - kr // 2, 0, rows - kr)
    row_idx = row_start[:, None] + jnp.arange(kr)[None, :]
    qg = q.reshape(B, rows, GRID_W, H, dh)
    kg = k.reshape(B, rows, GRID_W, H, dh)[:, row_idx]
    vg = v.reshape(B, rows, GRID_W, H, dh)[:, row_idx]
    col = jnp.arange(GRID_W)
    col_start = jnp.clip(col - WIN_COLS // 2, 0, GRID_W - WIN_COLS)
    in_win = (col[None, :] >= col_start[:, None]) & (col[None, :] < col_start[:, None] + WIN_COLS)
    ro_idx = row_idx - r[:, None] + (WIN_ROWS - 1)
    co_idx = jnp.clip(col[None, :] - col[:, None], -(WIN_COLS - 1), WIN_COLS - 1) + (WIN_COLS - 1)
    bias = rpb[:, ro_idx[:, None, :, None], co_idx[None, :, None, :]].astype(jnp.float32)
    scale = HEAD_DIM ** -0.5
    s_loc = jnp.einsum('brqhd,brkwhd->bhrqkw', qg, kg).astype(jnp.float32) * scale + bias[None]
    s_loc = jnp.where(in_win[:, None, :], s_loc, NEG_INF)
    s_ctx = jnp.einsum('brqhd,bchd->bhrqc', qg, k_ctx).astype(jnp.float32) * scale
    n_loc = kr * GRID_W
    s = jnp.concatenate([s_loc.reshape(B, H, rows, GRID_W, n_loc), s_ctx], axis=-1)
    p = jax.nn.softmax(s, axis=-1)
    p_loc = p[..., :n_loc].reshape(B, H, rows, GRID_W, kr, GRID_W).astype(v.dtype)
    p_ctx = p[..., n_loc:].astype(v.dtype)
    o = (jnp.einsum('bhrqkw,brkwhd->brqhd', p_loc, vg)
         + jnp.einsum('bhrqc,bchd->brqhd', p_ctx, v_ctx))
    return o.reshape(B, L, H * dh)

def multiscale_pool(u, w_pool, pool_scale):
    B, L, _ = u.shape
    u32 = u.astype(jnp.float32).reshape(B, L, N_POOL_GROUPS, POOL_GROUP_DIM)
    cs = jnp.concatenate([jnp.zeros((B, 1, N_POOL_GROUPS, POOL_GROUP_DIM), jnp.float32),
                          jnp.cumsum(u32, axis=1)], axis=1)
    t = jnp.arange(L)[:, None]
    w = jnp.array(POOL_WINDOWS, jnp.int32)[None, :]
    lo = jnp.clip(t - w // 2, 0, L)
    hi = jnp.clip(t + w - w // 2, 0, L)
    gid = jnp.arange(N_POOL_GROUPS)[None, :]
    sums = cs[:, hi, gid] - cs[:, lo, gid]
    cnt = (hi - lo).astype(jnp.float32)[None, :, :, None]
    pooled = (sums / cnt - u32).astype(u.dtype)
    out = jnp.einsum('blgc,gcd->blgd', pooled, w_pool).reshape(B, L, D_MODEL)
    return out * pool_scale

def expert_choice_ffn(h, w_router, w_gate, w_up, w_down):
    B, L, D = h.shape
    n = B * L
    xt = h.reshape(n, D)
    aff = jax.nn.softmax((xt @ w_router).astype(jnp.float32), axis=-1)
    cap = max(1, (CAPACITY_FACTOR * n) // N_EXPERTS)
    g, idx = lax.top_k(aff.T, cap)
    xe = xt[idx]
    a = jnp.einsum('ecd,edf->ecf', xe, w_gate)
    b = jnp.einsum('ecd,edf->ecf', xe, w_up)
    ye = jnp.einsum('ecf,efd->ecd', jax.nn.silu(a) * b, w_down) * g[..., None].astype(h.dtype)
    out = jnp.zeros((n, D), h.dtype).at[idx.reshape(-1)].add(ye.reshape(-1, D))
    return out.reshape(B, L, D)

def trunk_layer(x, cond, p, k_ctx=None, v_ctx=None):
    sh1, sc1, g1, sh2, sc2, g2 = ada_mod(cond, p['w_ada'], p['b_ada'])
    h = rms_norm(x, p['norm1']) * (1 + sc1) + sh1
    q, k, v, u, ga, gb = mixer_projections(h, p['w_in'], p['q_g'], p['k_g'])
    if k_ctx is None:
        att = context_attention(q, k, v)
    else:
        att = latent_neighbourhood_attention(q, k, v, k_ctx, v_ctx, p['rpb'])
    o_a = att @ p['w_att_proj']
    o_b = multiscale_pool(u, p['w_pool'], p['pool_scale'])
    merged = jax.nn.sigmoid(ga) * o_a + jax.nn.sigmoid(gb) * o_b
    x = x + g1 * (merged @ p['w_out'])
    h = rms_norm(x, p['norm2']) * (1 + sc2) + sh2
    x = x + g2 * expert_choice_ffn(h, p['w_router'], p['w_gate_e'], p['w_up_e'], p['w_down_e'])
    return x, k, v

def setup_inputs(seed: int = 0) -> dict:
    key = jax.random.key(seed)
    ks = jax.random.split(key, 24)

    def nrm(k, shape, s):
        return jax.random.normal(k, shape, jnp.float32) * s

    return {
        'x_prompt': nrm(ks[0], (BATCH, SEQ, D_MODEL), 1.0),
        'x_sample': nrm(ks[1], (DEC_BATCH, DEC_SEQ, D_MODEL), 1.0),
        'cache_k': nrm(ks[2], (DEC_BATCH, DEPTH, PAST_LEN, NA_HEADS, HEAD_DIM), 1.0),
        'cache_v': nrm(ks[3], (DEC_BATCH, DEPTH, PAST_LEN, NA_HEADS, HEAD_DIM), 1.0),
        'c': nrm(ks[4], (DEC_BATCH, D_MODEL), 1.0),
        'c_ctx': nrm(ks[5], (D_MODEL,), 1.0),
        'norm1_g': 1.0 + nrm(ks[6], (DEPTH, D_MODEL), 0.02),
        'norm2_g': 1.0 + nrm(ks[7], (DEPTH, D_MODEL), 0.02),
        'w_ada': nrm(ks[8], (DEPTH, D_MODEL, N_MOD * D_MODEL), 0.5 * D_MODEL ** -0.5),
        'b_ada': nrm(ks[9], (DEPTH, N_MOD * D_MODEL), 0.02),
        'w_in': nrm(ks[10], (DEPTH, D_MODEL, IN_WIDTH), D_MODEL ** -0.5),
        'q_norm_g': 1.0 + nrm(ks[11], (DEPTH, HEAD_DIM), 0.02),
        'k_norm_g': 1.0 + nrm(ks[12], (DEPTH, HEAD_DIM), 0.02),
        'rpb': nrm(ks[13], (DEPTH, NA_HEADS, 2 * WIN_ROWS - 1, 2 * WIN_COLS - 1), 0.1),
        'w_att_proj': nrm(ks[14], (DEPTH, NA_WIDTH, D_MODEL), NA_WIDTH ** -0.5),
        'w_pool': nrm(ks[15], (DEPTH, N_POOL_GROUPS, POOL_GROUP_DIM, POOL_OUT_DIM), POOL_GROUP_DIM ** -0.5),
        'pool_scale': 1.0 + nrm(ks[16], (DEPTH, D_MODEL), 0.02),
        'w_out': nrm(ks[17], (DEPTH, D_MODEL, D_MODEL), D_MODEL ** -0.5),
        'w_router': nrm(ks[18], (DEPTH, D_MODEL, N_EXPERTS), D_MODEL ** -0.5),
        'w_gate_e': nrm(ks[19], (DEPTH, N_EXPERTS, D_MODEL, D_EXPERT), D_MODEL ** -0.5),
        'w_up_e': nrm(ks[20], (DEPTH, N_EXPERTS, D_MODEL, D_EXPERT), D_MODEL ** -0.5),
        'w_down_e': nrm(ks[21], (DEPTH, N_EXPERTS, D_EXPERT, D_MODEL), D_EXPERT ** -0.5),
    }

def reference(x_prompt, x_sample, cache_k, cache_v, c, c_ctx, norm1_g, norm2_g, w_ada, b_ada,
              w_in, q_norm_g, k_norm_g, rpb, w_att_proj, w_pool, pool_scale, w_out,
              w_router, w_gate_e, w_up_e, w_down_e):
    params = []
    for layer in range(DEPTH):
        params.append({
            'norm1': norm1_g[layer], 'norm2': norm2_g[layer],
            'w_ada': w_ada[layer], 'b_ada': b_ada[layer], 'w_in': w_in[layer],
            'q_g': q_norm_g[layer], 'k_g': k_norm_g[layer], 'rpb': rpb[layer],
            'w_att_proj': w_att_proj[layer], 'w_pool': w_pool[layer],
            'pool_scale': pool_scale[layer], 'w_out': w_out[layer],
            'w_router': w_router[layer], 'w_gate_e': w_gate_e[layer],
            'w_up_e': w_up_e[layer], 'w_down_e': w_down_e[layer],
        })

    y_prompt = x_prompt
    k_states, v_states = [], []
    for layer in range(DEPTH):
        y_prompt, k_l, v_l = trunk_layer(y_prompt, c_ctx[None, :], params[layer])
        k_states.append(k_l)
        v_states.append(v_l)
    state_k_ctx = jnp.stack(k_states, axis=1)
    state_v_ctx = jnp.stack(v_states, axis=1)

    y_sample = x_sample
    for layer in range(DEPTH):
        y_sample, _, _ = trunk_layer(y_sample, c, params[layer], cache_k[:, layer], cache_v[:, layer])

    return (y_prompt, y_sample, state_k_ctx, state_v_ctx)


_drawn_inputs = setup_inputs


def setup_inputs(seed=0):
    import zlib

    import numpy as np

    out = dict(_drawn_inputs(seed))
    spreads = {}
    factors = {'cache_k': 5.817,
     'cache_v': 4.794,
     'norm1_g': 2.865,
     'norm2_g': 8.0,
     'q_norm_g': 8.0,
     'k_norm_g': 3.116,
     'rpb': 200.0,
     'pool_scale': 8.0}
    for name, (base, spread) in spreads.items():
        noise = np.random.default_rng([zlib.crc32(name.encode()), seed]).standard_normal(out[name].shape)
        drawn = base * np.exp(spread * noise) if base else spread * noise
        out[name] = __import__('jax').numpy.asarray(drawn.astype(out[name].dtype))
    for name, factor in factors.items():
        out[name] = (out[name] * factor).astype(out[name].dtype)
    return out
```

```python
from contextlib import ExitStack

import numpy as np

import concourse.bass as bass
from concourse import mybir

D = 1024
KD = D // 128
LAT, CTX = 512, 128
TOK = LAT + CTX
NT = TOK // 128
GRID_W, GRID_R = 64, 8
H, DH = 8, 64
PAST = 256
NE = 16
F = 2752
CAP_L, CAP_C = 2 * LAT // NE, 2 * CTX // NE
SLOTS = CAP_L + CAP_C
FC = 512
NCH = -(-F // FC)
NFB = -(-F // 128)
RING = 9
SLOT = KD * 512
STREAM = 3
EPS = 1e-6
UNITS = 4 * H
WINDOW_BASE = (0, 8, 24, 32)
BIAS_VARIANT = (0, 1, 1, 2)
POOL_HALO = 8

ADA1 = [("ada", n) for n in range(4)]
QKV = [("in", 1), ("in", 0), ("in", 2)]
GATES = [("in", n) for n in range(3, 8)]
ADA2 = [("ada", n) for n in range(4, 12)]
TAIL = [("att", 0), ("out", 0), ("out", 1)]
CHUNKS = ADA1 + QKV + GATES + ADA2 + TAIL
C_QKV, C_GATES, C_ADA2, C_TAIL = 4, 7, 12, 20
USES = [len([i for i in range(len(CHUNKS)) if i % STREAM == s]) if s < STREAM else 0 for s in range(RING)]


def fblocks(c):
    width = min(FC, F - c * FC)
    return [(f, min(128, width - f)) for f in range(0, width, 128)]


def step_kernel(nc, a, out):
    f32 = mybir.dt.float32
    ALU = mybir.AluOpType
    ACT = mybir.ActivationFunctionType
    AX = mybir.AxisListType.X
    ds = bass.ds

    w_ada = a["w_ada"][0].rearrange("(k p) n -> p k n", p=128)
    w_in = a["w_in"][0].rearrange("(k p) n -> p k n", p=128)
    w_att = a["w_att_proj"][0].rearrange("(k p) n -> p k n", p=128)
    w_out = a["w_out"][0].rearrange("(k p) n -> p k n", p=128)
    w_gate = a["w_gate_e"][0].rearrange("e (k p) f -> e p k f", p=128)
    w_up = a["w_up_e"][0].rearrange("e (k p) f -> e p k f", p=128)
    w_down = a["w_down_e"][0]
    xs = a["x_sample"][0].rearrange("(r j c) d -> r c j d", r=GRID_R, j=4)
    ys = out["y_sample"][0].rearrange("(r j c) d -> r c j d", r=GRID_R, j=4)
    rpb_flat = a["rpb"][0].rearrange("h r c -> (h r c)").rearrange("(a n) -> a n", a=1)
    NR = H * 15 * 31

    with ExitStack() as ctx:
        def sb(name, shape):
            return ctx.enter_context(nc.sbuf_tensor(name, shape, f32))

        def sem(name):
            return ctx.enter_context(nc.semaphore(name))

        rpb_pad = nc.dram_tensor("rpb_pad", [1, NR + 32], f32, kind="Internal").ap()

        x = sb("x", [128, NT, D])
        xn2 = sb("xn2", [128, NT, D])
        ring = sb("ring", [128, RING * SLOT])
        misc = sb("misc", [128, 5104])
        keep = sb("keep", [128, 192])
        vecT = sb("vecT", [128, 90])
        modT = sb("modT", [128, 48, 2])
        scale1 = sb("scale1", [128, 8, 2])
        scale2 = sb("scale2", [128, 8, 2])
        aff_all = sb("aff", [128, NT, NE + 1])
        rankT = sb("rankT", [128, NT, NE + 1])
        small = sb("small", [128, 160])
        gate_slot = sb("gate_slot", [SLOTS, 1])

        aff = aff_all[:, :, 0:NE]
        slots = [ring[:, s * SLOT:(s + 1) * SLOT] for s in range(RING)]

        def at(buf, start, *shape):
            n = 1
            for s in shape:
                n *= s
            v = buf[:, start:start + n]
            if len(shape) == 2:
                return v.rearrange("p (a b) -> p a b", b=shape[1])
            if len(shape) == 3:
                return v.rearrange("p (a b c) -> p a b c", b=shape[1], c=shape[2])
            return v

        ident, iota = keep[:, 0:128], keep[:, 128:192]
        hT = xn2[:, :, :].rearrange("p a b -> p (a b)").rearrange("p (k t) -> p k t", k=KD)
        v_tok = at(ring, 12288, NT, 512)
        v_mid = at(ring, 14848, 3, 512)
        v_past = at(ring, 16384, 2, 512)
        qT = at(ring, 17408, 4, TOK)
        kT = at(ring, 19968, 4, TOK + PAST)
        rpb_wide = at(ring, 23552, H, GRID_R, 48)
        att = [at(ring, 26624, 512), at(ring, 35840, 512)]
        k_state = at(ring, 26624, H, DH)
        attT = at(ring, 27136, 4, TOK)
        k_past = at(ring, 27136, 2, 512)
        bias = at(ring, 29696, 3 * H, 32, GRID_R)
        gbT = at(ring, 12288, KD, TOK)
        pooledT = at(ring, 17408, 4, TOK)
        u_lat = at(ring, 19968, 4, LAT + 2 * POOL_HALO)
        u_ctx = at(ring, 22080, 4, CTX + 2 * POOL_HALO)
        win = [at(ring, 22656, LAT + 2 * POOL_HALO), at(ring, 23184, LAT + 2 * POOL_HALO)]
        w_pool = at(ring, 24576, 4, 256)
        gate1_row = at(ring, 29696, 2, D)
        gaT = at(ring, 31744, KD, TOK)
        rows = misc[0:90, 3072:3200]
        xn = [at(misc, 0, D), at(misc, 1024, D)]
        squares = [at(misc, 2048, 512), at(misc, 2560, 512)]
        normed = [at(misc, 3072, 512), at(misc, 3584, 512)]
        probs = [at(misc, 0, 512), at(misc, 512, 512)]
        probsT = [at(misc, 1024, 512), at(misc, 1536, 512)]
        diag = at(misc, 2048, 4, 128)
        gated = at(misc, 0, D)
        h2T = at(misc, 1024, KD, 128)
        square_junk = at(misc, 2048, D)
        mask = at(misc, 4096, 3, 32)
        pool_fix = at(misc, 4192, 4, 2, 8)
        ones = at(misc, 4256, 128)
        w_router = at(misc, 4384, KD, NE)
        kg_row = at(misc, 4512, DH)
        condT = at(misc, 4576, 2, KD)
        sigT = at(misc, 4592, 2 * KD)
        gT = at(misc, 4608, 1, 2)
        affN = misc[0:NE, 0:TOK]
        left = misc[0:NE, 640:640 + TOK]
        rank = misc[0:NE, 1280:1280 + TOK]
        rank_perm = misc[0:NE, 1920:1920 + TOK]
        top8 = misc[0:NE, 2560:2576]
        ones_row = misc[0:NE, 2600:2600 + LAT]
        xeT = at(misc, 0, KD, SLOTS)
        actT = at(misc, 640, NFB, SLOTS)
        yT = at(misc, 2400, KD, SLOTS)
        y_tok = misc[0:SLOTS, 3040:3040 + D]
        sig = [at(misc, 3040, 320), at(misc, 3360, 320)]
        sel = at(misc, 4064, NT, SLOTS)
        selT = misc[0:SLOTS, 4464:4464 + TOK]

        ss1, rs1 = small[:, 0:5], small[:, 5:10]
        ss_qk = [small[:, 16:24], small[:, 24:32]]
        rs_qk = [small[:, 32:40], small[:, 40:48]]
        negmax = small[:, 48:88]
        expsum = small[:, 88:128]
        negmax_c, expsum_c = small[:, 80:88], small[:, 120:128]
        ss2, rs2 = small[:, 128:133], small[:, 133:138]
        rmax, rsum = small[:, 138:143], small[:, 143:148]
        inv_sum = small[:, 148:156]

        ps = ctx.enter_context(nc.psum_tensor("ps", [128, 8, 512], f32))

        rows_loaded, consts_loaded, x_loaded = sem("rows_loaded"), sem("consts_loaded"), sem("x_loaded")
        past_loaded, pad_written, wide_loaded = sem("past_loaded"), sem("pad_written"), sem("wide_loaded")
        pool_loaded, mid_loaded, stored = sem("pool_loaded"), sem("mid_loaded"), sem("stored")
        kstate_stored = sem("kstate_stored")
        slot_loaded = [sem(f"slot_loaded{s}") for s in range(RING)]
        vec_done, vec_ready = sem("vec_done"), sem("vec_ready")
        squared1, ms1_ready, root1, x_normed = sem("squared1"), sem("ms1_ready"), sem("root1"), sem("x_normed")
        x_turned, h_copied, h_ready = sem("x_turned"), sem("h_copied"), sem("h_ready")
        cond_sig, cond_ready = sem("cond_sig"), sem("cond_ready")
        mod_done, mod_ready = sem("mod_done"), sem("mod_ready")
        past_turned, past_ready = sem("past_turned"), sem("past_ready")
        proj_done, qk_squared, qk_ms, qk_root = sem("proj_done"), sem("qk_squared"), sem("qk_ms"), sem("qk_root")
        qk_normed, qk_turned, qkT_ready = sem("qk_normed"), sem("qk_turned"), sem("qkT_ready")
        v_copied, kstate_ready = sem("v_copied"), sem("kstate_ready")
        bias_ready = sem("bias_ready")
        scores_done, max_ready, probs_ready = sem("scores_done"), sem("max_ready"), sem("probs_ready")
        probs_turned, probsT_ready, pv_done = sem("probs_turned"), sem("probsT_ready"), sem("pv_done")
        att_scaled, att_turned, attT_ready = sem("att_scaled"), sem("att_turned"), sem("attT_ready")
        halo_ready, gate_done, gate_copied = sem("halo_ready"), sem("gate_done"), sem("gate_copied")
        pooled_ready = sem("pooled_ready")
        diag_ready, row_done, row_copied = sem("diag_ready"), sem("row_done"), sem("row_copied")
        branches_done, merged = sem("branches_done"), sem("merged")
        out_done, x2_ready, squared2, ms2_ready, root2 = (sem("out_done"), sem("x2_ready"), sem("squared2"),
                                                          sem("ms2_ready"), sem("root2"))
        xn2_ready, xn2_turned, h2_ready, logits_done = (sem("xn2_ready"), sem("xn2_turned"), sem("h2_ready"),
                                                        sem("logits_done"))
        max2_ready, exp2_ready, aff_ready, aff_turned = (sem("max2_ready"), sem("exp2_ready"), sem("aff_ready"),
                                                         sem("aff_turned"))
        rank_ready, rank_turned = sem("rank_ready"), sem("rank_turned")
        dve_step = sem("dve_step")
        expert_chunk_used, slots_refilled = sem("expert_chunk_used"), sem("slots_refilled")
        sel_built, sel_turned, selT_ready = sem("sel_built"), sem("sel_turned"), sem("selT_ready")
        gathered, gathered_scaled, xe_ready = sem("gathered"), sem("gathered_scaled"), sem("xe_ready")
        sig_ready, silu_ready, act_ready = sem("sig_ready"), sem("silu_ready"), sem("act_ready")
        y_scaled, y_turned, y_tok_ready = sem("y_scaled"), sem("y_turned"), sem("y_tok_ready")
        slotgate_ready = sem("slotgate_ready")
        scattered, banks_free = sem("scattered"), sem("banks_free")

        block = ctx.enter_context(nc.Block())

        def chunk_read(i):
            if i < C_QKV:
                return mod_done, i + 1
            if i < C_GATES:
                return proj_done, NT * (i - C_QKV + 1)
            if i < C_ADA2:
                return gate_done, 4 * (i - C_GATES + 1)
            if i < C_TAIL:
                return mod_done, C_QKV + i - C_ADA2 + 1
            return (branches_done, KD) if i == C_TAIL else (out_done, NT)

        def chunk_slot(i):
            return slots[i % STREAM].rearrange("p (k n) -> p k n", n=512)

        def expert_dst(j):
            s = slots[j % RING]
            if j < 2 * NCH:
                width = min(FC, F - (j // 2) * FC)
                return s[:, 0:KD * width].rearrange("p (k f) -> p k f", f=width)
            return s.rearrange("p (b n) -> p b n", n=D)

        def expert_transfers(e, j):
            if j < 2 * NCH:
                c = j // 2
                w = (w_gate, w_up)[j % 2]
                width = min(FC, F - c * FC)
                return [(expert_dst(j), w[ds(e, 1), :, :, c * FC:c * FC + width].rearrange("e p k f -> (e p) k f"))]
            c = j - 2 * NCH
            full = [n for _, n in fblocks(c) if n == 128]
            part = [n for _, n in fblocks(c) if n < 128]
            moves = [(expert_dst(j)[:, 0:len(full), :], w_down[ds(e, 1), c * FC:c * FC + 128 * len(full), :]
                      .rearrange("e (b p) n -> (e p) b n", p=128))]
            if part:
                moves.append((expert_dst(j)[0:part[0], len(full), :],
                              w_down[ds(e, 1), F - part[0]:F, :].rearrange("e p n -> (e p) n")))
            return moves

        def load_expert(eng, e, j, free_at=None):
            moves = expert_transfers(e, j)
            if free_at is not None:
                eng.wait_ge(expert_chunk_used, free_at)
                eng.sem_inc(slots_refilled, 1)
            for dst, src in moves:
                eng.dma_start(dst, src).then_inc(slot_loaded[j % RING], 16)

        PARTED = (3 * NCH - 1) % RING

        def arrived(e, j):
            s = j % RING
            per_expert = 3 if s == PARTED else 2
            extra = per_expert if j >= RING else 1
            return e * (16 * per_expert) + 16 * (USES[s] + extra)

        @block.sync
        def _(sp):
            for r in range(GRID_R):
                sp.dma_start(x[r:128:GRID_R, 0:4, :], xs[r]).then_inc(x_loaded, 16)
            sp.dma_start(x[:, 4, :], a["x_prompt"][0]).then_inc(x_loaded, 16)
            for i, (kind, n) in enumerate(CHUNKS):
                if i >= STREAM:
                    sp.wait_ge(*chunk_read(i - STREAM))
                s = i % STREAM
                if kind == "att":
                    sp.dma_start(slots[s].rearrange("p (k n) -> p k n", n=D), w_att).then_inc(slot_loaded[s], 16)
                else:
                    w = {"ada": w_ada, "in": w_in, "out": w_out}[kind]
                    sp.dma_start(chunk_slot(i), w[:, :, n * 512:(n + 1) * 512]).then_inc(slot_loaded[s], 16)
                if i == 2:
                    sp.dma_start(k_past, a["cache_k"][0, 0].rearrange("(t p) h d -> p t (h d)", p=128)
                                 ).then_inc(past_loaded, 16)
                    sp.dma_start(v_past, a["cache_v"][0, 0].rearrange("(t p) h d -> p t (h d)", p=128)
                                 ).then_inc(past_loaded, 16)
                if i == C_QKV + 1:
                    sp.wait_ge(pad_written, 48)
                    for r in range(GRID_R):
                        for h in range(H):
                            src = bass.AP(rpb_pad.tensor, (h * 15 + 7 - r) * 31, [[1, 16], [31, GRID_R], [1, 48]])
                            sp.dma_start(rpb_wide[r:128:GRID_R, h], src).then_inc(wide_loaded, 16)
                if i == C_GATES + 1:
                    sp.wait_ge(bias_ready, 3)
                    sp.dma_start(w_pool, a["w_pool"][0].rearrange("g p n -> p g n")).then_inc(pool_loaded, 16)
            sp.wait_ge(merged, KD)
            for j in (3, 4, 5, 6):
                load_expert(sp, 0, j)
            sp.wait_ge(out_done, NT)
            for j in (0, 1, 2):
                load_expert(sp, 0, j)
            sp.wait_ge(x2_ready, NT)
            for j in (7, 8):
                load_expert(sp, 0, j)
            with sp.Fori(0, NE - 1) as e:
                for j in range(RING, 2 * RING):
                    load_expert(sp, e, j, free_at=e * (2 * RING) + j - RING + 1)
                for j in range(RING):
                    load_expert(sp, e + 1, j, free_at=e * (2 * RING) + j + RING + 1)
            for j in range(RING, 2 * RING):
                load_expert(sp, NE - 1, j, free_at=(NE - 1) * 2 * RING + j - RING + 1)
            sp.wait_ge(banks_free, 1 + NE * NT)
            for r in range(GRID_R):
                sp.dma_start(ys[r], x[r:128:GRID_R, 0:4, :]).then_inc(stored, 16)
            sp.dma_start(out["y_prompt"][0], x[:, 4, :]).then_inc(stored, 16)
            sp.wait_ge(stored, 16 * (GRID_R + 1 + 1))
            sp.wait_ge(kstate_stored, 16)

        @block.tensor
        def _(pe):
            mm, tr = nc.tensor.matmul, nc.tensor.transpose

            def chunk_arrived(i):
                pe.wait_ge(slot_loaded[i % STREAM], 16 * (i // STREAM + 1))

            pe.wait_ge(rows_loaded, 160)
            pe.wait_ge(consts_loaded, 64)
            tr(ps[:, 7, 0:90], rows, ident[0:90, 0:90]).then_inc(vec_done, 1)
            for t in range(NT):
                pe.wait_ge(x_normed, t + 1)
                if t >= 3:
                    pe.wait_ge(h_copied, t - 2)
                for k in range(KD):
                    last = tr(ps[:, 2 * (t % 3) + k // 4, k % 4 * 128:(k % 4 + 1) * 128],
                              xn[t % 2][:, k * 128:(k + 1) * 128], ident)
                last.then_inc(x_turned, 1)

            def modulation(i0, i1):
                for i in range(i0, i1):
                    chunk_arrived(i)
                    w = chunk_slot(i)
                    for b in range(4):
                        n = CHUNKS[i][1] * 4 + b
                        for k in range(KD):
                            last = mm(ps[:, 6, 2 * n:2 * n + 2], w[:, k, b * 128:(b + 1) * 128], condT[:, :, k],
                                      start=(k == 0), stop=(k == KD - 1))
                    last.then_inc(mod_done, 1)

            pe.wait_ge(cond_ready, 1)
            modulation(0, C_QKV)
            pe.wait_ge(past_loaded, 32)
            pe.wait_ge(vec_ready, 1)
            pe.wait_ge(h_copied, 4)
            for t in range(2):
                for i in range(4):
                    last = tr(ps[:, 7 * t, i * 128:(i + 1) * 128], k_past[:, t, i * 128:(i + 1) * 128], ident)
                last.then_inc(past_turned, 1)
            pe.wait_ge(h_copied, NT)
            pe.wait_ge(past_ready, 1)
            for i in range(3 * NT + 1):
                if i < 3 * NT:
                    if i % NT == 0:
                        chunk_arrived(C_QKV + i // NT)
                    if 4 <= i < 2 * NT + 4:
                        pe.wait_ge(qk_normed, i - 3)
                    elif i >= 2 * NT + 4:
                        pe.wait_ge(v_copied, i - 2 * NT - 3)
                    t, w = i % NT, chunk_slot(C_QKV + i // NT)
                    for k in range(KD):
                        if i == 0:
                            pe.wait_ge(h_ready, k + 1)
                        last = mm(ps[:, i % 4, :], hT[:, k, t * 128:(t + 1) * 128], w[:, k, :],
                                  start=(k == 0), stop=(k == KD - 1))
                    last.then_inc(proj_done, 1)
                if 1 <= i <= 2 * NT:
                    m = i - 1
                    pe.wait_ge(qk_normed, m + 1)
                    if m >= 2:
                        pe.wait_ge(qkT_ready, m - 1)
                    for hp in range(4):
                        last = tr(ps[:, 4 + m % 2, hp * 128:(hp + 1) * 128],
                                  normed[m % 2][:, hp * 128:(hp + 1) * 128], ident)
                    last.then_inc(qk_turned, 1)

            pe.wait_ge(v_copied, NT)
            pe.wait_ge(qkT_ready, 2 * NT)
            pe.wait_ge(past_ready, 2)
            pe.wait_ge(mid_loaded, 32)
            NU = UNITS + 2
            for u in range(NU + 3):
                if u < NU:
                    if u >= 3:
                        pe.wait_ge(probs_ready, u - 2)
                    if u < UNITS:
                        j, h = divmod(u, H)
                        hp, o = h // 2, h % 2 * DH
                        q = qT[o:o + DH, hp, j * 128:(j + 1) * 128]
                        b0 = WINDOW_BASE[j] * GRID_R
                        mm(ps[:, u % 3, 0:256], q, kT[o:o + DH, hp, b0:b0 + 256], start=True, stop=True)
                        last = mm(ps[:, u % 3, 256:512], q, kT[o:o + DH, hp, TOK:TOK + PAST], start=True, stop=True)
                    else:
                        for i in range(4):
                            h = 2 * i + u - UNITS
                            hp, o = h // 2, h % 2 * DH
                            last = mm(ps[:, u % 3, i * 128:(i + 1) * 128], qT[o:o + DH, hp, LAT:TOK],
                                      kT[o:o + DH, hp, LAT:TOK], start=True, stop=True)
                    last.then_inc(scores_done, 1)
                if 1 <= u <= NU:
                    m = u - 1
                    pe.wait_ge(probs_ready, m + 1)
                    if m >= 2:
                        pe.wait_ge(probsT_ready, m - 1)
                    for i in range(4):
                        last = tr(ps[:, 3 + m % 2, i * 128:(i + 1) * 128], probs[m % 2][:, i * 128:(i + 1) * 128], ident)
                    last.then_inc(probs_turned, 1)
                if 2 <= u <= NU + 1:
                    m = u - 2
                    pe.wait_ge(probsT_ready, m + 1)
                    j = m // H
                    if m % H == 0 and j >= 2:
                        pe.wait_ge(att_scaled, j - 1)
                    if m < UNITS:
                        h = m % H
                        vk = [[v_tok[:, 0], v_tok[:, 1]], [v_mid[:, 0], v_mid[:, 1]],
                              [v_mid[:, 1], v_mid[:, 2]], [v_tok[:, 2], v_tok[:, 3]]][j] + [v_past[:, 0], v_past[:, 1]]
                        for i in range(4):
                            last = mm(ps[:, 5 + j % 2, h * DH:(h + 1) * DH], probsT[m % 2][:, i * 128:(i + 1) * 128],
                                      vk[i][:, h * DH:(h + 1) * DH], start=(i == 0), stop=(i == 3))
                    else:
                        for i in range(4):
                            h = 2 * i + m - UNITS
                            last = mm(ps[:, 5, h * DH:(h + 1) * DH], probsT[m % 2][:, i * 128:(i + 1) * 128],
                                      v_tok[:, 4, h * DH:(h + 1) * DH], start=True, stop=True)
                    last.then_inc(pv_done, 1)
                if u >= 3 and (u - 3) % H == H - 1 or u == NU + 2:
                    j = min((u - 3) // H, 4)
                    pe.wait_ge(att_scaled, j + 1)
                    if j:
                        pe.wait_ge(attT_ready, j)
                    for i in range(4):
                        last = tr(ps[:, 7, i * 128:(i + 1) * 128], att[j % 2][:, i * 128:(i + 1) * 128], ident)
                    last.then_inc(att_turned, 1)

            pe.wait_ge(probs_ready, NU)
            pe.wait_ge(probsT_ready, NU)
            pe.wait_ge(att_scaled, 5)
            for i in range(20):
                c = C_GATES + i // 4
                if i % 4 == 0:
                    chunk_arrived(c)
                if i >= 3:
                    pe.wait_ge(gate_copied, 2 * (i - 2))
                w = chunk_slot(c)
                for k in range(KD):
                    lhsT = w[:, k, i % 4 * 128:(i % 4 + 1) * 128]
                    mm(ps[:, i % 3, :], lhsT, hT[:, k, 0:LAT], start=(k == 0), stop=(k == KD - 1))
                    last = mm(ps[:, 3 + i % 3, 0:CTX], lhsT, hT[:, k, LAT:TOK], start=(k == 0), stop=(k == KD - 1))
                last.then_inc(gate_done, 1)

            modulation(C_ADA2, C_TAIL)
            pe.wait_ge(attT_ready, 5)
            for i in range(4):
                pe.wait_ge(diag_ready, i + 1)
                if i:
                    pe.wait_ge(row_copied, i)
                mm(ps[:, 7, :], ones, diag, start=True, stop=True).then_inc(row_done, 1)
            chunk_arrived(C_TAIL)
            pe.wait_ge(pool_loaded, 16)
            pe.wait_ge(pooled_ready, 2 * 4)
            pe.wait_ge(gate_copied, 40)
            wa = slots[C_TAIL % STREAM].rearrange("p (k n) -> p k n", n=D)
            for n in range(KD):
                if n == 1:
                    pe.wait_ge(mod_ready, 1)
                    pe.wait_ge(row_copied, 4)
                if n >= 2:
                    pe.wait_ge(merged, n - 1)
                b = n % 2 * 4
                for k in range(4):
                    lhsT = wa[:, k, n * 128:(n + 1) * 128]
                    mm(ps[:, b, :], lhsT, attT[:, k, 0:LAT], start=(k == 0), stop=(k == 3))
                    last = mm(ps[:, b + 1, 0:CTX], lhsT, attT[:, k, LAT:TOK], start=(k == 0), stop=(k == 3))
                lhsT = w_pool[:, n // 2, n % 2 * 128:(n % 2 + 1) * 128]
                mm(ps[:, b + 2, :], lhsT, pooledT[:, n // 2, 0:LAT], start=True, stop=True)
                last2 = mm(ps[:, b + 3, 0:CTX], lhsT, pooledT[:, n // 2, LAT:TOK], start=True, stop=True)
                last2.then_inc(branches_done, 1)
            for i in range(2):
                chunk_arrived(C_TAIL + 1 + i)
            pe.wait_ge(merged, KD)
            for t in range(NT + 2):
                if t < NT:
                    if t >= 2:
                        pe.wait_ge(x2_ready, t - 1)
                    for half in range(2):
                        w = chunk_slot(C_TAIL + 1 + half)
                        for k in range(KD):
                            last = mm(ps[:, t % 2 * 2 + half, :], gaT[:, k, t * 128:(t + 1) * 128], w[:, k, :],
                                      start=(k == 0), stop=(k == KD - 1))
                    last.then_inc(out_done, 1)
                if 1 <= t <= NT:
                    m = t - 1
                    pe.wait_ge(xn2_ready, m + 1)
                    if m:
                        pe.wait_ge(h2_ready, m)
                    for k in range(KD):
                        last = tr(ps[:, 4 + k // 4, k % 4 * 128:(k % 4 + 1) * 128], xn2[:, m, k * 128:(k + 1) * 128],
                                  ident)
                    last.then_inc(xn2_turned, 1)
                    pe.wait_ge(h2_ready, m + 1)
                    for k in range(KD):
                        last = mm(ps[:, 6, m * NE:(m + 1) * NE], h2T[:, k, :], w_router[:, k, :],
                                  start=(k == 0), stop=(k == KD - 1))
                    last.then_inc(logits_done, 1)
            pe.wait_ge(aff_ready, 1)
            for t in range(NT):
                last = tr(ps[0:NE, 7 if t < 4 else 4, t % 4 * 128:(t % 4 + 1) * 128], aff[:, t, :], ident)
            last.then_inc(aff_turned, 1)
            pe.wait_ge(rank_ready, 1)
            for t in range(NT):
                last = tr(ps[:, 6, t * NE:(t + 1) * NE], rank_perm[:, t * 128:(t + 1) * 128], ident[0:NE, 0:NE])
            last.then_inc(rank_turned, 1)

            def gather():
                for d in range(KD):
                    for t in range(NT):
                        mm(ps[:, 6 + d // 4, d % 4 * SLOTS:(d % 4 + 1) * SLOTS], xn2[:, t, d * 128:(d + 1) * 128],
                           sel[:, t, :], start=(t == 0), stop=(t == NT - 1))
                for t in range(NT):
                    last = mm(ps[0:SLOTS, 7, 4 * SLOTS:4 * SLOTS + NE + 1], sel[:, t, :], aff_all[:, t, :],
                              start=(t == 0), stop=(t == NT - 1))
                last.then_inc(gathered, 1)

            pe.wait_ge(sel_built, 1)
            gather()

            with pe.Fori(0, NE) as e:
                pe.wait_ge(xe_ready, e + 1)
                pe.wait_ge(slotgate_ready, e + 1)
                for t in range(NT):
                    last = tr(ps[0:SLOTS, 6 + t // 4, t % 4 * 128:(t % 4 + 1) * 128], sel[:, t, :], ident)
                last.then_inc(sel_turned, 1)
                pe.wait_ge(banks_free, e * NT + 1)
                for c in range(NCH):
                    if c >= 2:
                        pe.wait_ge(act_ready, e * NCH + c - 1)
                    for g in range(2):
                        j = 2 * c + g
                        pe.wait_ge(slot_loaded[j % RING], arrived(e, j))
                        w = expert_dst(j)
                        for b, (f, n) in enumerate(fblocks(c)):
                            for k in range(KD):
                                last = mm(ps[0:n, 2 * g + c % 2, b * SLOTS:(b + 1) * SLOTS], w[:, k, f:f + n],
                                          xeT[:, k, :], start=(k == 0), stop=(k == KD - 1))
                        last.then_inc(expert_chunk_used, 1)
                for c in range(NCH):
                    j = 2 * NCH + c
                    pe.wait_ge(act_ready, e * NCH + c + 1)
                    pe.wait_ge(slot_loaded[j % RING], arrived(e, j))
                    w = expert_dst(j)
                    for b, (f, n) in enumerate(fblocks(c)):
                        fb = c * (FC // 128) + b
                        for d in range(KD):
                            last = mm(ps[:, 4 + d // 4, d % 4 * SLOTS:(d % 4 + 1) * SLOTS],
                                      w[0:n, b, d * 128:(d + 1) * 128], actT[0:n, fb, :],
                                      start=(fb == 0 and d % 4 == 0), stop=(fb == NFB - 1), skip_group_check=True)
                    last.then_inc(expert_chunk_used, 1)
                pe.wait_ge(selT_ready, e + 1)
                pe.wait_ge(sel_built, e + 2)
                gather()
                pe.wait_ge(y_scaled, e + 1)
                for d in range(KD):
                    last = tr(ps[0:SLOTS, d // 4, d % 4 * 128:(d % 4 + 1) * 128], yT[:, d, :], ident)
                last.then_inc(y_turned, 1)
                pe.wait_ge(y_tok_ready, e + 1)
                for t in range(NT):
                    if t >= 3:
                        pe.wait_ge(banks_free, e * NT + 1 + t - 2)
                    for half in range(2):
                        last = mm(ps[:, (2, 4, 0, 2, 4)[t] + half, :], selT[:, t * 128:(t + 1) * 128],
                                  y_tok[:, half * 512:(half + 1) * 512], start=True, stop=True)
                    last.then_inc(scattered, 1)

        @block.scalar
        def _(act):
            A = nc.scalar.activation
            pieces = [("c", 0), ("c_ctx", 8), ("norm1_g", 16), ("norm2_g", 24), ("pool_scale", 32), ("b_ada", 40)]
            for name, r in pieces:
                src = a[name] if name == "c_ctx" else a[name][0]
                act.dma_start(rows[r:r + src.shape[0] // 128, :], src.rearrange("(k p) -> k p", p=128)
                              ).then_inc(rows_loaded, 16)
            for i, name in enumerate(("q_norm_g", "k_norm_g")):
                for half in range(2):
                    act.dma_start(rows[88 + i:89 + i, half * DH:(half + 1) * DH], a[name]).then_inc(rows_loaded, 16)
            act.dma_start(keep[:, :], a["const_keep"]).then_inc(consts_loaded, 16)
            act.dma_start(misc[:, 4096:4256], a["const_mixer"]).then_inc(consts_loaded, 16)
            act.dma_start(kg_row, a["k_norm_g"].broadcast_to([128, DH])).then_inc(consts_loaded, 16)
            act.dma_start(w_router, a["w_router"][0].rearrange("(k p) n -> p k n", p=128)).then_inc(consts_loaded, 16)
            act.dma_start(rpb_pad[:, 16:16 + NR], rpb_flat).then_inc(pad_written, 16)
            act.dma_start(rpb_pad[:, 0:16], rpb_flat[:, 0:16]).then_inc(pad_written, 16)
            act.dma_start(rpb_pad[:, 16 + NR:32 + NR], rpb_flat[:, NR - 16:NR]).then_inc(pad_written, 16)
            act.wait_ge(x_loaded, 16 * (GRID_R + 1))
            for t in range(NT):
                A(xn[t % 2], x[:, t, :], ACT.Square, accum_out=ss1[:, t:t + 1]).then_inc(squared1, 1)
                act.wait_ge(squared1, t + 1)
            act.wait_ge(ms1_ready, 1)
            A(rs1, ss1, ACT.Sqrt).then_inc(root1, 1)
            act.wait_ge(vec_ready, 1)
            A(sigT, vecT[:, 0:2 * KD], ACT.Sigmoid).then_inc(cond_sig, 1)
            for t in range(NT):
                act.wait_ge(x_turned, t + 1)
                b = 2 * (t % 3)
                A(hT[:, :, t * 128:(t + 1) * 128].rearrange("p (a k) n -> p a k n", a=2),
                  ps[:, b:b + 2, :].rearrange("p a (k n) -> p a k n", n=128), ACT.Copy).then_inc(h_copied, 1)
            for t in range(2):
                act.wait_ge(past_turned, t + 1)
                A(kT[:, :, TOK + t * 128:TOK + (t + 1) * 128],
                  ps[:, 7 * t, :].rearrange("p (k n) -> p k n", n=128), ACT.Copy).then_inc(past_ready, 1)

            def turned_out(m):
                act.wait_ge(qk_turned, m + 1)
                dst = (kT, qT)[m // NT][:, :, m % NT * 128:(m % NT + 1) * 128]
                A(dst, ps[:, 4 + m % 2, :].rearrange("p (k n) -> p k n", n=128), ACT.Copy,
                  scale=gT[:, 0, 1 - m // NT:2 - m // NT]).then_inc(qkT_ready, 1)

            for i in range(3 * NT):
                act.wait_ge(proj_done, i + 1)
                if i < 2 * NT:
                    if i >= 2:
                        act.wait_ge(qk_ms, i - 1)
                    A(squares[i % 2], ps[:, i % 4, :], ACT.Square).then_inc(qk_squared, 1)
                    act.wait_ge(qk_ms, i + 1)
                    A(rs_qk[i % 2], ss_qk[i % 2], ACT.Sqrt).then_inc(qk_root, 1)
                else:
                    A(v_tok[:, i - 2 * NT, :], ps[:, i % 4, :], ACT.Copy).then_inc(v_copied, 1)
                if 1 <= i <= 2 * NT:
                    turned_out(i - 1)
            act.wait_ge(v_copied, NT)
            act.dma_start(v_mid[0:64], v_tok[64:128, 0:3, :]).then_inc(mid_loaded, 16)
            act.dma_start(v_mid[64:128], v_tok[0:64, 1:4, :]).then_inc(mid_loaded, 16)
            act.dma_start(out["state_v"], v_tok[:, 4, :]).then_inc(stored, 16)
            act.wait_ge(kstate_ready, 1)
            act.dma_start(out["state_k"], k_state.rearrange("p h d -> p (h d)")).then_inc(kstate_stored, 16)

            NU = UNITS + 2
            for u in range(NU + 1):
                if u < NU:
                    act.wait_ge(max_ready, u + 1)
                    if u >= 2:
                        act.wait_ge(probs_turned, u - 1)
                    if u < UNITS:
                        A(probs[u % 2], ps[:, u % 3, :], ACT.Exp, bias=negmax[:, u:u + 1],
                          accum_out=expsum[:, u:u + 1]).then_inc(probs_ready, 1)
                    else:
                        for i in range(4):
                            h = 2 * i + u - UNITS
                            last = A(probs[u % 2][:, i * 128:(i + 1) * 128], ps[:, u % 3, i * 128:(i + 1) * 128],
                                     ACT.Exp, bias=negmax_c[:, h:h + 1], accum_out=expsum_c[:, h:h + 1])
                        last.then_inc(probs_ready, 1)
                if u >= 1:
                    m = u - 1
                    act.wait_ge(probs_turned, m + 1)
                    if m >= 2:
                        act.wait_ge(pv_done, m - 1)
                    A(probsT[m % 2], ps[:, 3 + m % 2, :], ACT.Copy).then_inc(probsT_ready, 1)

            act.wait_ge(halo_ready, 2)
            act.wait_ge(attT_ready, 5)
            for i in range(20):
                act.wait_ge(gate_done, i + 1)
                lat, con = ps[:, i % 3, :], ps[:, 3 + i % 3, 0:CTX]
                if i < 4:
                    A(u_lat[:, i, POOL_HALO:POOL_HALO + LAT].rearrange("p (r c) -> p r c", c=GRID_W),
                      lat.rearrange("p (c r) -> p r c", r=GRID_R), ACT.Copy).then_inc(gate_copied, 1)
                    A(u_ctx[:, i, POOL_HALO:POOL_HALO + CTX], con, ACT.Copy).then_inc(gate_copied, 1)
                else:
                    g = (gaT if i < 12 else gbT)[:, (i - 4) % KD, :]
                    A(g[:, 0:LAT], lat, ACT.Sigmoid).then_inc(gate_copied, 1)
                    A(g[:, LAT:TOK], con, ACT.Sigmoid).then_inc(gate_copied, 1)
            for i in range(4):
                act.wait_ge(row_done, i + 1)
                A(gate1_row[:, i // 2, i % 2 * 512:(i % 2 + 1) * 512], ps[:, 7, :], ACT.Copy).then_inc(row_copied, 1)
            for t in range(NT):
                act.wait_ge(x2_ready, t + 1)
                A(square_junk, x[:, t, :], ACT.Square, accum_out=ss2[:, t:t + 1]).then_inc(squared2, 1)
                act.wait_ge(ms2_ready, t + 1)
                A(rs2[:, t:t + 1], ss2[:, t:t + 1], ACT.Sqrt).then_inc(root2, 1)
            act.wait_ge(max2_ready, 1)
            A(aff, aff, ACT.Exp).then_inc(exp2_ready, 1)

            with act.Fori(0, NE) as e:
                act.wait_ge(sel_turned, e + 1)
                A(selT[:, 0:LAT], ps[0:SLOTS, 6, :], ACT.Copy)
                A(selT[:, LAT:TOK], ps[0:SLOTS, 7, 0:CTX], ACT.Copy).then_inc(selT_ready, 1)
                for c in range(NCH):
                    n = SLOTS * len(fblocks(c))
                    act.wait_ge(expert_chunk_used, e * (3 * NCH) + 2 * c + 1)
                    if c >= 2:
                        act.wait_ge(act_ready, e * NCH + c - 1)
                    A(sig[c % 2][:, 0:n], ps[:, c % 2, 0:n], ACT.Sigmoid).then_inc(sig_ready, 1)
                act.wait_ge(y_turned, e + 1)
                A(y_tok, ps[0:SLOTS, 0:2, :].rearrange("p a n -> p (a n)"), ACT.Copy,
                  scale=gate_slot[:, 0:1]).then_inc(y_tok_ready, 1)

        @block.vector
        def _(dve):
            V = nc.vector
            steps = [0]

            def then(ins):
                steps[0] += 1
                ins.then_inc(dve_step, 1)
                dve.wait_ge(dve_step, steps[0])

            V.memset(ones, 1.0)
            V.memset(rankT[:, :, NE:NE + 1], -1.0)
            then(V.memset(aff_all[:, :, NE:NE + 1], 0.0))
            dve.wait_ge(squared1, NT)
            V.tensor_scalar(ss1, ss1, 1.0 / D, EPS, ALU.mult, ALU.add).then_inc(ms1_ready, 1)
            dve.wait_ge(root1, 1)
            then(V.reciprocal(rs1, rs1))
            for t in range(NT):
                if t >= 2:
                    dve.wait_ge(x_turned, t - 1)
                V.tensor_scalar(xn[t % 2], x[:, t, :], rs1[:, t:t + 1], None, ALU.mult).then_inc(x_normed, 1)
                if t == 0:
                    dve.wait_ge(vec_done, 1)
                    V.tensor_copy(vecT[:, :], ps[:, 7, 0:90]).then_inc(vec_ready, 1)
                    dve.wait_ge(vec_ready, 1)
                    V.tensor_scalar(gT[:, 0, 0:1], vecT[:, 88:89], DH ** -0.5, None, ALU.mult)
                    V.tensor_copy(gT[:, 0, 1:2], vecT[:, 89:90])
                if t == 1:
                    dve.wait_ge(cond_sig, 1)
                    V.tensor_tensor(condT.rearrange("p a k -> p (a k)"), sigT, vecT[:, 0:2 * KD], ALU.mult
                                    ).then_inc(cond_ready, 1)
            b_ada = vecT[:, 40:88]
            dve.wait_ge(mod_done, C_QKV)
            then(V.tensor_tensor(modT[:, 0:16, :], ps[:, 6, 0:32].rearrange("p (n c) -> p n c", c=2),
                                 b_ada[:, 0:16].unsqueeze(2).broadcast_to([128, 16, 2]), ALU.add))
            then(V.scalar_tensor_tensor(scale1[:, :, :], modT[:, 8:16, :], 1.0,
                                        vecT[:, 16:24].unsqueeze(2).broadcast_to([128, 8, 2]), ALU.add, ALU.mult))
            dve.wait_ge(h_copied, NT)
            for k in range(KD):
                V.tensor_scalar(hT[:, k, 0:LAT], hT[:, k, 0:LAT], scale1[:, k, 0:1], modT[:, k, 0:1], ALU.mult, ALU.add)
                V.tensor_scalar(hT[:, k, LAT:TOK], hT[:, k, LAT:TOK], scale1[:, k, 1:2], modT[:, k, 1:2],
                                ALU.mult, ALU.add).then_inc(h_ready, 1)
            for i in range(2 * NT):
                dve.wait_ge(qk_squared, i + 1)
                then(V.tensor_reduce(ss_qk[i % 2], squares[i % 2].rearrange("p (h d) -> p h d", d=DH), AX, ALU.add))
                V.tensor_scalar(ss_qk[i % 2], ss_qk[i % 2], 1.0 / DH, EPS, ALU.mult, ALU.add).then_inc(qk_ms, 1)
                dve.wait_ge(qk_root, i + 1)
                then(V.reciprocal(rs_qk[i % 2], rs_qk[i % 2]))
                if i >= 2:
                    dve.wait_ge(qk_turned, i - 1)
                V.tensor_tensor(normed[i % 2].rearrange("p (h d) -> p h d", d=DH),
                                ps[:, i % 4, :].rearrange("p (h d) -> p h d", d=DH),
                                rs_qk[i % 2].unsqueeze(2).broadcast_to([128, H, DH]), ALU.mult).then_inc(qk_normed, 1)
                if i == NT - 1:
                    dve.wait_ge(qk_normed, NT)
                    V.tensor_tensor(k_state, normed[i % 2].rearrange("p (h d) -> p h d", d=DH),
                                    kg_row.unsqueeze(1).broadcast_to([128, H, DH]), ALU.mult).then_inc(kstate_ready, 1)
            NU = UNITS + 2
            dve.wait_ge(bias_ready, 3)

            def finish_tile(j):
                dve.wait_ge(pv_done, min(H * (j + 1), NU))
                sums = expsum[:, j * H:(j + 1) * H]
                then(V.reciprocal(inv_sum, sums))
                if j == 0:
                    dve.wait_ge(kstate_stored, 16)
                if j >= 2:
                    dve.wait_ge(att_turned, j - 1)
                V.tensor_tensor(att[j % 2].rearrange("p (h d) -> p h d", d=DH),
                                ps[:, 5 + j % 2, :].rearrange("p (h d) -> p h d", d=DH),
                                inv_sum.unsqueeze(2).broadcast_to([128, H, DH]), ALU.mult).then_inc(att_scaled, 1)

            def copy_turned(j):
                dve.wait_ge(att_turned, j + 1)
                V.tensor_copy(attT[:, :, j * 128:(j + 1) * 128],
                              ps[:, 7, :].rearrange("p (k n) -> p k n", n=128)).then_inc(attT_ready, 1)

            for u in range(NU):
                dve.wait_ge(scores_done, u + 1)
                s = ps[:, u % 3, :]
                if u < UNITS:
                    j, h = divmod(u, H)
                    then(V.tensor_tensor(s[:, 0:256], s[:, 0:256],
                                         bias[:, BIAS_VARIANT[j] * H + h].rearrange("p c r -> p (c r)"), ALU.add))
                    V.tensor_reduce(negmax[:, u:u + 1], s, AX, ALU.max, negate=True).then_inc(max_ready, 1)
                else:
                    V.tensor_reduce(negmax_c[:, u - UNITS:H:2], s.rearrange("p (h n) -> p h n", n=128), AX, ALU.max,
                                    negate=True).then_inc(max_ready, 1)
                if u >= 10 and u % H == 2 and u < NU - 1:
                    finish_tile(u // H - 1)
                if u >= 12 and u % H == 5:
                    copy_turned(u // H - 1)
            finish_tile(3)
            copy_turned(3)
            finish_tile(4)
            copy_turned(4)

            V.memset(u_lat[:, :, :], 0.0).then_inc(halo_ready, 1)
            V.memset(u_ctx[:, :, :], 0.0).then_inc(halo_ready, 1)
            for g in range(4):
                dve.wait_ge(gate_copied, 2 * (g + 1))
                for u_set, L, order in ((u_lat, LAT, True), (u_ctx, CTX, False)):
                    u, c = u_set[:, g, :], POOL_HALO
                    w, reach = 1, POOL_HALO - 1
                    then(V.tensor_tensor(win[0][:, 1:L + 2 * c], u[:, 0:L + 2 * c - 1], u[:, 1:L + 2 * c], ALU.add))
                    lo, hi, cur = 1, L + 2 * c, 0
                    for n in range(g):
                        sh = 1 << n
                        then(V.tensor_tensor(win[1 - cur][:, lo + sh:hi - sh], win[cur][:, lo:hi - 2 * sh],
                                             win[cur][:, lo + 2 * sh:hi], ALU.add))
                        lo, hi, cur = lo + sh, hi - sh, 1 - cur
                    f = win[cur]
                    then(V.tensor_tensor(f[:, c:c + 8], f[:, c:c + 8], pool_fix[:, g, 0, :], ALU.mult))
                    then(V.tensor_tensor(f[:, c + L - 8:c + L], f[:, c + L - 8:c + L], pool_fix[:, g, 1, :], ALU.mult))
                    if order:
                        dst = pooledT[:, g, 0:LAT].rearrange("p (c r) -> p r c", r=GRID_R)
                        fi = f[:, c:c + L].rearrange("p (r c) -> p r c", c=GRID_W)
                        ui = u[:, c:c + L].rearrange("p (r c) -> p r c", c=GRID_W)
                    else:
                        dst, fi, ui = pooledT[:, g, LAT:TOK], f[:, c:c + L], u[:, c:c + L]
                    V.scalar_tensor_tensor(dst, fi, 1.0 / (2 << g), ui, ALU.mult, ALU.subtract).then_inc(pooled_ready, 1)
                    dve.wait_ge(pooled_ready, 2 * g + (1 if order else 2))
            dve.wait_ge(mod_done, C_QKV + len(ADA2))
            then(V.tensor_tensor(modT[:, 16:48, :], ps[:, 6, 32:96].rearrange("p (n c) -> p n c", c=2),
                                 b_ada[:, 16:48].unsqueeze(2).broadcast_to([128, 32, 2]), ALU.add))
            V.scalar_tensor_tensor(scale2[:, :, :], modT[:, 32:40, :], 1.0,
                                   vecT[:, 24:32].unsqueeze(2).broadcast_to([128, 8, 2]), ALU.add, ALU.mult
                                   ).then_inc(mod_ready, 1)
            for i in range(4):
                if i:
                    dve.wait_ge(row_done, i)
                cols = modT[:, 16 + i % 2 * 4:20 + i % 2 * 4, i // 2:i // 2 + 1]
                V.tensor_tensor(diag, ident.unsqueeze(1).broadcast_to([128, 4, 128]),
                                cols.broadcast_to([128, 4, 128]), ALU.mult).then_inc(diag_ready, 1)
            for n in range(KD):
                dve.wait_ge(branches_done, n + 1)
                b = n % 2 * 4
                for o, m, w in ((0, LAT, 0), (LAT, CTX, 1)):
                    V.tensor_tensor(gaT[:, n, o:o + m], gaT[:, n, o:o + m], ps[:, b + w, 0:m], ALU.mult)
                    then(V.scalar_tensor_tensor(gbT[:, n, o:o + m], ps[:, b + 2 + w, 0:m], vecT[:, 32 + n:33 + n],
                                                gbT[:, n, o:o + m], ALU.mult, ALU.mult))
                V.tensor_tensor(gaT[:, n, :], gaT[:, n, :], gbT[:, n, :], ALU.add).then_inc(merged, 1)
            dve.wait_ge(row_copied, 4)
            for t in range(NT):
                dve.wait_ge(out_done, t + 1)
                b, s = t % 2 * 2, int(t == 4)
                then(V.tensor_tensor(gated.rearrange("p (a n) -> p a n", a=2), ps[:, b:b + 2, :],
                                     gate1_row[:, s, :].rearrange("p (a n) -> p a n", a=2), ALU.mult))
                V.tensor_tensor(x[:, t, :], x[:, t, :], gated, ALU.add).then_inc(x2_ready, 1)
                dve.wait_ge(squared2, t + 1)
                V.tensor_scalar(ss2[:, t:t + 1], ss2[:, t:t + 1], 1.0 / D, EPS, ALU.mult, ALU.add
                                ).then_inc(ms2_ready, 1)
                dve.wait_ge(root2, t + 1)
                then(V.reciprocal(rs2[:, t:t + 1], rs2[:, t:t + 1]))
                V.tensor_scalar(xn2[:, t, :], x[:, t, :], rs2[:, t:t + 1], None, ALU.mult).then_inc(xn2_ready, 1)
                dve.wait_ge(xn2_turned, t + 1)
                if t:
                    dve.wait_ge(logits_done, t)
                h4 = h2T.rearrange("p (a k) n -> p a k n", a=2)
                then(V.tensor_tensor(h4, ps[:, 4:6, :].rearrange("p a (k n) -> p a k n", n=128),
                                     scale2[:, :, s:s + 1].rearrange("p (a k) o -> p a k o", a=2)
                                     .broadcast_to([128, 2, 4, 128]), ALU.mult))
                V.tensor_tensor(h2T, h2T, modT[:, 24:32, s:s + 1].broadcast_to([128, 8, 128]), ALU.add
                                ).then_inc(h2_ready, 1)
            dve.wait_ge(logits_done, NT)
            logits = ps[:, 6, 0:NT * NE].rearrange("p (t n) -> p t n", n=NE)
            then(V.tensor_reduce(rmax, logits, AX, ALU.max))
            V.tensor_tensor(aff, logits, rmax.unsqueeze(2).broadcast_to([128, NT, NE]), ALU.subtract
                            ).then_inc(max2_ready, 1)
            dve.wait_ge(exp2_ready, 1)
            then(V.tensor_reduce(rsum, aff, AX, ALU.add))
            then(V.reciprocal(rsum, rsum))
            V.tensor_tensor(aff, aff, rsum.unsqueeze(2).broadcast_to([128, NT, NE]), ALU.mult
                            ).then_inc(aff_ready, 1)
            V.memset(ones_row, 1.0)
            dve.wait_ge(aff_turned, 1)
            V.tensor_copy(affN[:, 0:LAT].rearrange("p (r c) -> p r c", c=GRID_W),
                          ps[0:NE, 7, :].rearrange("p (c r) -> p r c", r=GRID_R))
            then(V.tensor_copy(affN[:, LAT:TOK], ps[0:NE, 4, 0:CTX]))
            for o, m, cap in ((0, LAT, CAP_L), (LAT, CTX, CAP_C)):
                src, dst = affN[:, o:o + m], left[:, o:o + m]
                for n in range(cap // 8):
                    t8 = top8[:, 0:8]
                    then(V.max(t8, src))
                    then(V.match_replace(dst, t8, src, -1.0))
                    src = dst
            taken = affN
            then(V.tensor_scalar(taken, left, 0.0, None, ALU.is_lt))
            then(V.tensor_tensor_scan(rank[:, 0:LAT], ones_row, taken[:, 0:LAT], 0.0, ALU.mult, ALU.add))
            then(V.tensor_tensor_scan(rank[:, LAT:TOK], ones_row[:, 0:CTX], taken[:, LAT:TOK], 0.0, ALU.mult, ALU.add))
            then(V.tensor_tensor(rank, rank, taken, ALU.mult))
            then(V.tensor_scalar(rank_perm[:, 0:LAT].rearrange("p (c r) -> p r c", r=GRID_R),
                                 rank[:, 0:LAT].rearrange("p (r c) -> p r c", c=GRID_W), -1.0, None, ALU.add))
            V.tensor_scalar(rank_perm[:, LAT:TOK], rank[:, LAT:TOK], -1.0, None, ALU.add).then_inc(rank_ready, 1)
            dve.wait_ge(rank_turned, 1)
            V.tensor_copy(rankT[:, :, 0:NE], ps[:, 6, 0:NT * NE].rearrange("p (t n) -> p t n", n=NE)
                          ).then_inc(banks_free, 1)
            dve.wait_ge(banks_free, 1)
            then(V.memset(sel, 0.0))

            def build_selection(e):
                V.tensor_tensor(sel[:, 0:4, 0:CAP_L], iota.unsqueeze(1).broadcast_to([128, 4, CAP_L]),
                                rankT[:, 0:4, ds(e, 1)].broadcast_to([128, 4, CAP_L]), ALU.is_equal)
                V.tensor_tensor(sel[:, 4, CAP_L:SLOTS], iota[:, 0:CAP_C],
                                rankT[:, 4, ds(e, 1)].broadcast_to([128, CAP_C]), ALU.is_equal).then_inc(sel_built, 1)

            def take_gathered(e):
                X = ps[:, 6:8, 0:4 * SLOTS].rearrange("p a (k s) -> p a k s", s=SLOTS)
                xe4 = xeT.rearrange("p (a k) s -> p a k s", a=2)
                for s, (o, m) in enumerate(((0, CAP_L), (CAP_L, CAP_C))):
                    last = V.tensor_tensor(xe4[:, :, :, o:o + m], X[:, :, :, o:o + m],
                                           scale2[:, :, s:s + 1].rearrange("p (a k) o -> p a k o", a=2)
                                           .broadcast_to([128, 2, 4, m]), ALU.mult)
                last.then_inc(gathered_scaled, 1)
                dve.wait_ge(gathered_scaled, e + 1)
                for s, (o, m) in enumerate(((0, CAP_L), (CAP_L, CAP_C))):
                    last = V.tensor_tensor(xeT[:, :, o:o + m], xeT[:, :, o:o + m],
                                           modT[:, 24:32, s:s + 1].broadcast_to([128, 8, m]), ALU.add)
                last.then_inc(xe_ready, 1)

            def take_slot_gate(col):
                V.tensor_copy(gate_slot[:, :], ps[0:SLOTS, 7, ds(col + 4 * SLOTS, 1)]).then_inc(slotgate_ready, 1)

            build_selection(0)
            dve.wait_ge(gathered, 1)
            take_gathered(0)
            take_slot_gate(0)

            with dve.Fori(0, NE) as e:
                dve.wait_ge(sel_turned, e + 1)
                build_selection(e + 1)
                for c in range(NCH):
                    n = SLOTS * len(fblocks(c))
                    s = sig[c % 2][:, 0:n]
                    dve.wait_ge(sig_ready, e * NCH + c + 1)
                    V.tensor_tensor(s, s, ps[:, c % 2, 0:n], ALU.mult).then_inc(silu_ready, 1)
                    dve.wait_ge(silu_ready, e * NCH + c + 1)
                    dve.wait_ge(expert_chunk_used, e * (3 * NCH) + 2 * c + 2)
                    V.tensor_tensor(actT[:, 4 * c:4 * c + len(fblocks(c)), :].rearrange("p b s -> p (b s)"),
                                    s, ps[:, 2 + c % 2, 0:n], ALU.mult).then_inc(act_ready, 1)
                dve.wait_ge(expert_chunk_used, (e + 1) * (3 * NCH))
                Y = ps[:, 4:6, 0:4 * SLOTS].rearrange("p a (k s) -> p a k s", s=SLOTS)
                y4 = yT.rearrange("p (a k) s -> p a k s", a=2)
                for s, (o, m) in enumerate(((0, CAP_L), (CAP_L, CAP_C))):
                    last = V.tensor_tensor(y4[:, :, :, o:o + m], Y[:, :, :, o:o + m],
                                           modT[:, 40:48, s:s + 1].rearrange("p (a k) o -> p a k o", a=2)
                                           .broadcast_to([128, 2, 4, m]), ALU.mult)
                last.then_inc(y_scaled, 1)
                dve.wait_ge(gathered, e + 2)
                take_gathered(e + 1)
                dve.wait_ge(y_tok_ready, e + 1)
                take_slot_gate(e + 1)
                for t in range(NT):
                    dve.wait_ge(scattered, e * NT + t + 1)
                    b = (2, 4, 0, 2, 4)[t]
                    V.tensor_tensor(x[:, t, :].rearrange("p (a n) -> p a n", a=2),
                                    x[:, t, :].rearrange("p (a n) -> p a n", a=2), ps[:, b:b + 2, :], ALU.add
                                    ).then_inc(banks_free, 1)

        @block.gpsimd
        def _(pool):
            pool.wait_ge(wide_loaded, 16 * GRID_R * H)
            pool.wait_ge(consts_loaded, 64)
            for v in range(3):
                for h in range(H):
                    last = nc.gpsimd.tensor_tensor(
                        bias[:, v * H + h], rpb_wide[:, h, :, 8 * v:32 + 8 * v][:, :, ::-1].rearrange("p r c -> p c r"),
                        mask[:, v, :].unsqueeze(2).broadcast_to([128, 32, GRID_R]), ALU.add)
                last.then_inc(bias_ready, 1)


def _constants():
    keep = np.zeros((128, 192), np.float32)
    keep[:, 0:128] = np.eye(128)
    keep[:, 128:192] = np.arange(64)
    mixer = np.zeros((128, 160), np.float32)
    for v, (j, base) in enumerate(((0, 0), (1, 8), (3, 32))):
        qc = 16 * j + np.arange(128)[:, None] // 8
        kc = base + np.arange(32)[None, :]
        start = np.clip(qc - 8, 0, 48)
        mixer[:, v * 32:(v + 1) * 32] = np.where((kc >= start) & (kc < start + 16), 0.0, -1e30)
    fix = np.ones((4, 2, 8), np.float64)
    for g in range(4):
        w = 2 << g
        for i in range(8):
            fix[g, 0, i] = w / (i + w - w // 2 - max(i - w // 2, 0))
            fix[g, 1, i] = w / (min(i - 8 + w - w // 2, 0) - (i - 8 - w // 2))
    mixer[:, 96:160] = fix.reshape(1, 64)
    return {"const_keep": keep, "const_mixer": mixer}


_OUTS = {"y_prompt": (1, CTX, D), "y_sample": (1, LAT, D), "state_k": (CTX, H * DH), "state_v": (CTX, H * DH)}


def kernel(**inputs):
    import concourse.bacc as bacc
    from concourse.bass_utils import run_bass_kernel_spmd

    nc = bacc.Bacc("TRN2", target_bir_lowering=False, num_devices=1)
    arrays, a, out = {}, {}, {}
    inputs = {**inputs, "rpb": np.asarray(inputs["rpb"])[..., ::-1]}
    for name, v in {**inputs, **_constants()}.items():
        v = np.ascontiguousarray(v)
        arrays[f"in_{name}"] = v
        a[name] = nc.dram_tensor(f"in_{name}", v.shape, mybir.dt.from_np(v.dtype), kind="ExternalInput").ap()
    for name, shape in _OUTS.items():
        out[name] = nc.dram_tensor(f"out_{name}", shape, mybir.dt.float32, kind="ExternalOutput").ap()
    step_kernel(nc, a, out)
    r = run_bass_kernel_spmd(nc, [arrays], core_ids=[0]).results[0]
    state = (1, 1, CTX, H, DH)
    return (r["out_y_prompt"], r["out_y_sample"], r["out_state_k"].reshape(state), r["out_state_v"].reshape(state))
```

```python
from contextlib import ExitStack

import numpy as np

import concourse.bass as bass
from concourse import mybir

D = 1024
KD = D // 128
LAT, CTX = 512, 128
TOK = LAT + CTX
NT = TOK // 128
GRID_W, GRID_R = 64, 8
H, DH = 8, 64
PAST = 256
NE = 16
F = 2752
CAP_L, CAP_C = 2 * LAT // NE, 2 * CTX // NE
SLOTS = CAP_L + CAP_C
FC = 512
NCH = -(-F // FC)
NFB = -(-F // 128)
RING = 6
SLOT = KD * 512
PIECE = SLOT // 2
WBUF = 3
STREAM = 3
EPS = 1e-6
UNITS = 4 * H
WINDOW_BASE = (0, 8, 24, 32)
BIAS_VARIANT = (0, 1, 1, 2)
POOL_HALO = 8

ADA1 = [("ada", n) for n in range(4)]
QKV = [("in", 1), ("in", 0), ("in", 2)]
GATES = [("in", n) for n in range(3, 8)]
ADA2 = [("ada", n) for n in range(4, 12)]
TAIL = [("att", 0), ("out", 0), ("out", 1)]
CHUNKS = ADA1 + QKV + GATES + ADA2 + TAIL
C_QKV, C_GATES, C_ADA2, C_TAIL = 4, 7, 12, 20
H_EARLY = 5
H_CUT_AT = 24
GATE1_END = C_QKV + 2
USES = [len([i for i in range(len(CHUNKS)) if i % STREAM == s]) if s < STREAM else 0 for s in range(RING)]


def start(c):
    return 0 if c == 0 else F - (NCH - c) * FC


def width(c):
    return start(c + 1) - start(c) if c + 1 < NCH else FC


def fblocks(c):
    w = width(c)
    n = 128 if w % 128 == 0 else w // 2
    return [(f, n) for f in range(0, w, n)]


ORDER = [("gate", 0), ("up", 0)]
for _c in range(1, NCH):
    ORDER += [("gate", _c), ("up", _c), ("down", _c - 1)]
ORDER += [("down", NCH - 1)]
PIECES = []
for _j, (_kind, _c) in enumerate(ORDER):
    if _kind == "down":
        _n = len(fblocks(_c))
        PIECES += [(_j, _kind, _c, b, 2) for b in range(0, _n, 2)]
    elif width(_c) * KD <= PIECE:
        PIECES += [(_j, _kind, _c, 0, KD)]
    else:
        PIECES += [(_j, _kind, _c, b, KD // 2) for b in (0, KD // 2)]
NP = len(PIECES)
assert NP % WBUF == 0 and len(ORDER) % RING == 0
FIRST = {p[1:3]: min(i for i, q in enumerate(PIECES) if q[1:3] == p[1:3]) for p in PIECES}
LAST = {p[1:3]: max(i for i, q in enumerate(PIECES) if q[1:3] == p[1:3]) for p in PIECES}
SCALE_AT = 1
SCATTER_AT = 4


def step_kernel(nc, a, out):
    f32, f32r, u32 = mybir.dt.float32, mybir.dt.float32r, mybir.dt.uint32
    ALU = mybir.AluOpType
    ACT = mybir.ActivationFunctionType
    AX = mybir.AxisListType.X
    ds = bass.ds

    w_ada = a["w_ada"][0].rearrange("(k p) n -> p k n", p=128)
    w_in = a["w_in"][0].rearrange("(k p) n -> p k n", p=128)
    w_att = a["w_att_proj"][0].rearrange("(k p) n -> p k n", p=128)
    w_out = a["w_out"][0].rearrange("(k p) n -> p k n", p=128)
    w_gate = a["w_gate_e"][0].rearrange("e (k p) f -> e p k f", p=128)
    w_up = a["w_up_e"][0].rearrange("e (k p) f -> e p k f", p=128)
    w_down = a["w_down_e"][0]
    xs = a["x_sample"][0].rearrange("(r j c) d -> j c r d", r=GRID_R, j=4)
    ys = out["y_sample"][0].rearrange("(r j c) d -> j c r d", r=GRID_R, j=4)
    rpb_flat = a["rpb"][0].rearrange("h r c -> (h r c)").rearrange("(a n) -> a n", a=1)
    NR = H * 15 * 31

    with ExitStack() as ctx:
        top = [-(-nc.sbuf_base // 64) * 64]

        def place(name, offset, shape, dt=f32):
            return nc.alloc_sbuf_tensor_at(name, shape, dt, offset=offset)

        def sb(name, shape, dt=f32):
            n = 4 * int(np.prod(shape[1:]))
            top[0] += -(-n // 32) * 32
            return place(name, top[0] - -(-n // 32) * 32, shape, dt)

        def sem(name):
            return ctx.enter_context(nc.semaphore(name))

        rpb_pad = nc.dram_tensor("rpb_pad", [1, NR + 32], f32, kind="Internal").ap()
        xn_rows = nc.dram_tensor("xn_rows", [TOK, D], f32, kind="Internal").ap()

        x = sb("x", [128, NT, D])
        keep = sb("keep", [128, 128])
        vecT = sb("vecT", [128, 90])
        modT = sb("modT", [128, 48, 2])
        scale1 = sb("scale1", [128, 8, 2])
        scale2 = sb("scale2", [128, 8, 2])
        small = sb("small", [128, 160])
        gates = sb("gates", [SLOTS, NE + 1])
        places = sb("places", [SLOTS, NE + 2])
        places_int = sb("places_int", [SLOTS, NE + 2], u32)
        place_now = sb("place_now", [SLOTS, 1], u32)

        shared = top[0]
        ring = place("ring", shared, [128, RING * SLOT])
        behind = shared + 4 * RING * SLOT
        mixer = place("mixer", shared, [128, RING * SLOT + 2 * WBUF * PIECE])
        w_hi = place("w_hi", behind, [128, WBUF, PIECE], f32r)
        w_lo = place("w_lo", behind + 4 * WBUF * PIECE, [128, WBUF, PIECE], f32r)
        behind += 8 * WBUF * PIECE
        misc = place("misc", behind, [128, 4640])
        hT_all = place("hT_all", behind + 4 * 4640, [128, KD, TOK])
        mixer_r = place("mixer_r", shared, [128, RING * SLOT + 2 * WBUF * PIECE], f32r)
        misc_r = place("misc_r", behind, [128, 4640], f32r)
        hT_r = place("hT_r", behind + 4 * 4640, [128, KD, TOK], f32r)
        end_of_mixer = behind + 4 * (4640 + KD * TOK)
        top[0] = behind
        x_rows = sb("x_rows", [SLOTS, D])
        xe_hi = sb("xe_hi", [128, KD, SLOTS], f32r)
        xe_lo = sb("xe_lo", [128, KD, SLOTS], f32r)
        hid = sb("hid", [SLOTS, 2, FC])
        hT_hi = sb("hT_hi", [128, 2, 4, SLOTS], f32r)
        hT_lo = sb("hT_lo", [128, 2, 4, SLOTS], f32r)
        y_f = sb("y_f", [128, D])
        y_hi = sb("y_hi", [SLOTS, D], f32r)
        y_lo = sb("y_lo", [SLOTS, D], f32r)
        back = sb("back", [SLOTS, TOK], f32r)
        iota = sb("iota", [SLOTS, TOK])
        gate2_row = sb("gate2_row", [SLOTS, D])
        assert max(top[0], end_of_mixer) <= nc.sbuf_usable_end

        slots = [ring[:, s * SLOT:(s + 1) * SLOT] for s in range(RING)]
        stream = [mixer[:, s * SLOT:(s + 1) * SLOT] for s in range(STREAM)]
        xe_f = y_f[:, 0:KD * SLOTS].rearrange("p (k s) -> p k s", s=SLOTS)

        def at(buf, start, *shape):
            n = 1
            for s in shape:
                n *= s
            v = buf[:, start:start + n]
            if len(shape) == 2:
                return v.rearrange("p (a b) -> p a b", b=shape[1])
            if len(shape) == 3:
                return v.rearrange("p (a b c) -> p a b c", b=shape[1], c=shape[2])
            return v

        ident = keep[:, 0:128]
        hT = hT_all[:, :, :]
        v_tok = at(mixer, 12288, NT, 512)
        v_mid = at(mixer, 14848, 3, 512)
        v_past = at(mixer, 16384, 2, 512)
        qT = at(mixer, 17408, 4, TOK)
        kT = at(mixer, 19968, 4, TOK + PAST)
        rpb_wide = at(mixer, 23552, H, GRID_R, 48)
        att = [at(mixer, 26624, 512), at(mixer, 35840, 512)]
        k_state = at(mixer, 26624, H, DH)
        attT = at(mixer, 27136, 4, TOK)
        k_past = at(mixer, 27136, 2, 512)
        bias = at(mixer, 29696, 3 * H, 32, GRID_R)
        gbT = at(mixer, 12288, KD, TOK)
        pooledT = at(mixer, 17408, 4, TOK)
        u_lat = at(mixer, 19968, 4, LAT + 2 * POOL_HALO)
        u_ctx = at(mixer, 22080, 4, CTX + 2 * POOL_HALO)
        win = [at(mixer, 22656, LAT + 2 * POOL_HALO), at(mixer, 23184, LAT + 2 * POOL_HALO)]
        w_pool = at(mixer, 24576, 4, 256)
        gate1_row = at(mixer, 29696, 2, D)
        gaT = at(mixer, 31744, KD, TOK)
        h_hi = [at(mixer_r, 23712 + 512 * k if k < H_EARLY else 29696 + 512 * (k - H_EARLY), LAT) for k in range(KD)]
        h_lo = hT_r[:, :, 0:LAT]
        block_hi = [at(misc_r, 0, KD, 128), at(misc_r, 1024, KD, 128)]
        block_lo = [at(misc_r, 2048, KD, 128), at(misc_r, 3072, KD, 128)]
        merged_hi, merged_lo = [place(name, shared + 4 * o, [128, KD, TOK], f32r)[:, :, :]
                                for name, o in (("merged_hi", 12288), ("merged_lo", 31744))]
        out_hi = [place(f"out_hi{half}", shared + 4 * o, [128, KD, 512], f32r)[:, :, :]
                  for half, o in enumerate((19968, 25600))]
        out_lo = [place(f"out_lo{half}", shared + 4 * SLOT * ((C_TAIL + 1 + half) % STREAM), [128, KD, 512], f32r)
                  [:, :, :] for half in range(2)]
        rows = misc[0:90, 3072:3200]
        xn = [at(misc, 0, D), at(misc, 1024, D)]
        squares = [at(misc, 2048, 512), at(misc, 2560, 512)]
        normed = [at(misc, 3072, 512), at(misc, 3584, 512)]
        probs = [at(misc, 0, 512), at(misc, 512, 512)]
        mod_row = at(misc, 2048, 2, 512)
        q_apart = misc[:, 2048:4096].rearrange("p (b o h n) -> p b o h n", b=2, o=2, h=4)
        probsT = [at(misc, 1024, 512), at(misc, 1536, 512)]
        diag = at(misc, 3072, 4, 128)
        diag2 = [at(misc, 2048, 4, 128), at(misc, 2560, 4, 128)]
        gated = at(misc, 0, D)
        h2T = at(misc, 1024, KD, 128)
        square_junk = at(misc, 2048, D)
        mask = at(misc, 4096, 3, 32)
        pool_fix = at(misc, 4192, 4, 2, 8)
        ones = at(misc, 4256, 128)
        slot_sets = at(misc, 4384, 2, SLOTS)
        condT = at(misc, 4544, 2, KD)
        sigT = at(misc, 4560, 2 * KD)
        gT = at(misc, 4576, 1, 2)
        kg_row = at(mixer, 36352, DH)
        w_router = at(hT_all.rearrange("p k t -> p (k t)"), 0, KD, NE)
        xn2 = [at(hT_all.rearrange("p k t -> p (k t)"), 1024 * (1 + i), D) for i in range(2)]
        aff = at(hT_all.rearrange("p k t -> p (k t)"), 3072, NT, NE)
        affN = misc[0:NE, 0:TOK]
        left = misc[0:NE, 640:640 + TOK]
        best = misc[0:NE, 1280:1280 + SLOTS]
        best_place = misc[0:NE, 1360:1360 + SLOTS]
        found = misc[0:NE, 1440:1440 + SLOTS].bitcast(u32)
        found_col = misc[0:NE, 1520:1520 + SLOTS].bitcast(u32)

        ss1, rs1 = small[:, 0:5], small[:, 5:10]
        ss_qk = [small[:, 16:24], small[:, 24:32]]
        rs_qk = [small[:, 32:40], small[:, 40:48]]
        negmax = small[:, 48:88]
        expsum = small[:, 88:128]
        negmax_c, expsum_c = small[:, 80:88], small[:, 120:128]
        ss2, rs2 = small[:, 128:133], small[:, 133:138]
        rmax, rsum = small[:, 138:143], small[:, 143:148]
        inv_sum = small[:, 148:156]

        ps = ctx.enter_context(nc.psum_tensor("ps", [128, 8, 512], f32))

        rows_loaded, consts_loaded = sem("rows_loaded"), sem("consts_loaded")
        x_loaded = [sem(f"x_loaded{t}") for t in range(NT)]
        past_loaded, pad_written, wide_loaded = sem("past_loaded"), sem("pad_written"), sem("wide_loaded")
        pool_loaded, mid_loaded, stored = sem("pool_loaded"), sem("mid_loaded"), sem("stored")
        kstate_stored = sem("kstate_stored")
        slot_loaded = [sem(f"slot_loaded{s}") for s in range(RING)]
        cond_loaded, cond_turned = sem("cond_loaded"), sem("cond_turned")
        vec_done, vec_ready = sem("vec_done"), sem("vec_ready")
        squared1, ms1_ready, root1, x_normed = sem("squared1"), sem("ms1_ready"), sem("root1"), sem("x_normed")
        x_turned, h_copied, h_ready = sem("x_turned"), sem("h_copied"), sem("h_ready")
        cond_sig, cond_ready = sem("cond_sig"), sem("cond_ready")
        mod_done, mod_copied, mod_turned = sem("mod_done"), sem("mod_copied"), sem("mod_turned")
        mod_ready, q_spread = sem("mod_ready"), sem("q_spread")
        diag2_ready, row2_done = sem("diag2_ready"), sem("row2_done")
        past_turned, past_ready = sem("past_turned"), sem("past_ready")
        proj_done, qk_squared, qk_ms, qk_root = sem("proj_done"), sem("qk_squared"), sem("qk_ms"), sem("qk_root")
        qk_normed, qk_turned, qkT_ready = sem("qk_normed"), sem("qk_turned"), sem("qkT_ready")
        v_copied, kstate_ready = sem("v_copied"), sem("kstate_ready")
        bias_ready = sem("bias_ready")
        scores_done, max_ready, probs_ready = sem("scores_done"), sem("max_ready"), sem("probs_ready")
        probs_turned, probsT_ready, pv_done = sem("probs_turned"), sem("probsT_ready"), sem("pv_done")
        att_scaled, att_turned, attT_ready = sem("att_scaled"), sem("att_turned"), sem("attT_ready")
        h_cut_high, h_cut, block_high, block_cut = (sem("h_cut_high"), sem("h_cut"), sem("block_high"),
                                                    sem("block_cut"))
        halo_ready, gate_done, gate_copied = sem("halo_ready"), sem("gate_done"), sem("gate_copied")
        pooled_ready = sem("pooled_ready")
        diag_ready, row_done, row_copied = sem("diag_ready"), sem("row_done"), sem("row_copied")
        branches_done, merged = sem("branches_done"), sem("merged")
        merged_high, merged_cut = sem("merged_high"), sem("merged_cut")
        out_high, out_cut = sem("out_high"), sem("out_cut")
        out_done, x2_ready, squared2, ms2_ready, root2 = (sem("out_done"), sem("x2_ready"), sem("squared2"),
                                                          sem("ms2_ready"), sem("root2"))
        xn2_ready, xn2_turned, h2_ready, logits_done = (sem("xn2_ready"), sem("xn2_turned"), sem("h2_ready"),
                                                        sem("logits_done"))
        max2_ready, exp2_ready, aff_ready, aff_turned = (sem("max2_ready"), sem("exp2_ready"), sem("aff_ready"),
                                                         sem("aff_turned"))
        best_ready, best_turned = sem("best_ready"), sem("best_turned")
        router_loaded = sem("router_loaded")
        rows_saved = [sem("rows_saved0"), sem("rows_saved1")]
        gate2_ready, iota_loaded = sem("gate2_ready"), sem("iota_loaded")
        dve_step, pool_step = sem("dve_step"), sem("pool_step")
        hi_ready, lo_ready, pieces_used = sem("hi_ready"), sem("lo_ready"), sem("pieces_used")
        slots_refilled, gathers_begun = sem("slots_refilled"), sem("gathers_begun")
        place_ready, gathered, xe_turned = sem("place_ready"), sem("gathered"), sem("xe_turned")
        xe_scaled, xe_mod, xe_high, xe_ready = sem("xe_scaled"), sem("xe_mod"), sem("xe_high"), sem("xe_ready")
        silu_ready, h_done, h_turned = sem("silu_ready"), sem("h_done"), sem("h_turned")
        h_high, hT_ready = sem("h_high"), sem("hT_ready")
        y_scaled, y_high, y_ready = sem("y_scaled"), sem("y_high"), sem("y_ready")
        back_ready, scattered, added = sem("back_ready"), sem("scattered"), sem("added")

        block = ctx.enter_context(nc.Block())

        def chunk_read(i):
            if i < C_QKV:
                return mod_done, i + 1
            if i < C_GATES:
                return proj_done, NT * (i - C_QKV + 1)
            if i < C_ADA2:
                return gate_done, 4 * (i - C_GATES + 1)
            if i < C_TAIL:
                return mod_done, C_QKV + i - C_ADA2 + 1
            return (branches_done, KD) if i == C_TAIL else (out_done, 2 * NT)

        def chunk_slot(i):
            return stream[i % STREAM].rearrange("p (k n) -> p k n", n=512)

        def expert_dst(j):
            kind, c = ORDER[j]
            n = D if kind == "down" else width(c)
            blocks = len(fblocks(c)) if kind == "down" else KD
            return slots[j % RING][:, 0:blocks * n].rearrange("p (b n) -> p b n", n=n)

        def load_expert(eng, e, j, free_at=None):
            kind, c = ORDER[j]
            dst = expert_dst(j)
            if free_at is not None:
                eng.wait_ge(lo_ready, free_at)
                eng.sem_inc(slots_refilled, 1)
            if kind == "down":
                n = fblocks(c)[0][1]
                dst = dst[0:n]
                src = w_down[ds(e, 1), start(c):start(c) + width(c), :].rearrange("e (b p) n -> (e p) b n", p=n)
            else:
                w = w_gate if kind == "gate" else w_up
                src = w[ds(e, 1), :, :, start(c):start(c) + width(c)].rearrange("e p k f -> (e p) k f")
            eng.dma_start(dst, src).then_inc(slot_loaded[j % RING], 16)

        def arrived(e, j):
            return e * (16 * (len(ORDER) // RING)) + 16 * (USES[j % RING] + j // RING + 1)

        def piece_shape(p):
            j, kind, c, b0, nb = PIECES[p]
            return (fblocks(c)[0][1], nb * D) if kind == "down" else (128, nb * width(c))

        def piece(p):
            j, kind, c, b0, nb = PIECES[p]
            return expert_dst(j)[0:piece_shape(p)[0], b0:b0 + nb, :].rearrange("p b n -> p (b n)")

        def pieces_before(j):
            return len([p for p in PIECES if p[0] < j])

        @block.sync
        def _(sp):
            def load_x(t):
                src = xs[t] if t < 4 else a["x_prompt"][0]
                sp.dma_start(x[:, t, :], src).then_inc(x_loaded[t], 16)

            sp.dma_start(rows[KD:2 * KD, :], a["c_ctx"].rearrange("(k p) -> k p", p=128)).then_inc(cond_loaded, 16)
            load_x(0)
            for i, (kind, n) in enumerate(CHUNKS):
                if i >= STREAM:
                    sp.wait_ge(*chunk_read(i - STREAM))
                s = i % STREAM
                if kind == "att":
                    sp.dma_start(stream[s].rearrange("p (k n) -> p k n", n=D), w_att).then_inc(slot_loaded[s], 16)
                else:
                    w = {"ada": w_ada, "in": w_in, "out": w_out}[kind]
                    sp.dma_start(chunk_slot(i), w[:, :, n * 512:(n + 1) * 512]).then_inc(slot_loaded[s], 16)
                if i < 2:
                    load_x(2 * i + 1)
                    load_x(2 * i + 2)
                if i == 2:
                    sp.dma_start(k_past, a["cache_k"][0, 0].rearrange("(t p) h d -> p t (h d)", p=128)
                                 ).then_inc(past_loaded, 16)
                    sp.dma_start(v_past, a["cache_v"][0, 0].rearrange("(t p) h d -> p t (h d)", p=128)
                                 ).then_inc(past_loaded, 16)
                if i == C_QKV + 1:
                    sp.wait_ge(pad_written, 48)
                    for r in range(GRID_R):
                        for h in range(H):
                            src = bass.AP(rpb_pad.tensor, (h * 15 + 7 - r) * 31, [[1, 16], [31, GRID_R], [1, 48]])
                            sp.dma_start(rpb_wide[r:128:GRID_R, h], src).then_inc(wide_loaded, 16)
                if i == C_ADA2 + 2:
                    sp.dma_start(w_pool, a["w_pool"][0].rearrange("g p n -> p g n")).then_inc(pool_loaded, 16)
            sp.wait_ge(gate_done, 20)
            sp.dma_start(w_router, a["w_router"][0].rearrange("(k p) n -> p k n", p=128)).then_inc(router_loaded, 16)
            sp.wait_ge(branches_done, KD)
            load_expert(sp, 0, 2)
            sp.wait_ge(out_done, 2 * NT)
            for j in (0, 1, 3, 4, 5):
                load_expert(sp, 0, j)
            sp.wait_ge(best_ready, 1)
            sp.wait_ge(rows_saved[0], 16 * 3)
            sp.wait_ge(rows_saved[1], 16 * 2)
            sp.dma_start(iota[:, :], a["const_iota"]).then_inc(iota_loaded, 16)
            J = len(ORDER)
            with sp.Fori(0, NE - 1) as e:
                for j in range(RING, J + RING):
                    free_at = e * NP + pieces_before(j - RING + 1)
                    load_expert(sp, e + j // J, j % J, free_at)
            for j in range(RING, J):
                load_expert(sp, NE - 1, j, (NE - 1) * NP + pieces_before(j - RING + 1))
            for t in range(NT):
                sp.wait_ge(added, 1 + NE * 2 * NT + 2 * (t + 1))
                sp.dma_start(ys[t] if t < 4 else out["y_prompt"][0], x[:, t, :]).then_inc(stored, 16)
            sp.wait_ge(stored, 16 * (NT + 1))
            sp.wait_ge(kstate_stored, 16)

        @block.tensor
        def _(pe):
            mm, tr = nc.tensor.matmul, nc.tensor.transpose

            def chunk_arrived(i):
                pe.wait_ge(slot_loaded[i % STREAM], 16 * (i // STREAM + 1))

            def product(m, bank):
                i = m if m < C_QKV else C_ADA2 + m - C_QKV
                chunk_arrived(i)
                for k in range(KD):
                    last = mm(ps[0:2, bank, :], condT[:, :, k], chunk_slot(i)[:, k, :],
                              start=(k == 0), stop=(k == KD - 1))
                last.then_inc(mod_done, 1)

            def turn_modulation(m, bank, o):
                pe.wait_ge(mod_copied, m + 1)
                for b in range(4):
                    last = tr(ps[:, bank, o + 2 * b:o + 2 * b + 2], mod_row[0:2, m % 2, b * 128:(b + 1) * 128],
                              ident[0:2, 0:2])
                last.then_inc(mod_turned, 1)

            def turn_x(t):
                pe.wait_ge(x_normed, t + 1)
                if t >= 3:
                    pe.wait_ge(h_copied, t - 2)
                for k in range(KD):
                    last = tr(ps[:, 2 * (t % 3) + k // 4, k % 4 * 128:(k % 4 + 1) * 128],
                              xn[t % 2][:, k * 128:(k + 1) * 128], ident)
                last.then_inc(x_turned, 1)

            pe.wait_ge(cond_loaded, 48)
            tr(ps[:, 7, 0:2 * KD], rows[0:2 * KD], ident[0:2 * KD, 0:2 * KD]).then_inc(cond_turned, 1)
            pe.wait_ge(cond_ready, 1)
            product(0, 6)
            turn_modulation(0, 7, 32)
            product(1, 6)
            turn_x(0)
            turn_x(1)
            turn_modulation(1, 7, 40)
            product(2, 6)
            turn_x(2)
            turn_x(3)
            turn_modulation(2, 7, 48)
            pe.wait_ge(rows_loaded, 128)
            tr(ps[:, 7, 128:218], rows, ident[0:90, 0:90]).then_inc(vec_done, 1)
            product(3, 6)
            turn_x(4)
            pe.wait_ge(vec_ready, 1)
            turn_modulation(3, 7, 56)
            pe.wait_ge(past_loaded, 32)
            pe.wait_ge(h_copied, 4)
            for t in range(2):
                for i in range(4):
                    last = tr(ps[:, 6 * t, i * 128:(i + 1) * 128], k_past[:, t, i * 128:(i + 1) * 128], ident)
                last.then_inc(past_turned, 1)
            pe.wait_ge(h_copied, NT)
            pe.wait_ge(past_ready, 1)
            for i in range(3 * NT + 1):
                if i < 3 * NT:
                    if i % NT == 0:
                        chunk_arrived(C_QKV + i // NT)
                    if 4 <= i < 2 * NT + 4:
                        pe.wait_ge(qk_normed, i - 3)
                    elif i >= 2 * NT + 4:
                        pe.wait_ge(v_copied, i - 2 * NT - 3)
                    t, w = i % NT, chunk_slot(C_QKV + i // NT)
                    for k in range(KD):
                        if i == 0:
                            pe.wait_ge(h_ready, k + 1)
                        last = mm(ps[:, i % 4, :], hT[:, k, t * 128:(t + 1) * 128], w[:, k, :],
                                  start=(k == 0), stop=(k == KD - 1))
                    last.then_inc(proj_done, 1)
                if 1 <= i <= 2 * NT:
                    m = i - 1
                    pe.wait_ge(qk_normed, m + 1)
                    if m >= 2:
                        pe.wait_ge(qkT_ready, m - 1)
                    for hp in range(4):
                        last = tr(ps[:, 4 + m % 2, hp * 128:(hp + 1) * 128],
                                  normed[m % 2][:, hp * 128:(hp + 1) * 128], ident)
                    last.then_inc(qk_turned, 1)

            pe.wait_ge(qkT_ready, 2 * NT)
            pe.wait_ge(past_ready, 2)
            NU = UNITS + 2
            for u in range(NU + 3):
                if u < NU:
                    if u >= 3:
                        pe.wait_ge(probs_ready, u - 2)
                    else:
                        pe.wait_ge(v_copied, 3 + u)
                    j, h = divmod(u, H)
                    if u % H == 0:
                        pe.wait_ge(q_spread, j + 1)
                    if u < UNITS:
                        q = q_apart[:, j % 2, h % 2, h // 2, :]
                        b0 = WINDOW_BASE[j] * GRID_R
                        mm(ps[:, u % 3, 0:256], q, kT[:, h // 2, b0:b0 + 256], start=True, stop=True)
                        last = mm(ps[:, u % 3, 256:512], q, kT[:, h // 2, TOK:TOK + PAST], start=True, stop=True)
                    else:
                        for i in range(4):
                            last = mm(ps[:, u % 3, i * 128:(i + 1) * 128], q_apart[:, j % 2, u - UNITS, i, :],
                                      kT[:, i, LAT:TOK], start=True, stop=True)
                    last.then_inc(scores_done, 1)
                if 1 <= u <= NU:
                    m = u - 1
                    pe.wait_ge(probs_ready, m + 1)
                    if m >= 2:
                        pe.wait_ge(probsT_ready, m - 1)
                    for i in range(4):
                        last = tr(ps[:, 3 + m % 2, i * 128:(i + 1) * 128], probs[m % 2][:, i * 128:(i + 1) * 128], ident)
                    last.then_inc(probs_turned, 1)
                if 2 <= u <= NU + 1:
                    m = u - 2
                    pe.wait_ge(probsT_ready, m + 1)
                    j = m // H
                    if m == H:
                        pe.wait_ge(mid_loaded, 32)
                    if m % H == 0 and j >= 2:
                        pe.wait_ge(att_scaled, j - 1)
                    if m < UNITS:
                        h = m % H
                        vk = [[v_tok[:, 0], v_tok[:, 1]], [v_mid[:, 0], v_mid[:, 1]],
                              [v_mid[:, 1], v_mid[:, 2]], [v_tok[:, 2], v_tok[:, 3]]][j] + [v_past[:, 0], v_past[:, 1]]
                        for i in range(4):
                            last = mm(ps[:, 5 + j % 2, h * DH:(h + 1) * DH], probsT[m % 2][:, i * 128:(i + 1) * 128],
                                      vk[i][:, h * DH:(h + 1) * DH], start=(i == 0), stop=(i == 3))
                    else:
                        for i in range(4):
                            h = 2 * i + m - UNITS
                            last = mm(ps[:, 5, h * DH:(h + 1) * DH], probsT[m % 2][:, i * 128:(i + 1) * 128],
                                      v_tok[:, 4, h * DH:(h + 1) * DH], start=True, stop=True)
                    last.then_inc(pv_done, 1)
                if u >= 3 and (u - 3) % H == H - 1 or u == NU + 2:
                    j = min((u - 3) // H, 4)
                    pe.wait_ge(att_scaled, j + 1)
                    if j:
                        pe.wait_ge(attT_ready, j)
                    for i in range(4):
                        last = tr(ps[:, 7, i * 128:(i + 1) * 128], att[j % 2][:, i * 128:(i + 1) * 128], ident)
                    last.then_inc(att_turned, 1)

            pe.wait_ge(probs_ready, NU)
            pe.wait_ge(probsT_ready, NU)
            pe.wait_ge(att_scaled, 5)
            for i in range(20):
                c = C_GATES + i // 4
                if i % 4 == 0:
                    chunk_arrived(c)
                if i >= 3:
                    pe.wait_ge(gate_copied, 2 * (i - 2))
                w = chunk_slot(c)
                pe.wait_ge(block_cut, i + 1)
                for k in range(KD):
                    if i == 0:
                        pe.wait_ge(h_cut, k + 1)
                    for n, (wb, h) in enumerate(((block_hi, h_hi[k]), (block_hi, h_lo[:, k, :]), (block_lo, h_hi[k]))):
                        mm(ps[:, i % 3, :], wb[i % 2][:, k, :], h, start=(k == 0 and n == 0),
                           stop=(k == KD - 1 and n == 2))
                    last = mm(ps[:, 3 + i % 3, 0:CTX], w[:, k, i % 4 * 128:(i % 4 + 1) * 128], hT[:, k, LAT:TOK],
                              start=(k == 0), stop=(k == KD - 1))
                last.then_inc(gate_done, 1)

            pe.wait_ge(gate_copied, 38)
            pe.wait_ge(attT_ready, 5)
            for m in range(C_QKV, C_QKV + len(ADA2)):
                product(m, (2, 5)[m % 2])
                if m > C_QKV:
                    turn_modulation(m - 1, 6 if m - 1 >= GATE1_END else 0, 8 * (m - 1))
                i = m - GATE1_END - 1
                if 0 <= i < 4:
                    pe.wait_ge(diag_ready, i + 1)
                    if i:
                        pe.wait_ge(row_copied, i)
                    mm(ps[:, 7, :], ones, diag, start=True, stop=True).then_inc(row_done, 1)
            turn_modulation(m, 6, 8 * m)
            chunk_arrived(C_TAIL)
            pe.wait_ge(pool_loaded, 16)
            pe.wait_ge(pooled_ready, 2 * 4)
            pe.wait_ge(gate_copied, 40)
            wa = stream[C_TAIL % STREAM].rearrange("p (k n) -> p k n", n=D)
            for n in range(KD):
                if n == 1:
                    pe.wait_ge(mod_ready, 1)
                    pe.wait_ge(row_copied, 4)
                if n >= 2:
                    pe.wait_ge(merged, n - 1)
                b = n % 2 * 4
                for k in range(4):
                    lhsT = wa[:, k, n * 128:(n + 1) * 128]
                    mm(ps[:, b, :], lhsT, attT[:, k, 0:LAT], start=(k == 0), stop=(k == 3))
                    last = mm(ps[:, b + 1, 0:CTX], lhsT, attT[:, k, LAT:TOK], start=(k == 0), stop=(k == 3))
                lhsT = w_pool[:, n // 2, n % 2 * 128:(n % 2 + 1) * 128]
                mm(ps[:, b + 2, :], lhsT, pooledT[:, n // 2, 0:LAT], start=True, stop=True)
                last2 = mm(ps[:, b + 3, 0:CTX], lhsT, pooledT[:, n // 2, LAT:TOK], start=True, stop=True)
                last2.then_inc(branches_done, 1)
            pe.wait_ge(merged, KD)
            pe.wait_ge(router_loaded, 16)
            def router(m):
                pe.wait_ge(h2_ready, m + 1)
                for k in range(KD):
                    last = mm(ps[:, 6, m * NE:(m + 1) * NE], h2T[:, k, :], w_router[:, k, :],
                              start=(k == 0), stop=(k == KD - 1))
                last.then_inc(logits_done, 1)

            def turn_normed(m):
                if m:
                    pe.wait_ge(h2_ready, m)
                pe.wait_ge(xn2_ready, m + 1)
                for k in range(KD):
                    last = tr(ps[:, 4 + k // 4, k % 4 * 128:(k % 4 + 1) * 128],
                              xn2[m % 2][:, k * 128:(k + 1) * 128], ident)
                last.then_inc(xn2_turned, 1)

            for t in range(NT):
                if t >= 2:
                    pe.wait_ge(x2_ready, t - 1)
                for half in range(2):
                    for k in range(KD):
                        if t == 0:
                            pe.wait_ge(merged_cut, k + 1)
                            pe.wait_ge(out_cut, half * KD + k + 1)
                        for n, (h, w) in enumerate(((merged_hi, out_hi), (merged_lo, out_hi), (merged_hi, out_lo))):
                            last = mm(ps[:, t % 2 * 2 + half, :], h[:, k, t * 128:(t + 1) * 128], w[half][:, k, :],
                                      start=(k == 0 and n == 0), stop=(k == KD - 1 and n == 2))
                    last.then_inc(out_done, 1)
                    if half == 0 and t:
                        turn_normed(t - 1)
                if t:
                    router(t - 1)
            turn_normed(NT - 1)
            router(NT - 1)
            pe.wait_ge(aff_ready, 1)
            for t in range(NT):
                last = tr(ps[0:NE, 7 if t < 4 else 4, t % 4 * 128:(t % 4 + 1) * 128], aff[:, t, :], ident)
            last.then_inc(aff_turned, 1)
            pe.wait_ge(x2_ready, NT)
            for i in range(4):
                pe.wait_ge(diag2_ready, i + 1)
                mm(ps[0:SLOTS, i // 2, :], slot_sets[:, i % 2, :], diag2[i % 2], start=(i % 2 == 0), stop=(i % 2 == 1)
                   ).then_inc(row2_done, 1)
            pe.wait_ge(best_ready, 1)
            tr(ps[0:SLOTS, 5, 0:NE], best, ident[0:NE, 0:NE])
            tr(ps[0:SLOTS, 5, NE:2 * NE], best_place, ident[0:NE, 0:NE]).then_inc(best_turned, 1)

            def turn_gathered(e):
                pe.wait_ge(gathered, 16 * (e + 1))
                for d in range(KD):
                    last = tr(ps[:, d // 4 * 2, d % 4 * SLOTS:(d % 4 + 1) * SLOTS], x_rows[:, d * 128:(d + 1) * 128],
                              ident[0:SLOTS, 0:SLOTS])
                last.then_inc(xe_turned, 1)

            def turn_hidden(e, c):
                pe.wait_ge(h_done, e * NCH + c + 1)
                for b, (f, n) in enumerate(fblocks(c)):
                    last = tr(ps[0:n, 6, b * SLOTS:(b + 1) * SLOTS], hid[:, c % 2, f:f + n], ident[0:SLOTS, 0:SLOTS])
                last.then_inc(h_turned, 1)

            def scatter(e, i, bank=7, banks=1):
                if i >= banks or banks == 1:
                    pe.wait_ge(added, e * 2 * NT + i + 2 - banks)
                t, half = divmod(i, 2)
                for n, y in enumerate((y_hi, y_lo)):
                    last = mm(ps[:, bank, :], back[:, t * 128:(t + 1) * 128], y[:, half * 512:(half + 1) * 512],
                              start=(n == 0), stop=(n == 1))
                last.then_inc(scattered, 1)

            pe.wait_ge(gate2_ready, 2)
            turn_gathered(0)
            with pe.Fori(0, NE) as e:
                for p, (j, kind, c, b0, nb) in enumerate(PIECES):
                    hi, lo = w_hi[:, p % WBUF, :], w_lo[:, p % WBUF, :]
                    last_piece = p == LAST[kind, c]
                    if kind == "down":
                        if p == FIRST[kind, c]:
                            pe.wait_ge(hT_ready, e * NCH + c + 1)
                            if c == 0:
                                pe.wait_ge(y_scaled, e + 1)
                        kb = fblocks(c)[0][1]
                        first_of_all, last_of_all = c == 0 and b0 == 0, c == NCH - 1 and last_piece
                        pairs = [(hT_hi, hi), (hT_lo, hi)], [(hT_hi, lo)]
                        for part in range(2):
                            pe.wait_ge((hi_ready, lo_ready)[part], e * NP + p + 1)
                            for b in range(nb):
                                for half in range(2):
                                    for n, (h, w) in enumerate(pairs[part]):
                                        last = mm(ps[0:SLOTS, 4 + half, :], h[0:kb, c % 2, b0 + b, :],
                                                  w[0:kb, b * D + half * 512:b * D + (half + 1) * 512],
                                                  start=(first_of_all and part == 0 and b == 0 and n == 0),
                                                  stop=(last_of_all and part == 1 and b == nb - 1))
                    else:
                        bank, w0 = c % 2 + (2 if kind == "up" else 0), width(c)
                        if p == FIRST[kind, c]:
                            if c < 2:
                                pe.wait_ge(xe_ready, e + 1)
                            else:
                                pe.wait_ge(h_done, e * NCH + c - 1)
                        pairs = [(xe_hi, hi), (xe_lo, hi)], [(xe_hi, lo)]
                        for part in range(2):
                            pe.wait_ge((hi_ready, lo_ready)[part], e * NP + p + 1)
                            for b in range(nb):
                                for n, (h, w) in enumerate(pairs[part]):
                                    last = mm(ps[0:SLOTS, bank, 0:w0], h[:, b0 + b, :], w[:, b * w0:(b + 1) * w0],
                                              start=(b0 + b == 0 and part == 0 and n == 0),
                                              stop=(last_piece and part == 1 and b == nb - 1))
                    last.then_inc(pieces_used, 1)
                    if 0 <= p - SCATTER_AT < 2 * NT:
                        if p == SCATTER_AT:
                            pe.wait_ge(y_ready, e + 1)
                            pe.wait_ge(back_ready, e + 1)
                        scatter(e, p - SCATTER_AT)
                    if kind == "gate" and c >= 1 and last_piece:
                        turn_hidden(e, c - 1)
                    if (kind, c) == ("up", NCH - 1) and last_piece:
                        turn_gathered(e + 1)
                    if p == FIRST["down", NCH - 2]:
                        turn_hidden(e, NCH - 1)
            pe.wait_ge(y_ready, NE + 1)
            pe.wait_ge(back_ready, NE + 1)
            for i in range(2 * NT):
                scatter(NE, i, i % 4, 4)

        @block.scalar
        def _(act):
            A = nc.scalar.activation

            def load_rows(name, r, loaded):
                src = a[name][0]
                act.dma_start(rows[r:r + src.shape[0] // 128, :], src.rearrange("(k p) -> k p", p=128)
                              ).then_inc(loaded, 16)

            act.dma_start(keep[:, :], a["const_keep"]).then_inc(cond_loaded, 16)
            load_rows("c", 0, cond_loaded)
            for name, r in (("norm1_g", 16), ("norm2_g", 24), ("pool_scale", 32), ("b_ada", 40)):
                load_rows(name, r, rows_loaded)
            for i, name in enumerate(("q_norm_g", "k_norm_g")):
                for half in range(2):
                    act.dma_start(rows[88 + i:89 + i, half * DH:(half + 1) * DH], a[name]).then_inc(rows_loaded, 16)
            act.dma_start(misc[:, 4096:4544], a["const_mixer"]).then_inc(consts_loaded, 16)
            act.dma_start(kg_row, a["k_norm_g"].broadcast_to([128, DH])).then_inc(consts_loaded, 16)
            act.dma_start(rpb_pad[:, 16:16 + NR], rpb_flat).then_inc(pad_written, 16)
            act.dma_start(rpb_pad[:, 0:16], rpb_flat[:, 0:16]).then_inc(pad_written, 16)
            act.dma_start(rpb_pad[:, 16 + NR:32 + NR], rpb_flat[:, NR - 16:NR]).then_inc(pad_written, 16)

            def copy_modulation(m, bank):
                act.wait_ge(mod_done, m + 1)
                A(mod_row[0:2, m % 2, :], ps[0:2, bank, :], ACT.Copy).then_inc(mod_copied, 1)

            def copy_h(t):
                act.wait_ge(x_turned, t + 1)
                b = 2 * (t % 3)
                A(hT[:, :, t * 128:(t + 1) * 128].rearrange("p (a k) n -> p a k n", a=2),
                  ps[:, b:b + 2, :].rearrange("p a (k n) -> p a k n", n=128), ACT.Copy).then_inc(h_copied, 1)

            act.wait_ge(cond_turned, 1)
            A(sigT, ps[:, 7, 0:2 * KD], ACT.Sigmoid).then_inc(cond_sig, 1)
            copy_modulation(0, 6)
            for t in range(NT):
                act.wait_ge(x_loaded[t], 16)
                A(xn[t % 2], x[:, t, :], ACT.Square, accum_out=ss1[:, t:t + 1]).then_inc(squared1, 1)
                act.wait_ge(squared1, t + 1)
            act.wait_ge(ms1_ready, 1)
            A(rs1, ss1, ACT.Sqrt).then_inc(root1, 1)
            copy_modulation(1, 6)
            copy_h(0)
            copy_h(1)
            copy_modulation(2, 6)
            copy_h(2)
            copy_h(3)
            copy_modulation(3, 6)
            copy_h(4)
            for t in range(2):
                act.wait_ge(past_turned, t + 1)
                A(kT[:, :, TOK + t * 128:TOK + (t + 1) * 128],
                  ps[:, 6 * t, :].rearrange("p (k n) -> p k n", n=128), ACT.Copy).then_inc(past_ready, 1)

            def turned_out(m):
                act.wait_ge(qk_turned, m + 1)
                dst = (kT, qT)[m // NT][:, :, m % NT * 128:(m % NT + 1) * 128]
                A(dst, ps[:, 4 + m % 2, :].rearrange("p (k n) -> p k n", n=128), ACT.Copy,
                  scale=gT[:, 0, 1 - m // NT:2 - m // NT]).then_inc(qkT_ready, 1)

            for i in range(3 * NT):
                act.wait_ge(proj_done, i + 1)
                if i < 2 * NT:
                    if i >= 2:
                        act.wait_ge(qk_ms, i - 1)
                    A(squares[i % 2], ps[:, i % 4, :], ACT.Square).then_inc(qk_squared, 1)
                    act.wait_ge(qk_ms, i + 1)
                    A(rs_qk[i % 2], ss_qk[i % 2], ACT.Sqrt).then_inc(qk_root, 1)
                else:
                    A(v_tok[:, i - 2 * NT, :], ps[:, i % 4, :], ACT.Copy).then_inc(v_copied, 1)
                if 1 <= i <= 2 * NT:
                    turned_out(i - 1)
            act.wait_ge(v_copied, NT)
            act.dma_start(v_mid[0:64], v_tok[64:128, 0:3, :]).then_inc(mid_loaded, 16)
            act.dma_start(v_mid[64:128], v_tok[0:64, 1:4, :]).then_inc(mid_loaded, 16)
            act.dma_start(out["state_v"], v_tok[:, 4, :]).then_inc(stored, 16)
            act.wait_ge(kstate_ready, 1)
            act.dma_start(out["state_k"], k_state.rearrange("p h d -> p (h d)")).then_inc(kstate_stored, 16)

            NU = UNITS + 2

            def cut_high(k):
                A(h_hi[k], hT[:, k, 0:LAT], ACT.Copy).then_inc(h_cut_high, 1)

            def block_high_part(i):
                c = C_GATES + i // 4
                if i % 4 == 0:
                    act.wait_ge(slot_loaded[c % STREAM], 16 * (c // STREAM + 1))
                A(block_hi[i % 2], chunk_slot(c)[:, :, i % 4 * 128:(i % 4 + 1) * 128], ACT.Copy).then_inc(block_high, 1)

            for u in range(NU + 1):
                if 0 <= u - H_CUT_AT < H_EARLY:
                    if u == H_CUT_AT:
                        act.wait_ge(bias_ready, 3)
                    cut_high(u - H_CUT_AT)
                if u == UNITS + 1:
                    for k in range(H_EARLY, KD):
                        cut_high(k)
                if u < NU:
                    act.wait_ge(max_ready, u + 1)
                    if u >= 2:
                        act.wait_ge(probs_turned, u - 1)
                    if u < UNITS:
                        A(probs[u % 2], ps[:, u % 3, :], ACT.Exp, bias=negmax[:, u:u + 1],
                          accum_out=expsum[:, u:u + 1]).then_inc(probs_ready, 1)
                    else:
                        for i in range(4):
                            h = 2 * i + u - UNITS
                            last = A(probs[u % 2][:, i * 128:(i + 1) * 128], ps[:, u % 3, i * 128:(i + 1) * 128],
                                     ACT.Exp, bias=negmax_c[:, h:h + 1], accum_out=expsum_c[:, h:h + 1])
                        last.then_inc(probs_ready, 1)
                if u >= 1:
                    m = u - 1
                    act.wait_ge(probs_turned, m + 1)
                    if m >= 2:
                        act.wait_ge(pv_done, m - 1)
                    A(probsT[m % 2], ps[:, 3 + m % 2, :], ACT.Copy).then_inc(probsT_ready, 1)

            block_high_part(0)
            act.wait_ge(pv_done, NU)
            block_high_part(1)
            act.wait_ge(halo_ready, 2)
            act.wait_ge(attT_ready, 5)
            for i in range(20):
                act.wait_ge(gate_done, i + 1)
                if i < 18:
                    block_high_part(i + 2)
                lat, con = ps[:, i % 3, :], ps[:, 3 + i % 3, 0:CTX]
                if i < 4:
                    A(u_lat[:, i, POOL_HALO:POOL_HALO + LAT].rearrange("p (r c) -> p r c", c=GRID_W),
                      lat.rearrange("p (c r) -> p r c", r=GRID_R), ACT.Copy).then_inc(gate_copied, 1)
                    A(u_ctx[:, i, POOL_HALO:POOL_HALO + CTX], con, ACT.Copy).then_inc(gate_copied, 1)
                else:
                    g = (gaT if i < 12 else gbT)[:, (i - 4) % KD, :]
                    A(g[:, 0:LAT], lat, ACT.Sigmoid).then_inc(gate_copied, 1)
                    A(g[:, LAT:TOK], con, ACT.Sigmoid).then_inc(gate_copied, 1)
            for m in range(C_QKV, C_QKV + len(ADA2)):
                copy_modulation(m, (2, 5)[m % 2])
                i = m - GATE1_END - 1
                if 0 <= i < 4:
                    act.wait_ge(row_done, i + 1)
                    A(gate1_row[:, i // 2, i % 2 * 512:(i % 2 + 1) * 512], ps[:, 7, :], ACT.Copy).then_inc(row_copied, 1)

            def out_high_part(half):
                c = C_TAIL + 1 + half
                act.wait_ge(slot_loaded[c % STREAM], 16 * (c // STREAM + 1))
                for k in range(KD):
                    A(out_hi[half][:, k, :], chunk_slot(c)[:, k, :], ACT.Copy).then_inc(out_high, 1)

            act.wait_ge(pooled_ready, 8)
            out_high_part(0)
            for n in range(KD):
                act.wait_ge(merged, n + 1)
                A(merged_hi[:, n, :], gaT[:, n, :], ACT.Copy).then_inc(merged_high, 1)
            act.wait_ge(branches_done, KD)
            out_high_part(1)
            for t in range(NT + 1):
                if t >= 1:
                    m = t - 1
                    act.wait_ge(xn2_turned, m + 1)
                    if m:
                        act.wait_ge(logits_done, m)
                    for k in range(KD):
                        last = A(h2T[:, k, :], ps[:, 4 + k // 4, k % 4 * 128:(k % 4 + 1) * 128], ACT.Identity,
                                 scale=scale2[:, k, m // 4:m // 4 + 1], bias=modT[:, 24 + k, m // 4:m // 4 + 1])
                    last.then_inc(h2_ready, 1)
                if t < NT:
                    act.wait_ge(x2_ready, t + 1)
                    A(square_junk, x[:, t, :], ACT.Square, accum_out=ss2[:, t:t + 1]).then_inc(squared2, 1)
                    act.wait_ge(ms2_ready, t + 1)
                    A(rs2[:, t:t + 1], ss2[:, t:t + 1], ACT.Sqrt).then_inc(root2, 1)
                    act.wait_ge(xn2_ready, t + 1)
                    act.dma_start(xn_rows[t * 128:(t + 1) * 128, :], xn2[t % 2]
                                  ).then_inc(rows_saved[t % 2], 16)
            act.wait_ge(max2_ready, 1)
            A(aff, aff, ACT.Exp).then_inc(exp2_ready, 1)
            for half in range(2):
                act.wait_ge(row2_done, 2 * half + 2)
                A(gate2_row[:, half * 512:(half + 1) * 512], ps[0:SLOTS, half, :], ACT.Copy).then_inc(gate2_ready, 1)

            def high_columns(e):
                act.wait_ge(xe_mod, e + 1)
                A(xe_hi[:, :, :], xe_f, ACT.Copy).then_inc(xe_high, 1)

            def silu(e, c):
                act.wait_ge(pieces_used, WBUF + e * NP + LAST["gate", c] + 1)
                if c < 2:
                    act.wait_ge(h_turned, e * NCH + NCH)
                else:
                    act.wait_ge(h_turned, e * NCH + NCH + c - 1)
                A(hid[:, c % 2, 0:width(c)], ps[0:SLOTS, c % 2, 0:width(c)], ACT.Silu).then_inc(silu_ready, 1)

            def high_hidden(e, c):
                act.wait_ge(h_turned, e * NCH + NCH + c + 1)
                kb, nb = fblocks(c)[0][1], len(fblocks(c))
                A(hT_hi[0:kb, c % 2, 0:nb, :], ps[0:kb, 6, 0:nb * SLOTS].rearrange("p (b s) -> p b s", s=SLOTS),
                  ACT.Copy).then_inc(h_high, 1)

            def high_rows(e):
                act.wait_ge(y_scaled, e + 1)
                act.wait_ge(scattered, 2 * NT * (e + 1))
                A(y_hi[:, :], y_f[0:SLOTS, :], ACT.Copy).then_inc(y_high, 1)

            high_columns(0)
            with act.Fori(0, NE) as e:
                for p, (j, kind, c, b0, nb) in enumerate(PIECES):
                    if p == FIRST[kind, c]:
                        act.wait_ge(slot_loaded[j % RING], arrived(e, j))
                    act.wait_ge(pieces_used, e * NP + p + 1)
                    rows_, n = piece_shape(p)
                    A(w_hi[0:rows_, p % WBUF, 0:n], piece(p), ACT.Copy).then_inc(hi_ready, 1)
                    for cc in range(NCH):
                        if cc < NCH - 1 and p == LAST["up", cc + 1]:
                            high_hidden(e, cc)
                        if p == LAST["gate", cc] + 2:
                            silu(e, cc)
                    if p == SCALE_AT + 1:
                        high_rows(e)
                    if p == FIRST["down", NCH - 1]:
                        high_columns(e + 1)
                        high_hidden(e, NCH - 1)
            high_rows(NE)

        @block.vector
        def _(dve):
            V = nc.vector
            steps = [0]

            def then(ins):
                steps[0] += 1
                ins.then_inc(dve_step, 1)
                dve.wait_ge(dve_step, steps[0])

            dve.wait_ge(cond_sig, 1)
            V.tensor_tensor(condT.rearrange("p a k -> p (a k)"), sigT, ps[:, 7, 0:2 * KD], ALU.mult
                            ).then_inc(cond_ready, 1)
            dve.wait_ge(squared1, NT)
            V.tensor_scalar(ss1, ss1, 1.0 / D, EPS, ALU.mult, ALU.add).then_inc(ms1_ready, 1)
            dve.wait_ge(root1, 1)
            then(V.reciprocal(rs1, rs1))
            for t in range(NT):
                if t >= 2:
                    dve.wait_ge(x_turned, t - 1)
                V.tensor_scalar(xn[t % 2], x[:, t, :], rs1[:, t:t + 1], None, ALU.mult).then_inc(x_normed, 1)
            dve.wait_ge(vec_done, 1)
            V.tensor_copy(vecT[:, :], ps[:, 7, 128:218]).then_inc(vec_ready, 1)
            dve.wait_ge(vec_ready, 1)
            V.tensor_scalar(gT[:, 0, 0:1], vecT[:, 88:89], DH ** -0.5, None, ALU.mult)
            V.tensor_copy(gT[:, 0, 1:2], vecT[:, 89:90])
            b_ada = vecT[:, 40:88]
            dve.wait_ge(mod_turned, C_QKV)
            then(V.tensor_tensor(modT[:, 0:16, :], ps[:, 7, 32:64].rearrange("p (n c) -> p n c", c=2),
                                 b_ada[:, 0:16].unsqueeze(2).broadcast_to([128, 16, 2]), ALU.add))
            then(V.scalar_tensor_tensor(scale1[:, :, :], modT[:, 8:16, :], 1.0,
                                        vecT[:, 16:24].unsqueeze(2).broadcast_to([128, 8, 2]), ALU.add, ALU.mult))
            dve.wait_ge(h_copied, NT)
            for k in range(KD):
                V.tensor_scalar(hT[:, k, 0:LAT], hT[:, k, 0:LAT], scale1[:, k, 0:1], modT[:, k, 0:1], ALU.mult, ALU.add)
                V.tensor_scalar(hT[:, k, LAT:TOK], hT[:, k, LAT:TOK], scale1[:, k, 1:2], modT[:, k, 1:2],
                                ALU.mult, ALU.add).then_inc(h_ready, 1)
            for i in range(2 * NT):
                dve.wait_ge(qk_squared, i + 1)
                then(V.tensor_reduce(ss_qk[i % 2], squares[i % 2].rearrange("p (h d) -> p h d", d=DH), AX, ALU.add))
                V.tensor_scalar(ss_qk[i % 2], ss_qk[i % 2], 1.0 / DH, EPS, ALU.mult, ALU.add).then_inc(qk_ms, 1)
                dve.wait_ge(qk_root, i + 1)
                then(V.reciprocal(rs_qk[i % 2], rs_qk[i % 2]))
                if i >= 2:
                    dve.wait_ge(qk_turned, i - 1)
                V.tensor_tensor(normed[i % 2].rearrange("p (h d) -> p h d", d=DH),
                                ps[:, i % 4, :].rearrange("p (h d) -> p h d", d=DH),
                                rs_qk[i % 2].unsqueeze(2).broadcast_to([128, H, DH]), ALU.mult).then_inc(qk_normed, 1)
                if i == NT - 1:
                    dve.wait_ge(qk_normed, NT)
                    dve.wait_ge(consts_loaded, 32)
                    V.tensor_tensor(k_state, normed[i % 2].rearrange("p (h d) -> p h d", d=DH),
                                    kg_row.unsqueeze(1).broadcast_to([128, H, DH]), ALU.mult).then_inc(kstate_ready, 1)
            NU = UNITS + 2
            dve.wait_ge(bias_ready, 3)

            def finish_tile(j):
                dve.wait_ge(pv_done, min(H * (j + 1), NU))
                sums = expsum[:, j * H:(j + 1) * H]
                then(V.reciprocal(inv_sum, sums))
                if j == 0:
                    dve.wait_ge(kstate_stored, 16)
                if j >= 2:
                    dve.wait_ge(att_turned, j - 1)
                V.tensor_tensor(att[j % 2].rearrange("p (h d) -> p h d", d=DH),
                                ps[:, 5 + j % 2, :].rearrange("p (h d) -> p h d", d=DH),
                                inv_sum.unsqueeze(2).broadcast_to([128, H, DH]), ALU.mult).then_inc(att_scaled, 1)

            def copy_turned(j):
                dve.wait_ge(att_turned, j + 1)
                V.tensor_copy(attT[:, :, j * 128:(j + 1) * 128],
                              ps[:, 7, :].rearrange("p (k n) -> p k n", n=128)).then_inc(attT_ready, 1)

            def cut_low(k):
                dve.wait_ge(h_cut_high, k + 1)
                V.tensor_tensor(h_lo[:, k, :], hT[:, k, 0:LAT], h_hi[k].bitcast(f32), ALU.subtract).then_inc(h_cut, 1)

            def block_low_part(i):
                dve.wait_ge(block_high, i + 1)
                V.tensor_tensor(block_lo[i % 2], chunk_slot(C_GATES + i // 4)[:, :, i % 4 * 128:(i % 4 + 1) * 128],
                                block_hi[i % 2].bitcast(f32), ALU.subtract).then_inc(block_cut, 1)

            for u in range(NU):
                if 1 <= u - H_CUT_AT <= H_EARLY:
                    cut_low(u - H_CUT_AT - 1)
                dve.wait_ge(scores_done, u + 1)
                s = ps[:, u % 3, :]
                if u < UNITS:
                    j, h = divmod(u, H)
                    then(V.tensor_tensor(s[:, 0:256], s[:, 0:256],
                                         bias[:, BIAS_VARIANT[j] * H + h].rearrange("p c r -> p (c r)"), ALU.add))
                    V.tensor_reduce(negmax[:, u:u + 1], s, AX, ALU.max, negate=True).then_inc(max_ready, 1)
                else:
                    V.tensor_reduce(negmax_c[:, u - UNITS:H:2], s.rearrange("p (h n) -> p h n", n=128), AX, ALU.max,
                                    negate=True).then_inc(max_ready, 1)
                if u >= 10 and u % H == 2 and u < NU - 1:
                    finish_tile(u // H - 1)
                if u >= 12 and u % H == 5:
                    copy_turned(u // H - 1)
            cut_low(5)
            finish_tile(3)
            copy_turned(3)
            cut_low(6)
            cut_low(7)
            finish_tile(4)
            block_low_part(0)
            copy_turned(4)
            block_low_part(1)

            V.memset(u_lat[:, :, :], 0.0).then_inc(halo_ready, 1)
            V.memset(u_ctx[:, :, :], 0.0).then_inc(halo_ready, 1)
            for g in range(4):
                block_low_part(g + 2)
                dve.wait_ge(gate_copied, 2 * (g + 1))
                for u_set, L, order in ((u_lat, LAT, True), (u_ctx, CTX, False)):
                    u, c = u_set[:, g, :], POOL_HALO
                    w, reach = 1, POOL_HALO - 1
                    then(V.tensor_tensor(win[0][:, 1:L + 2 * c], u[:, 0:L + 2 * c - 1], u[:, 1:L + 2 * c], ALU.add))
                    lo, hi, cur = 1, L + 2 * c, 0
                    for n in range(g):
                        sh = 1 << n
                        then(V.tensor_tensor(win[1 - cur][:, lo + sh:hi - sh], win[cur][:, lo:hi - 2 * sh],
                                             win[cur][:, lo + 2 * sh:hi], ALU.add))
                        lo, hi, cur = lo + sh, hi - sh, 1 - cur
                    f = win[cur]
                    then(V.tensor_tensor(f[:, c:c + 8], f[:, c:c + 8], pool_fix[:, g, 0, :], ALU.mult))
                    then(V.tensor_tensor(f[:, c + L - 8:c + L], f[:, c + L - 8:c + L], pool_fix[:, g, 1, :], ALU.mult))
                    if order:
                        dst = pooledT[:, g, 0:LAT].rearrange("p (c r) -> p r c", r=GRID_R)
                        fi = f[:, c:c + L].rearrange("p (r c) -> p r c", c=GRID_W)
                        ui = u[:, c:c + L].rearrange("p (r c) -> p r c", c=GRID_W)
                    else:
                        dst, fi, ui = pooledT[:, g, LAT:TOK], f[:, c:c + L], u[:, c:c + L]
                    V.scalar_tensor_tensor(dst, fi, 1.0 / (2 << g), ui, ALU.mult, ALU.subtract).then_inc(pooled_ready, 1)
                    dve.wait_ge(pooled_ready, 2 * g + (1 if order else 2))
            for i in range(6, 20):
                block_low_part(i)
            dve.wait_ge(mod_turned, GATE1_END)
            then(V.tensor_tensor(modT[:, 16:24, :], ps[:, 0, 32:48].rearrange("p (n c) -> p n c", c=2),
                                 b_ada[:, 16:24].unsqueeze(2).broadcast_to([128, 8, 2]), ALU.add))
            for i in range(4):
                if i:
                    dve.wait_ge(row_done, i)
                cols = modT[:, 16 + i % 2 * 4:20 + i % 2 * 4, i // 2:i // 2 + 1]
                V.tensor_tensor(diag, ident.unsqueeze(1).broadcast_to([128, 4, 128]),
                                cols.broadcast_to([128, 4, 128]), ALU.mult).then_inc(diag_ready, 1)
            dve.wait_ge(mod_turned, C_QKV + len(ADA2))
            then(V.tensor_tensor(modT[:, 24:48, :], ps[:, 6, 48:96].rearrange("p (n c) -> p n c", c=2),
                                 b_ada[:, 24:48].unsqueeze(2).broadcast_to([128, 24, 2]), ALU.add))
            V.scalar_tensor_tensor(scale2[:, :, :], modT[:, 32:40, :], 1.0,
                                   vecT[:, 24:32].unsqueeze(2).broadcast_to([128, 8, 2]), ALU.add, ALU.mult
                                   ).then_inc(mod_ready, 1)

            def merged_low_part(n):
                dve.wait_ge(merged_high, n + 1)
                V.tensor_tensor(merged_lo[:, n, :], gaT[:, n, :], merged_hi[:, n, :].bitcast(f32), ALU.subtract
                                ).then_inc(merged_cut, 1)

            def out_low_part(half, k):
                dve.wait_ge(out_high, half * KD + k + 1)
                V.tensor_tensor(out_lo[half][:, k, :], chunk_slot(C_TAIL + 1 + half)[:, k, :],
                                out_hi[half][:, k, :].bitcast(f32), ALU.subtract).then_inc(out_cut, 1)

            for n in range(KD):
                dve.wait_ge(branches_done, n + 1)
                b = n % 2 * 4
                for o, m, w in ((0, LAT, 0), (LAT, CTX, 1)):
                    V.tensor_tensor(gaT[:, n, o:o + m], gaT[:, n, o:o + m], ps[:, b + w, 0:m], ALU.mult)
                    then(V.scalar_tensor_tensor(gbT[:, n, o:o + m], ps[:, b + 2 + w, 0:m], vecT[:, 32 + n:33 + n],
                                                gbT[:, n, o:o + m], ALU.mult, ALU.mult))
                V.tensor_tensor(gaT[:, n, :], gaT[:, n, :], gbT[:, n, :], ALU.add).then_inc(merged, 1)
                out_low_part(0, n)
                if n:
                    merged_low_part(n - 1)
            merged_low_part(KD - 1)
            for k in range(KD):
                out_low_part(1, k)
            dve.wait_ge(row_copied, 4)
            for t in range(NT):
                for half in range(2):
                    dve.wait_ge(out_done, 2 * t + half + 1)
                    cols = slice(half * 512, (half + 1) * 512)
                    then(V.tensor_tensor(gated[:, cols], ps[:, t % 2 * 2 + half, :], gate1_row[:, int(t == 4), cols],
                                         ALU.mult))
                    last = V.tensor_tensor(x[:, t, cols], x[:, t, cols], gated[:, cols], ALU.add)
                last.then_inc(x2_ready, 1)
                dve.wait_ge(squared2, t + 1)
                V.tensor_scalar(ss2[:, t:t + 1], ss2[:, t:t + 1], 1.0 / D, EPS, ALU.mult, ALU.add
                                ).then_inc(ms2_ready, 1)
                dve.wait_ge(root2, t + 1)
                then(V.reciprocal(rs2[:, t:t + 1], rs2[:, t:t + 1]))
                if t >= 2:
                    dve.wait_ge(rows_saved[t % 2], 16 * (t // 2))
                    dve.wait_ge(xn2_turned, t - 1)
                V.tensor_scalar(xn2[t % 2], x[:, t, :], rs2[:, t:t + 1], None, ALU.mult).then_inc(xn2_ready, 1)
            dve.wait_ge(logits_done, NT)
            logits = ps[:, 6, 0:NT * NE].rearrange("p (t n) -> p t n", n=NE)
            then(V.tensor_reduce(rmax, logits, AX, ALU.max))
            V.tensor_tensor(aff, logits, rmax.unsqueeze(2).broadcast_to([128, NT, NE]), ALU.subtract
                            ).then_inc(max2_ready, 1)
            dve.wait_ge(exp2_ready, 1)
            then(V.tensor_reduce(rsum, aff, AX, ALU.add))
            then(V.reciprocal(rsum, rsum))
            V.tensor_tensor(aff, aff, rsum.unsqueeze(2).broadcast_to([128, NT, NE]), ALU.mult
                            ).then_inc(aff_ready, 1)
            dve.wait_ge(aff_turned, 1)
            V.tensor_copy(affN[:, 0:LAT].rearrange("p (r c) -> p r c", c=GRID_W),
                          ps[0:NE, 7, :].rearrange("p (c r) -> p r c", r=GRID_R))
            then(V.tensor_copy(affN[:, LAT:TOK], ps[0:NE, 4, 0:CTX]))
            for o, m, s0, cap in ((0, LAT, 0, CAP_L), (LAT, CTX, CAP_L, CAP_C)):
                src, dst = affN[:, o:o + m], left[:, o:o + m]
                for n in range(s0, s0 + cap, 8):
                    then(V.max(best[:, n:n + 8], src))
                    V.max_index(found[:, n:n + 8], best[:, n:n + 8], src)
                    then(V.match_replace(dst, best[:, n:n + 8], src, -1.0))
                    src = dst
            lat = found[:, 0:CAP_L]
            then(V.tensor_scalar(found_col[:, 0:CAP_L], lat, GRID_W - 1, 3, ALU.bitwise_and, ALU.logical_shift_left))
            then(V.tensor_scalar(lat, lat, 6, None, ALU.logical_shift_right))
            then(V.tensor_tensor(lat, lat, found_col[:, 0:CAP_L], ALU.bitwise_or))
            then(V.tensor_copy(best_place, found))
            V.tensor_scalar(best_place[:, CAP_L:SLOTS], best_place[:, CAP_L:SLOTS], float(LAT), None, ALU.add
                            ).then_inc(best_ready, 1)
            dve.wait_ge(best_turned, 1)
            V.tensor_copy(places[:, 0:NE], ps[0:SLOTS, 5, NE:2 * NE])
            then(V.memset(places[:, NE:NE + 2], 0.0))
            then(V.tensor_copy(places_int[:, :], places[:, :]))
            V.tensor_copy(place_now[:, :], places_int[:, 0:1]).then_inc(place_ready, 1)
            V.memset(gates[:, 0:1], 0.0)
            then(V.tensor_copy(gates[:, 1:NE + 1], ps[0:SLOTS, 5, 0:NE]))
            then(V.memset(ps[0:SLOTS, 4:6, :], 0.0))
            dve.wait_ge(rows_saved[0], 16 * 3)
            dve.wait_ge(rows_saved[1], 16 * 2)
            V.memset(back[:, :].bitcast(f32), 0.0).then_inc(back_ready, 1)
            dve.wait_ge(gate2_ready, 2)
            dve.sem_inc(pieces_used, WBUF)
            dve.sem_inc(scattered, 2 * NT)
            dve.sem_inc(added, 1)
            dve.sem_inc(h_turned, NCH)

            def fit_columns(e):
                dve.wait_ge(xe_turned, e + 1)
                X = ps[:, 0:3:2, 0:4 * SLOTS].rearrange("p a (k s) -> p a k s", s=SLOTS)
                xe4 = xe_f.rearrange("p (a k) s -> p a k s", a=2)
                for s, (o, m) in enumerate(((0, CAP_L), (CAP_L, CAP_C))):
                    last = V.tensor_tensor(xe4[:, :, :, o:o + m], X[:, :, :, o:o + m],
                                           scale2[:, :, s:s + 1].rearrange("p (a k) o -> p a k o", a=2)
                                           .broadcast_to([128, 2, 4, m]), ALU.mult)
                last.then_inc(xe_scaled, 1)
                dve.wait_ge(xe_scaled, e + 1)
                for s, (o, m) in enumerate(((0, CAP_L), (CAP_L, CAP_C))):
                    last = V.tensor_tensor(xe_f[:, :, o:o + m], xe_f[:, :, o:o + m],
                                           modT[:, 24:32, s:s + 1].broadcast_to([128, 8, m]), ALU.add)
                last.then_inc(xe_mod, 1)

            def hidden(e, c):
                dve.wait_ge(pieces_used, WBUF + e * NP + LAST["up", c] + 1)
                dve.wait_ge(silu_ready, e * NCH + c + 1)
                h = hid[:, c % 2, 0:width(c)]
                V.tensor_tensor(h, h, ps[0:SLOTS, 2 + c % 2, 0:width(c)], ALU.mult).then_inc(h_done, 1)

            def low_hidden(e, c):
                dve.wait_ge(h_high, e * NCH + c + 1)
                kb, nb = fblocks(c)[0][1], len(fblocks(c))
                V.tensor_tensor(hT_lo[0:kb, c % 2, 0:nb, :],
                                ps[0:kb, 6, 0:nb * SLOTS].rearrange("p (b s) -> p b s", s=SLOTS),
                                hT_hi[0:kb, c % 2, 0:nb, :].bitcast(f32), ALU.subtract).then_inc(hT_ready, 1)

            def scale_rows(e):
                dve.wait_ge(pieces_used, WBUF + e * NP)
                dve.wait_ge(xe_ready, e + 1)
                V.scalar_tensor_tensor(y_f[0:SLOTS, :].rearrange("p (a n) -> p a n", a=2), ps[0:SLOTS, 4:6, :],
                                       gates[:, ds(e, 1)], gate2_row[:, :].rearrange("p (a n) -> p a n", a=2),
                                       ALU.mult, ALU.mult).then_inc(y_scaled, 1)

            def add_back(e, i, bank=7):
                dve.wait_ge(scattered, 2 * NT + e * 2 * NT + i + 1)
                t, half = divmod(i, 2)
                xt = x[:, t, half * 512:(half + 1) * 512]
                V.tensor_tensor(xt, xt, ps[:, bank, :], ALU.add).then_inc(added, 1)

            fit_columns(0)
            dve.wait_ge(iota_loaded, 16)
            dve.wait_ge(gathered, 16)
            V.tensor_copy(place_now[:, :], places_int[:, 1:2]).then_inc(place_ready, 1)
            with dve.Fori(0, NE) as e:
                for p, (j, kind, c, b0, nb) in enumerate(PIECES):
                    rows_, n = piece_shape(p)
                    dve.wait_ge(hi_ready, e * NP + p + 1)
                    V.tensor_tensor(w_lo[0:rows_, p % WBUF, 0:n], piece(p), w_hi[0:rows_, p % WBUF, 0:n].bitcast(f32),
                                    ALU.subtract).then_inc(lo_ready, 1)
                    if p == SCALE_AT:
                        scale_rows(e)
                    if 0 <= p - SCATTER_AT - 1 < 2 * NT:
                        add_back(e, p - SCATTER_AT - 1)
                    for cc in range(NCH):
                        if p == LAST["up", cc] + (2 if cc < NCH - 1 else 1):
                            hidden(e, cc)
                        if cc < NCH - 1 and p == LAST["up", cc + 1]:
                            low_hidden(e, cc)
                    if p == SCATTER_AT + 2 * NT + 2:
                        V.tensor_scalar(back[:, :], iota[:, :], places[:, ds(e, 1)], None, ALU.is_equal
                                        ).then_inc(back_ready, 1)
                        dve.wait_ge(gathered, 16 * (e + 2))
                        V.tensor_copy(place_now[:, :], places_int[:, ds(e + 2, 1)]).then_inc(place_ready, 1)
                    if p == FIRST["down", NCH - 2]:
                        fit_columns(e + 1)
                    if p == FIRST["down", NCH - 1]:
                        low_hidden(e, NCH - 1)
            scale_rows(NE)
            dve.wait_ge(y_high, NE + 1)
            V.tensor_tensor(y_lo[:, :], y_f[0:SLOTS, :], y_hi[:, :].bitcast(f32), ALU.subtract).then_inc(y_ready, 1)
            for i in range(2 * NT):
                add_back(NE, i, i % 4)

        @block.gpsimd
        def _(pool):
            pool.wait_ge(wide_loaded, 16 * GRID_R * H)
            pool.wait_ge(consts_loaded, 32)
            for v in range(3):
                for h in range(H):
                    last = nc.gpsimd.tensor_tensor(
                        bias[:, v * H + h], rpb_wide[:, h, :, 8 * v:32 + 8 * v][:, :, ::-1].rearrange("p r c -> p c r"),
                        mask[:, v, :].unsqueeze(2).broadcast_to([128, 32, GRID_R]), ALU.add)
                last.then_inc(bias_ready, 1)
            G = nc.gpsimd
            pool.wait_ge(qkT_ready, 2 * NT)
            pool.wait_ge(bias_ready, 3)
            G.memset(q_apart[DH:128, :, 0], 0.0).then_inc(pool_step, 1)
            pool.wait_ge(pool_step, 1)
            G.memset(q_apart[0:DH, :, 1], 0.0).then_inc(pool_step, 1)
            for j in range(NT):
                pool.wait_ge(pool_step, 2 + j)
                if j >= 2:
                    pool.wait_ge(scores_done, H * (j - 1))
                t = slice(j * 128, (j + 1) * 128)
                G.tensor_copy(q_apart[0:DH, j % 2, 0], qT[0:DH, :, t]).then_inc(pool_step, 1)
                pool.wait_ge(pool_step, 3 + j)
                G.tensor_copy(q_apart[DH:128, j % 2, 1], qT[DH:128, :, t]).then_inc(q_spread, 1)
                pool.wait_ge(q_spread, j + 1)
            pool.wait_ge(mod_ready, 1)
            pool.wait_ge(squared2, NT)
            for i in range(4):
                if i >= 2:
                    pool.wait_ge(row2_done, i - 1)
                cols = modT[:, 40 + i // 2 * 4:44 + i // 2 * 4, i % 2:i % 2 + 1]
                G.tensor_tensor(diag2[i % 2], ident.unsqueeze(1).broadcast_to([128, 4, 128]),
                                cols.broadcast_to([128, 4, 128]), ALU.mult).then_inc(diag2_ready, 1)
            pool.wait_ge(rows_saved[0], 16 * 3)
            pool.wait_ge(rows_saved[1], 16 * 2)

            def gather(e):
                pool.wait_ge(place_ready, e + 1)
                pool.sem_inc(gathers_begun, 1)
                nc.gpsimd.indirect_dma_start(
                    out=x_rows[:, :], out_offset=None, in_=xn_rows,
                    in_offset=bass.IndirectOffsetOnAxis(ap=place_now[:, 0:1], axis=0)).then_inc(gathered, 16)

            def low_columns(e):
                pool.wait_ge(xe_high, e + 1)
                G.tensor_tensor(xe_lo[:, :, :], xe_f, xe_hi[:, :, :].bitcast(f32), ALU.subtract).then_inc(xe_ready, 1)

            def low_rows(e):
                pool.wait_ge(y_high, e + 1)
                G.tensor_tensor(y_lo[:, :], y_f[0:SLOTS, :], y_hi[:, :].bitcast(f32), ALU.subtract
                                ).then_inc(y_ready, 1)

            gather(0)
            with pool.Fori(0, NE) as e:
                pool.wait_ge(xe_turned, e + 1)
                gather(e + 1)
                low_columns(e)
                low_rows(e)
            low_columns(NE)


def _constants():
    keep = np.eye(128, dtype=np.float32)
    mixer = np.zeros((128, 448), np.float32)
    for v, (j, base) in enumerate(((0, 0), (1, 8), (3, 32))):
        qc = 16 * j + np.arange(128)[:, None] // 8
        kc = base + np.arange(32)[None, :]
        start = np.clip(qc - 8, 0, 48)
        mixer[:, v * 32:(v + 1) * 32] = np.where((kc >= start) & (kc < start + 16), 0.0, -1e30)
    fix = np.ones((4, 2, 8), np.float64)
    for g in range(4):
        w = 2 << g
        for i in range(8):
            fix[g, 0, i] = w / (i + w - w // 2 - max(i - w // 2, 0))
            fix[g, 1, i] = w / (min(i - 8 + w - w // 2, 0) - (i - 8 - w // 2))
    mixer[:, 96:160] = fix.reshape(1, 64)
    mixer[:, 160:288] = 1.0
    mixer[:, 288:288 + CAP_L] = 1.0
    mixer[:, 288 + SLOTS + CAP_L:288 + 2 * SLOTS] = 1.0
    iota = np.tile(np.arange(TOK, dtype=np.float32), (SLOTS, 1))
    return {"const_keep": keep, "const_mixer": mixer, "const_iota": iota}


_OUTS = {"y_prompt": (1, CTX, D), "y_sample": (1, LAT, D), "state_k": (CTX, H * DH), "state_v": (CTX, H * DH)}


def kernel(**inputs):
    import concourse.bacc as bacc
    from concourse.bass_utils import run_bass_kernel_spmd

    nc = bacc.Bacc("TRN2", target_bir_lowering=False, num_devices=1)
    arrays, a, out = {}, {}, {}
    inputs = {**inputs, "rpb": np.asarray(inputs["rpb"])[..., ::-1]}
    for name, v in {**inputs, **_constants()}.items():
        v = np.ascontiguousarray(v)
        arrays[f"in_{name}"] = v
        a[name] = nc.dram_tensor(f"in_{name}", v.shape, mybir.dt.from_np(v.dtype), kind="ExternalInput").ap()
    for name, shape in _OUTS.items():
        out[name] = nc.dram_tensor(f"out_{name}", shape, mybir.dt.float32, kind="ExternalOutput").ap()
    step_kernel(nc, a, out)
    r = run_bass_kernel_spmd(nc, [arrays], core_ids=[0]).results[0]
    state = (1, 1, CTX, H, DH)
    return (r["out_y_prompt"], r["out_y_sample"], r["out_state_k"].reshape(state), r["out_state_v"].reshape(state))
```

```python
from contextlib import ExitStack

import numpy as np

import concourse.bass as bass
from concourse import mybir

D = 1024
KD = D // 128
LAT, CTX = 512, 128
TOK = LAT + CTX
NT = TOK // 128
GRID_W, GRID_R = 64, 8
H, DH = 8, 64
PAST = 256
NE = 16
F = 2752
CAP_L, CAP_C = 2 * LAT // NE, 2 * CTX // NE
SLOTS = CAP_L + CAP_C
FC = 512
NCH = -(-F // FC)
NFB = -(-F // 128)
RING = 6
SLOT = KD * 512
PIECE = SLOT // 2
WBUF = 3
STREAM = 3
EPS = 1e-6
UNITS = 4 * H
WINDOW_BASE = (0, 8, 24, 32)
BIAS_VARIANT = (0, 1, 1, 2)
POOL_HALO = 8

ADA1 = [("ada", n) for n in range(4)]
QKV = [("in", 1), ("in", 0), ("in", 2)]
GATES = [("in", n) for n in range(3, 8)]
ADA2 = [("ada", n) for n in range(4, 10)]
TAIL = [("att", 0), ("out", 0), ("out", 1)]
ADA3 = [("ada", n) for n in range(10, 12)]
CHUNKS = ADA1 + QKV + GATES + ADA2 + TAIL + ADA3
C_QKV, C_GATES, C_ADA2, C_TAIL, C_ADA3 = 4, 7, 12, 18, 21
SLOT_OF = (0, 1, 2, 0) + (1, 0, 1) + (0, 1, 0, 1, 0) + (1, 0, 2, 1, 0, 1) + (2, 1, 0) + (2, 5)
TILES = (NT - 1,) + tuple(range(NT - 1))
GATE1_END = C_QKV + 2
USES = [SLOT_OF.count(s) for s in range(RING)]
assert len(SLOT_OF) == len(CHUNKS)


def start(c):
    return 0 if c == 0 else F - (NCH - c) * FC


def width(c):
    return start(c + 1) - start(c) if c + 1 < NCH else FC


def fblocks(c):
    w = width(c)
    n = 128 if w % 128 == 0 else w // 2
    return [(f, n) for f in range(0, w, n)]


ORDER = [("gate", 0), ("up", 0)]
for _c in range(1, NCH):
    ORDER += [("gate", _c), ("up", _c), ("down", _c - 1)]
ORDER += [("down", NCH - 1)]
PIECES = []
for _j, (_kind, _c) in enumerate(ORDER):
    if _kind == "down":
        _n = len(fblocks(_c))
        PIECES += [(_j, _kind, _c, b, 2) for b in range(0, _n, 2)]
    elif width(_c) * KD <= PIECE:
        PIECES += [(_j, _kind, _c, 0, KD)]
    else:
        PIECES += [(_j, _kind, _c, b, KD // 2) for b in (0, KD // 2)]
NP = len(PIECES)
assert NP % WBUF == 0 and len(ORDER) % RING == 0
FIRST = {p[1:3]: min(i for i, q in enumerate(PIECES) if q[1:3] == p[1:3]) for p in PIECES}
LAST = {p[1:3]: max(i for i, q in enumerate(PIECES) if q[1:3] == p[1:3]) for p in PIECES}
SCALE_AT = 1
SCATTER_AT = 4


def step_kernel(nc, a, out):
    f32, f32r, u32 = mybir.dt.float32, mybir.dt.float32r, mybir.dt.uint32
    ALU = mybir.AluOpType
    ACT = mybir.ActivationFunctionType
    AX = mybir.AxisListType.X
    ds = bass.ds

    w_ada = a["w_ada"][0].rearrange("(k p) n -> p k n", p=128)
    w_in = a["w_in"][0].rearrange("(k p) n -> p k n", p=128)
    w_att = a["w_att_proj"][0].rearrange("(k p) n -> p k n", p=128)
    w_out = a["w_out"][0].rearrange("(k p) n -> p k n", p=128)
    w_gate = a["w_gate_e"][0].rearrange("e (k p) f -> e p k f", p=128)
    w_up = a["w_up_e"][0].rearrange("e (k p) f -> e p k f", p=128)
    w_down = a["w_down_e"][0]
    xs = a["x_sample"][0].rearrange("(r j c) d -> j c r d", r=GRID_R, j=4)
    ys = out["y_sample"][0].rearrange("(r j c) d -> j c r d", r=GRID_R, j=4)
    rpb_flat = a["rpb"][0].rearrange("h r c -> (h r c)").rearrange("(a n) -> a n", a=1)
    NR = H * 15 * 31

    with ExitStack() as ctx:
        top = [-(-nc.sbuf_base // 64) * 64]

        def place(name, offset, shape, dt=f32):
            return nc.alloc_sbuf_tensor_at(name, shape, dt, offset=offset)

        def sb(name, shape, dt=f32):
            n = 4 * int(np.prod(shape[1:]))
            top[0] += -(-n // 32) * 32
            return place(name, top[0] - -(-n // 32) * 32, shape, dt)

        def sem(name):
            return ctx.enter_context(nc.semaphore(name))

        rpb_pad = nc.dram_tensor("rpb_pad", [1, NR + 32], f32, kind="Internal").ap()
        xn_rows = nc.dram_tensor("xn_rows", [TOK, D], f32, kind="Internal").ap()

        x = sb("x", [128, NT, D])
        keep = sb("keep", [128, 128])
        vecT = sb("vecT", [128, 90])
        modT = sb("modT", [128, 40, 2])
        scale1 = sb("scale1", [128, 8, 2])
        scale2 = sb("scale2", [128, 8, 2])
        small = sb("small", [128, 160])
        gates = sb("gates", [SLOTS, NE + 1])
        places = sb("places", [SLOTS, NE + 2])
        places_int = sb("places_int", [SLOTS, NE + 2], u32)
        place_now = sb("place_now", [SLOTS, 1], u32)

        shared = top[0]
        ring = place("ring", shared, [128, RING * SLOT])
        behind = shared + 4 * RING * SLOT
        mixer = place("mixer", shared, [128, RING * SLOT + 2 * WBUF * PIECE])
        w_hi = place("w_hi", behind, [128, WBUF, PIECE], f32r)
        w_lo = place("w_lo", behind + 4 * WBUF * PIECE, [128, WBUF, PIECE], f32r)
        behind += 8 * WBUF * PIECE
        misc = place("misc", behind, [128, 4640])
        hT_all = place("hT_all", behind + 4 * 4640, [128, KD, TOK])
        misc_r = place("misc_r", behind, [128, 4640], f32r)
        hT_r = place("hT_r", behind + 4 * 4640, [128, KD, TOK], f32r)
        end_of_mixer = behind + 4 * (4640 + KD * TOK)
        top[0] = behind
        x_rows = sb("x_rows", [SLOTS, D])
        xe_hi = sb("xe_hi", [128, KD, SLOTS], f32r)
        xe_lo = sb("xe_lo", [128, KD, SLOTS], f32r)
        hid = sb("hid", [SLOTS, 2, FC])
        hT_hi = sb("hT_hi", [128, 2, 4, SLOTS], f32r)
        hT_lo = sb("hT_lo", [128, 2, 4, SLOTS], f32r)
        y_f = sb("y_f", [128, D])
        y_hi = sb("y_hi", [SLOTS, D], f32r)
        y_lo = sb("y_lo", [SLOTS, D], f32r)
        back = sb("back", [SLOTS, TOK], f32r)
        iota = sb("iota", [SLOTS, TOK])
        gate2_row = sb("gate2_row", [SLOTS, D])
        assert max(top[0], end_of_mixer) <= nc.sbuf_usable_end

        slots = [ring[:, s * SLOT:(s + 1) * SLOT] for s in range(RING)]
        stream = [mixer[:, s * SLOT:(s + 1) * SLOT] for s in range(STREAM)]
        xe_f = y_f[:, 0:KD * SLOTS].rearrange("p (k s) -> p k s", s=SLOTS)

        def at(buf, start, *shape):
            n = 1
            for s in shape:
                n *= s
            v = buf[:, start:start + n]
            if len(shape) == 2:
                return v.rearrange("p (a b) -> p a b", b=shape[1])
            if len(shape) == 3:
                return v.rearrange("p (a b c) -> p a b c", b=shape[1], c=shape[2])
            return v

        ident = keep[:, 0:128]
        hT = hT_all[:, :, :]
        v_tok = at(mixer, 12288, NT, 512)
        v_mid = at(mixer, 14848, 3, 512)
        v_past = at(mixer, 16384, 2, 512)
        qT = at(mixer, 17408, 4, TOK)
        kT = at(mixer, 19968, 4, TOK + PAST)
        rpb_wide = at(mixer, 23552, H, GRID_R, 48)
        att = [at(mixer, 26624, 512), at(mixer, 35840, 512)]
        k_state = at(mixer, 26624, H, DH)
        attT = at(mixer, 27136, 4, TOK)
        k_past = at(mixer, 27136, 2, 512)
        bias = at(mixer, 29696, 3 * H, 32, GRID_R)
        gbT = at(mixer, 12288, KD, TOK)
        pooledT = at(mixer, 17408, 4, TOK)
        u_lat = at(mixer, 19968, 4, LAT + 2 * POOL_HALO)
        u_ctx = at(mixer, 22080, 4, CTX + 2 * POOL_HALO)
        win = [at(mixer, 22656, LAT + 2 * POOL_HALO), at(mixer, 23184, LAT + 2 * POOL_HALO)]
        w_pool = at(mixer, 24576, 4, 256)
        gate1_row = at(mixer, 29696, 2, D)
        gaT = at(mixer, 31744, KD, TOK)
        stream_r = [place(f"stream_r{s}", shared + 4 * SLOT * s, [128, KD, 512], f32r)[:, :, :] for s in range(STREAM)]
        h_hi, h_lo = stream_r[2], hT_r[:, :, 0:LAT]
        in_hi_a = place("in_hi_a", shared + 4 * 27136, [128, 5, 512], f32r)
        in_hi = [in_hi_a[:, k, :] for k in range(5)] + [misc_r[:, 512 * k:512 * (k + 1)] for k in range(3)]
        block_hi = [at(misc_r, 0, KD, 128), at(misc_r, 1024, KD, 128)]
        block_lo = [at(misc_r, 2048, KD, 128), at(misc_r, 3072, KD, 128)]
        att_hi_a = place("att_hi_a", shared + 4 * 25600, [128, 3, LAT], f32r)
        att_hi_b = place("att_hi_b", shared + 4 * 24064, [128, 1, LAT], f32r)
        att_hi = [att_hi_a[:, k, :] for k in range(3)] + [att_hi_b[:, 0, :]]
        att_lo = place("att_lo", shared + 4 * 27136, [128, 4, TOK], f32r)[:, :, 0:LAT]
        wa_hi = [at(misc_r, 512 * i, 4, 128) for i in range(2)]
        wa_lo = [at(misc_r, 1024 + 512 * i, 4, 128) for i in range(2)]
        merged_hi, merged_lo = [place(name, shared + 4 * o, [128, KD, TOK], f32r)[:, :, :]
                                for name, o in (("merged_hi", 12288), ("merged_lo", 31744))]
        out_hi = [place(f"out_hi{half}", shared + 4 * o, [128, KD, 512], f32r)[:, :, :]
                  for half, o in enumerate((19968, 25600))]
        out_lo = [stream_r[SLOT_OF[C_TAIL + 1 + half]] for half in range(2)]
        rows = misc[0:90, 3072:3200]
        xn = [at(misc, 0, D), at(misc, 1024, D)]
        squares = [at(misc, 2048, 512), at(misc, 2560, 512)]
        normed = [at(misc, 3072, 512), at(misc, 3584, 512)]
        probs = [at(misc, 0, 512), at(misc, 512, 512)]
        mod_row = at(misc, 2048, 2, 512)
        q_apart = misc[:, 2048:4096].rearrange("p (b o h n) -> p b o h n", b=2, o=2, h=4)
        probsT = [at(misc, 1024, 512), at(misc, 1536, 512)]
        diag = [at(misc, 3072, 4, 128), at(misc, 3584, 4, 128)]
        gated = at(misc, 0, D)
        h2T = at(misc, 1024, KD, 128)
        square_junk = at(misc, 2048, D)
        mask = at(misc, 4096, 3, 32)
        pool_fix = at(misc, 4192, 4, 2, 8)
        ones = at(misc, 4256, 128)
        slot_sets = misc[0:2, 4384:4384 + SLOTS]
        condT = at(misc, 4544, 2, KD)
        sigT = at(misc, 4560, 2 * KD)
        gT = at(misc, 4576, 1, 2)
        kg_row = at(mixer, 36352, DH)
        w_router = at(hT_all.rearrange("p k t -> p (k t)"), 4224, KD, NE)
        b_gate2 = hT_all.rearrange("p k t -> p (k t)")[0:2, 0:D]
        xn2 = [at(hT_all.rearrange("p k t -> p (k t)"), 1024 * (1 + i), D) for i in range(2)]
        aff = at(hT_all.rearrange("p k t -> p (k t)"), 3072, NT, NE)
        affN = misc[0:NE, 0:TOK]
        left = misc[0:NE, 640:640 + TOK]
        best = misc[0:NE, 1280:1280 + SLOTS]
        best_place = misc[0:NE, 1360:1360 + SLOTS]
        found = misc[0:NE, 1440:1440 + SLOTS].bitcast(u32)
        found_col = misc[0:NE, 1520:1520 + SLOTS].bitcast(u32)

        ss1, rs1 = small[:, 0:5], small[:, 5:10]
        ss_qk = [small[:, 16:24], small[:, 24:32]]
        rs_qk = [small[:, 32:40], small[:, 40:48]]
        negmax = small[:, 48:88]
        expsum = small[:, 88:128]
        negmax_c, expsum_c = small[:, 80:88], small[:, 120:128]
        ss2, rs2 = small[:, 128:133], small[:, 133:138]
        rmax, rsum = small[:, 138:143], small[:, 143:148]
        inv_sum = small[:, 148:156]

        ps = ctx.enter_context(nc.psum_tensor("ps", [128, 8, 512], f32))

        rows_loaded, consts_loaded = sem("rows_loaded"), sem("consts_loaded")
        x_loaded = [sem(f"x_loaded{t}") for t in range(NT)]
        past_loaded, pad_written, wide_loaded = sem("past_loaded"), sem("pad_written"), sem("wide_loaded")
        pool_loaded, mid_loaded, stored = sem("pool_loaded"), sem("mid_loaded"), sem("stored")
        kstate_stored = sem("kstate_stored")
        slot_loaded = [sem(f"slot_loaded{s}") for s in range(RING)]
        cond_loaded, cond_turned = sem("cond_loaded"), sem("cond_turned")
        vec_done, vec_ready = sem("vec_done"), sem("vec_ready")
        squared1, ms1_ready, root1, x_normed = sem("squared1"), sem("ms1_ready"), sem("root1"), sem("x_normed")
        x_turned, h_copied, h_ready = sem("x_turned"), sem("h_copied"), sem("h_ready")
        cond_sig, cond_ready = sem("cond_sig"), sem("cond_ready")
        mod_done, mod_copied, mod_turned = sem("mod_done"), sem("mod_copied"), sem("mod_turned")
        mod_ready, q_spread = sem("mod_ready"), sem("q_spread")
        row2_done = sem("row2_done")
        past_turned, past_ready = sem("past_turned"), sem("past_ready")
        proj_done, qk_squared, qk_ms, qk_root = sem("proj_done"), sem("qk_squared"), sem("qk_ms"), sem("qk_root")
        qk_normed, qk_turned, qkT_ready = sem("qk_normed"), sem("qk_turned"), sem("qkT_ready")
        v_copied, kstate_ready = sem("v_copied"), sem("kstate_ready")
        bias_ready = sem("bias_ready")
        scores_done, max_ready, probs_ready = sem("scores_done"), sem("max_ready"), sem("probs_ready")
        probs_turned, probsT_ready, pv_done = sem("probs_turned"), sem("probsT_ready"), sem("pv_done")
        att_scaled, att_turned, attT_ready = sem("att_scaled"), sem("att_turned"), sem("attT_ready")
        h_lat_ready, in_high, in_cut = sem("h_lat_ready"), sem("in_high"), sem("in_cut")
        h_cut_high, h_cut, block_high, block_cut = (sem("h_cut_high"), sem("h_cut"), sem("block_high"),
                                                    sem("block_cut"))
        halo_ready, gate_done, gate_copied = sem("halo_ready"), sem("gate_done"), sem("gate_copied")
        pooled_ready = sem("pooled_ready")
        diag_ready, row_done, row_copied = sem("diag_ready"), sem("row_done"), sem("row_copied")
        branches_done, merged = sem("branches_done"), sem("merged")
        att_high, att_cut, wa_high, wa_cut = sem("att_high"), sem("att_cut"), sem("wa_high"), sem("wa_cut")
        merged_high, merged_cut = sem("merged_high"), sem("merged_cut")
        out_high, out_cut = sem("out_high"), [sem("out_cut0"), sem("out_cut1")]
        out_done, x2_ready, squared2, ms2_ready, root2 = (sem("out_done"), sem("x2_ready"), sem("squared2"),
                                                          sem("ms2_ready"), sem("root2"))
        xn2_ready, xn2_turned, h2_ready, logits_done = (sem("xn2_ready"), sem("xn2_turned"), sem("h2_ready"),
                                                        sem("logits_done"))
        max2_ready, exp2_ready, aff_ready, aff_turned = (sem("max2_ready"), sem("exp2_ready"), sem("aff_ready"),
                                                         sem("aff_turned"))
        best_ready, best_turned = sem("best_ready"), sem("best_turned")
        router_loaded, bias2_loaded = sem("router_loaded"), sem("bias2_loaded")
        rows_saved = [sem("rows_saved0"), sem("rows_saved1")]
        gate2_ready, iota_loaded = sem("gate2_ready"), sem("iota_loaded")
        dve_step, pool_step = sem("dve_step"), sem("pool_step")
        hi_ready, lo_ready, pieces_used = sem("hi_ready"), sem("lo_ready"), sem("pieces_used")
        slots_refilled, gathers_begun = sem("slots_refilled"), sem("gathers_begun")
        place_ready, gathered, xe_turned = sem("place_ready"), sem("gathered"), sem("xe_turned")
        xe_scaled, xe_mod, xe_high, xe_ready = sem("xe_scaled"), sem("xe_mod"), sem("xe_high"), sem("xe_ready")
        silu_ready, h_done, h_turned = sem("silu_ready"), sem("h_done"), sem("h_turned")
        h_high, hT_ready = sem("h_high"), sem("hT_ready")
        y_scaled, y_high, y_ready = sem("y_scaled"), sem("y_high"), sem("y_ready")
        back_ready, scattered, added = sem("back_ready"), sem("scattered"), sem("added")

        block = ctx.enter_context(nc.Block())

        def chunk_read(i):
            if i < C_QKV:
                return mod_done, i + 1
            if i < C_GATES:
                return proj_done, NT * (i - C_QKV + 1)
            if i < C_ADA2:
                return gate_done, 4 * (i - C_GATES + 1)
            if i < C_TAIL:
                return mod_done, C_QKV + i - C_ADA2 + 1
            if i < C_ADA3:
                return (branches_done, KD) if i == C_TAIL else (out_done, 2 * NT)
            return mod_done, C_QKV + len(ADA2) + i - C_ADA3 + 1

        def chunk_slot(i):
            return at(mixer, SLOT_OF[i] * SLOT, KD, 512)

        def chunk_there(i):
            return slot_loaded[SLOT_OF[i]], 16 * SLOT_OF[:i + 1].count(SLOT_OF[i])

        def expert_dst(j):
            kind, c = ORDER[j]
            n = D if kind == "down" else width(c)
            blocks = len(fblocks(c)) if kind == "down" else KD
            return slots[j % RING][:, 0:blocks * n].rearrange("p (b n) -> p b n", n=n)

        def load_expert(eng, e, j, free_at=None):
            kind, c = ORDER[j]
            dst = expert_dst(j)
            if free_at is not None:
                eng.wait_ge(lo_ready, free_at)
                eng.sem_inc(slots_refilled, 1)
            if kind == "down":
                n = fblocks(c)[0][1]
                dst = dst[0:n]
                src = w_down[ds(e, 1), start(c):start(c) + width(c), :].rearrange("e (b p) n -> (e p) b n", p=n)
            else:
                w = w_gate if kind == "gate" else w_up
                src = w[ds(e, 1), :, :, start(c):start(c) + width(c)].rearrange("e p k f -> (e p) k f")
            eng.dma_start(dst, src).then_inc(slot_loaded[j % RING], 16)

        def arrived(e, j):
            return e * (16 * (len(ORDER) // RING)) + 16 * (USES[j % RING] + j // RING + 1)

        def piece_shape(p):
            j, kind, c, b0, nb = PIECES[p]
            return (fblocks(c)[0][1], nb * D) if kind == "down" else (128, nb * width(c))

        def piece(p):
            j, kind, c, b0, nb = PIECES[p]
            return expert_dst(j)[0:piece_shape(p)[0], b0:b0 + nb, :].rearrange("p b n -> p (b n)")

        def pieces_before(j):
            return len([p for p in PIECES if p[0] < j])

        def proj_bank(i):
            return i % 4 if i < 3 * NT - 1 else 3

        def out_low_part(eng, E, half, k):
            eng.wait_ge(out_high, half * KD + k + 1)
            E.tensor_tensor(out_lo[half][:, k, :], chunk_slot(C_TAIL + 1 + half)[:, k, :],
                            out_hi[half][:, k, :].bitcast(f32), ALU.subtract).then_inc(out_cut[half], 1)

        @block.sync
        def _(sp):
            def load_x(t):
                src = xs[t] if t < 4 else a["x_prompt"][0]
                sp.dma_start(x[:, t, :], src).then_inc(x_loaded[t], 16)

            sp.dma_start(rows[KD:2 * KD, :], a["c_ctx"].rearrange("(k p) -> k p", p=128)).then_inc(cond_loaded, 16)
            load_x(0)
            for i, (kind, n) in enumerate(CHUNKS[:C_ADA3]):
                s = SLOT_OF[i]
                if i == C_ADA2 + 2:
                    sp.wait_ge(*chunk_read(C_ADA2 - 1))
                elif s in SLOT_OF[:i]:
                    last = max(j for j in range(i) if SLOT_OF[j] == s)
                    sp.wait_ge(*chunk_read(last))
                if i == C_GATES + 1:
                    sp.wait_ge(v_copied, NT)
                    sp.dma_start(v_mid[0:64], v_tok[64:128, 0:3, :]).then_inc(mid_loaded, 16)
                    sp.dma_start(v_mid[64:128], v_tok[0:64, 1:4, :]).then_inc(mid_loaded, 16)
                    sp.dma_start(out["state_v"], v_tok[:, 4, :]).then_inc(stored, 16)
                    sp.wait_ge(kstate_ready, 1)
                    sp.dma_start(out["state_k"], k_state.rearrange("p h d -> p (h d)")).then_inc(kstate_stored, 16)
                if kind == "att":
                    sp.dma_start(stream[s].rearrange("p (k n) -> p k n", n=D), w_att).then_inc(slot_loaded[s], 16)
                else:
                    w = {"ada": w_ada, "in": w_in, "out": w_out}[kind]
                    sp.dma_start(chunk_slot(i), w[:, :, n * 512:(n + 1) * 512]).then_inc(slot_loaded[s], 16)
                if i < 2:
                    load_x(2 * i + 1)
                    load_x(2 * i + 2)
                if i == 2:
                    sp.dma_start(k_past, a["cache_k"][0, 0].rearrange("(t p) h d -> p t (h d)", p=128)
                                 ).then_inc(past_loaded, 16)
                    sp.dma_start(v_past, a["cache_v"][0, 0].rearrange("(t p) h d -> p t (h d)", p=128)
                                 ).then_inc(past_loaded, 16)
                if i == C_QKV + 1:
                    sp.wait_ge(pad_written, 48)
                    for r in range(GRID_R):
                        for h in range(H):
                            src = bass.AP(rpb_pad.tensor, (h * 15 + 7 - r) * 31, [[1, 16], [31, GRID_R], [1, 48]])
                            sp.dma_start(rpb_wide[r:128:GRID_R, h], src).then_inc(wide_loaded, 16)
                if i == C_ADA2 + 2:
                    sp.dma_start(w_pool, a["w_pool"][0].rearrange("g p n -> p g n")).then_inc(pool_loaded, 16)
            sp.wait_ge(gate_done, 20)
            sp.dma_start(w_router, a["w_router"][0].rearrange("(k p) n -> p k n", p=128)).then_inc(router_loaded, 16)
            sp.dma_start(b_gate2, a["b_ada"][:, 5 * D:6 * D].broadcast_to([2, D])).then_inc(bias2_loaded, 16)
            for i in range(C_ADA3, C_ADA3 + 2):
                sp.wait_ge(*((branches_done, KD) if i == C_ADA3 else (out_done, 2 * NT)))
                sp.dma_start(chunk_slot(i), w_ada[:, :, CHUNKS[i][1] * 512:(CHUNKS[i][1] + 1) * 512]
                             ).then_inc(slot_loaded[SLOT_OF[i]], 16)
            for j in (0, 1, 3, 4):
                load_expert(sp, 0, j)
            for i in range(C_ADA3, C_ADA3 + 2):
                sp.wait_ge(*chunk_read(i))
                if i > C_ADA3:
                    sp.wait_ge(gathered, 16)
                load_expert(sp, 0, SLOT_OF[i])
            sp.wait_ge(best_ready, 1)
            sp.wait_ge(rows_saved[0], 16 * 3)
            sp.wait_ge(rows_saved[1], 16 * 2)
            sp.dma_start(iota[:, :], a["const_iota"]).then_inc(iota_loaded, 16)
            J = len(ORDER)
            with sp.Fori(0, NE - 1) as e:
                for j in range(RING, J + RING):
                    free_at = e * NP + pieces_before(j - RING + 1)
                    load_expert(sp, e + j // J, j % J, free_at)
            for j in range(RING, J):
                load_expert(sp, NE - 1, j, (NE - 1) * NP + pieces_before(j - RING + 1))
            for t in range(NT):
                sp.wait_ge(added, 1 + NE * 2 * NT + 2 * (t + 1))
                sp.dma_start(ys[t] if t < 4 else out["y_prompt"][0], x[:, t, :]).then_inc(stored, 16)
            sp.wait_ge(stored, 16 * (NT + 1))
            sp.wait_ge(kstate_stored, 16)

        @block.tensor
        def _(pe):
            mm, tr = nc.tensor.matmul, nc.tensor.transpose

            def chunk_arrived(i):
                pe.wait_ge(*chunk_there(i))

            def product(m, bank, bias_row=None):
                i = [i for i, (kind, n) in enumerate(CHUNKS) if kind == "ada"][m]
                chunk_arrived(i)
                if bias_row is not None:
                    mm(ps[0:2, bank, :], ident[0:2, 0:2], bias_row, start=True, stop=False)
                for k in range(KD):
                    last = mm(ps[0:2, bank, :], condT[:, :, k], chunk_slot(i)[:, k, :],
                              start=(k == 0 and bias_row is None), stop=(k == KD - 1))
                last.then_inc(mod_done, 1)

            def turn_modulation(m, bank, o):
                pe.wait_ge(mod_copied, m + 1)
                for b in range(4):
                    last = tr(ps[:, bank, o + 2 * b:o + 2 * b + 2], mod_row[0:2, m % 2, b * 128:(b + 1) * 128],
                              ident[0:2, 0:2])
                last.then_inc(mod_turned, 1)

            def turn_x(t):
                pe.wait_ge(x_normed, t + 1)
                if t >= 3:
                    pe.wait_ge(h_copied, t - 2)
                for k in range(KD):
                    last = tr(ps[:, 2 * (t % 3) + k // 4, k % 4 * 128:(k % 4 + 1) * 128],
                              xn[t % 2][:, k * 128:(k + 1) * 128], ident)
                last.then_inc(x_turned, 1)

            pe.wait_ge(cond_loaded, 48)
            tr(ps[:, 7, 0:2 * KD], rows[0:2 * KD], ident[0:2 * KD, 0:2 * KD]).then_inc(cond_turned, 1)
            pe.wait_ge(cond_ready, 1)
            product(0, 6)
            turn_modulation(0, 7, 32)
            product(1, 6)
            turn_x(0)
            turn_x(1)
            turn_modulation(1, 7, 40)
            product(2, 6)
            turn_x(2)
            turn_x(3)
            turn_modulation(2, 7, 48)
            pe.wait_ge(rows_loaded, 128)
            tr(ps[:, 7, 128:218], rows, ident[0:90, 0:90]).then_inc(vec_done, 1)
            product(3, 6)
            turn_x(4)
            pe.wait_ge(vec_ready, 1)
            turn_modulation(3, 7, 56)
            pe.wait_ge(past_loaded, 32)
            pe.wait_ge(h_copied, 4)
            for t in range(2):
                for i in range(4):
                    last = tr(ps[:, 6 * t, i * 128:(i + 1) * 128], k_past[:, t, i * 128:(i + 1) * 128], ident)
                last.then_inc(past_turned, 1)
            pe.wait_ge(h_copied, NT)
            pe.wait_ge(past_ready, 1)
            NU = UNITS + 2

            def scores(u):
                if u >= 3:
                    pe.wait_ge(probs_ready, u - 2)
                j, h = divmod(u, H)
                if u % H == 0:
                    pe.wait_ge(q_spread, j + 1)
                if u < UNITS:
                    q = q_apart[:, j % 2, h % 2, h // 2, :]
                    b0 = WINDOW_BASE[j] * GRID_R
                    mm(ps[:, u % 3, 0:256], q, kT[:, h // 2, b0:b0 + 256], start=True, stop=True)
                    last = mm(ps[:, u % 3, 256:512], q, kT[:, h // 2, TOK:TOK + PAST], start=True, stop=True)
                else:
                    for i in range(4):
                        last = mm(ps[:, u % 3, i * 128:(i + 1) * 128], q_apart[:, j % 2, u - UNITS, i, :],
                                  kT[:, i, LAT:TOK], start=True, stop=True)
                last.then_inc(scores_done, 1)

            for i in range(3 * NT + 1):
                if i < 3 * NT:
                    if i % NT == 0:
                        chunk_arrived(C_QKV + i // NT)
                    if 4 <= i < 2 * NT + 4:
                        pe.wait_ge(qk_normed, i - 3)
                    elif i == 3 * NT - 1:
                        pe.wait_ge(v_copied, 3)
                        pe.wait_ge(qkT_ready, 2 * NT)
                        pe.wait_ge(past_ready, 2)
                        scores(0)
                    t, w = TILES[i % NT], chunk_slot(C_QKV + i // NT)
                    tile = slice(t * 128, (t + 1) * 128)
                    if t == NT - 1:
                        for k in range(KD):
                            if i == 0:
                                pe.wait_ge(h_ready, k + 1)
                            last = mm(ps[:, proj_bank(i), :], hT[:, k, tile], w[:, k, :],
                                      start=(k == 0), stop=(k == KD - 1))
                    else:
                        for k in range(KD):
                            if i % NT == 1:
                                pe.wait_ge(in_high, i // NT * KD + k + 1)
                            if i == 1:
                                pe.wait_ge(h_cut, k + 1)
                            mm(ps[:, proj_bank(i), :], h_hi[:, k, tile], in_hi[k], start=(k == 0), stop=False)
                            mm(ps[:, proj_bank(i), :], h_lo[:, k, tile], in_hi[k], start=False, stop=False)
                        for k in range(KD):
                            if i % NT == 1:
                                pe.wait_ge(in_cut, i // NT * KD + k + 1)
                            last = mm(ps[:, proj_bank(i), :], h_hi[:, k, tile],
                                      stream_r[SLOT_OF[C_QKV + i // NT]][:, k, :], start=False, stop=(k == KD - 1))
                    last.then_inc(proj_done, 1)
                if 1 <= i <= 2 * NT:
                    m = i - 1
                    pe.wait_ge(qk_normed, m + 1)
                    if m >= 2:
                        pe.wait_ge(qkT_ready, m - 1)
                    for hp in range(4):
                        last = tr(ps[:, 4 + m % 2, hp * 128:(hp + 1) * 128],
                                  normed[m % 2][:, hp * 128:(hp + 1) * 128], ident)
                    last.then_inc(qk_turned, 1)

            pe.wait_ge(v_copied, NT - 1)
            for u in range(NU + 3):
                if 1 <= u < NU:
                    scores(u)
                if 1 <= u <= NU:
                    m = u - 1
                    pe.wait_ge(probs_ready, m + 1)
                    if m == 0:
                        pe.wait_ge(v_copied, NT)
                    if m >= 2:
                        pe.wait_ge(probsT_ready, m - 1)
                    for i in range(4):
                        cols = slice(i * 128, (i + 1) * 128)
                        last = tr(ps[:, 3 + m % 2, cols], probs[m % 2][:, cols], ident)
                    last.then_inc(probs_turned, 1)
                if 2 <= u <= NU + 1:
                    m = u - 2
                    pe.wait_ge(probsT_ready, m + 1)
                    j = m // H
                    if m == H:
                        pe.wait_ge(mid_loaded, 32)
                    if m % H == 0 and j >= 2:
                        pe.wait_ge(att_scaled, j - 1)
                    if m < UNITS:
                        h = m % H
                        vk = [[v_tok[:, 0], v_tok[:, 1]], [v_mid[:, 0], v_mid[:, 1]],
                              [v_mid[:, 1], v_mid[:, 2]], [v_tok[:, 2], v_tok[:, 3]]][j] + [v_past[:, 0], v_past[:, 1]]
                        for i in range(4):
                            last = mm(ps[:, 5 + j % 2, h * DH:(h + 1) * DH], probsT[m % 2][:, i * 128:(i + 1) * 128],
                                      vk[i][:, h * DH:(h + 1) * DH], start=(i == 0), stop=(i == 3))
                    else:
                        for i in range(4):
                            h = 2 * i + m - UNITS
                            last = mm(ps[:, 5, h * DH:(h + 1) * DH], probsT[m % 2][:, i * 128:(i + 1) * 128],
                                      v_tok[:, 4, h * DH:(h + 1) * DH], start=True, stop=True)
                    last.then_inc(pv_done, 1)
                if u >= 3 and (u - 3) % H == H - 1 or u == NU + 2:
                    j = min((u - 3) // H, 4)
                    pe.wait_ge(att_scaled, j + 1)
                    if j:
                        pe.wait_ge(attT_ready, j)
                    for i in range(4):
                        last = tr(ps[:, 7, i * 128:(i + 1) * 128], att[j % 2][:, i * 128:(i + 1) * 128], ident)
                    last.then_inc(att_turned, 1)

            pe.wait_ge(probs_ready, NU)
            pe.wait_ge(probsT_ready, NU)
            pe.wait_ge(att_scaled, 5)
            for i in range(20):
                c = C_GATES + i // 4
                if i % 4 == 0:
                    chunk_arrived(c)
                if i >= 3:
                    pe.wait_ge(gate_copied, 2 * (i - 2))
                w = chunk_slot(c)
                pe.wait_ge(block_cut, i + 1)
                for k in range(KD):
                    for n, (wb, h) in enumerate(((block_hi, h_hi), (block_hi, h_lo), (block_lo, h_hi))):
                        mm(ps[:, i % 3, :], wb[i % 2][:, k, :], h[:, k, :], start=(k == 0 and n == 0),
                           stop=(k == KD - 1 and n == 2))
                    last = mm(ps[:, 3 + i % 3, 0:CTX], w[:, k, i % 4 * 128:(i % 4 + 1) * 128], hT[:, k, LAT:TOK],
                              start=(k == 0), stop=(k == KD - 1))
                last.then_inc(gate_done, 1)

            pe.wait_ge(gate_copied, 38)
            pe.wait_ge(attT_ready, 5)
            for m in range(C_QKV, C_QKV + len(ADA2) + 1):
                if m < C_QKV + len(ADA2):
                    product(m, (2, 5)[m % 2])
                if m > C_QKV:
                    turn_modulation(m - 1, 6 if m - 1 >= GATE1_END else 0, 8 * (m - 1))
                i = m - GATE1_END - 1
                if 0 <= i < 4:
                    pe.wait_ge(diag_ready, i + 1)
                    if i:
                        pe.wait_ge(row_copied, i)
                    mm(ps[:, 7, :], ones, diag[i % 2], start=True, stop=True).then_inc(row_done, 1)
            chunk_arrived(C_TAIL)
            pe.wait_ge(pool_loaded, 16)
            pe.wait_ge(pooled_ready, 2 * 4)
            pe.wait_ge(gate_copied, 40)
            pe.wait_ge(att_cut, 4)
            wa = stream[SLOT_OF[C_TAIL]].rearrange("p (k n) -> p k n", n=D)
            for n in range(KD):
                if n == 1:
                    pe.wait_ge(mod_ready, 1)
                    pe.wait_ge(row_copied, 4)
                if n >= 2:
                    pe.wait_ge(merged, n - 1)
                b = n % 2 * 4
                pe.wait_ge(wa_cut, n + 1)
                for k in range(4):
                    for i, (w, h) in enumerate(((wa_hi, att_hi[k]), (wa_hi, att_lo[:, k, :]), (wa_lo, att_hi[k]))):
                        mm(ps[:, b, :], w[n % 2][:, k, :], h, start=(k == 0 and i == 0), stop=(k == 3 and i == 2))
                    last = mm(ps[:, b + 1, 0:CTX], wa[:, k, n * 128:(n + 1) * 128], attT[:, k, LAT:TOK],
                              start=(k == 0), stop=(k == 3))
                lhsT = w_pool[:, n // 2, n % 2 * 128:(n % 2 + 1) * 128]
                mm(ps[:, b + 2, :], lhsT, pooledT[:, n // 2, 0:LAT], start=True, stop=True)
                last2 = mm(ps[:, b + 3, 0:CTX], lhsT, pooledT[:, n // 2, LAT:TOK], start=True, stop=True)
                last2.then_inc(branches_done, 1)
            pe.wait_ge(merged, KD)
            pe.wait_ge(router_loaded, 16)
            def router(m):
                pe.wait_ge(h2_ready, m + 1)
                for k in range(KD):
                    last = mm(ps[:, 6, m * NE:(m + 1) * NE], h2T[:, k, :], w_router[:, k, :],
                              start=(k == 0), stop=(k == KD - 1))
                last.then_inc(logits_done, 1)

            def turn_normed(m):
                if m:
                    pe.wait_ge(h2_ready, m)
                pe.wait_ge(xn2_ready, m + 1)
                for k in range(KD):
                    last = tr(ps[:, 4 + k // 4, k % 4 * 128:(k % 4 + 1) * 128],
                              xn2[m % 2][:, k * 128:(k + 1) * 128], ident)
                last.then_inc(xn2_turned, 1)

            for t in range(NT):
                if t >= 2:
                    pe.wait_ge(x2_ready, t - 1)
                for half in range(2):
                    for k in range(KD):
                        if t == 0:
                            pe.wait_ge(merged_cut, k + 1)
                            pe.wait_ge(out_cut[half], k + 1)
                        for n, (h, w) in enumerate(((merged_hi, out_hi), (merged_lo, out_hi), (merged_hi, out_lo))):
                            last = mm(ps[:, t % 2 * 2 + half, :], h[:, k, t * 128:(t + 1) * 128], w[half][:, k, :],
                                      start=(k == 0 and n == 0), stop=(k == KD - 1 and n == 2))
                    last.then_inc(out_done, 1)
                    if half == 0 and t:
                        turn_normed(t - 1)
                if t:
                    router(t - 1)
            turn_normed(NT - 1)
            router(NT - 1)
            pe.wait_ge(aff_ready, 1)
            for t in range(NT):
                last = tr(ps[0:NE, 7 if t < 4 else 4, t % 4 * 128:(t % 4 + 1) * 128], aff[:, t, :], ident)
            last.then_inc(aff_turned, 1)
            pe.wait_ge(x2_ready, NT)
            pe.wait_ge(squared2, NT)
            pe.wait_ge(bias2_loaded, 16)
            for half in range(2):
                product(C_QKV + len(ADA2) + half, half, b_gate2[:, half * 512:(half + 1) * 512])
            for half in range(2):
                m = C_QKV + len(ADA2) + half
                pe.wait_ge(mod_copied, m + 1)
                mm(ps[0:SLOTS, 2 + half, :], slot_sets, mod_row[0:2, m % 2, :], start=True, stop=True
                   ).then_inc(row2_done, 1)
            pe.wait_ge(best_ready, 1)
            tr(ps[0:SLOTS, 5, 0:NE], best, ident[0:NE, 0:NE])
            tr(ps[0:SLOTS, 5, NE:2 * NE], best_place, ident[0:NE, 0:NE]).then_inc(best_turned, 1)

            def turn_gathered(e):
                pe.wait_ge(gathered, 16 * (e + 1))
                for d in range(KD):
                    last = tr(ps[:, d // 4 * 2, d % 4 * SLOTS:(d % 4 + 1) * SLOTS], x_rows[:, d * 128:(d + 1) * 128],
                              ident[0:SLOTS, 0:SLOTS])
                last.then_inc(xe_turned, 1)

            def turn_hidden(e, c):
                pe.wait_ge(h_done, e * NCH + c + 1)
                for b, (f, n) in enumerate(fblocks(c)):
                    last = tr(ps[0:n, 6, b * SLOTS:(b + 1) * SLOTS], hid[:, c % 2, f:f + n], ident[0:SLOTS, 0:SLOTS])
                last.then_inc(h_turned, 1)

            def scatter(e, i, bank=7, banks=1):
                if i >= banks or banks == 1:
                    pe.wait_ge(added, e * 2 * NT + i + 2 - banks)
                t, half = divmod(i, 2)
                for n, y in enumerate((y_hi, y_lo)):
                    last = mm(ps[:, bank, :], back[:, t * 128:(t + 1) * 128], y[:, half * 512:(half + 1) * 512],
                              start=(n == 0), stop=(n == 1))
                last.then_inc(scattered, 1)

            pe.wait_ge(gate2_ready, 2)
            turn_gathered(0)
            with pe.Fori(0, NE) as e:
                for p, (j, kind, c, b0, nb) in enumerate(PIECES):
                    hi, lo = w_hi[:, p % WBUF, :], w_lo[:, p % WBUF, :]
                    last_piece = p == LAST[kind, c]
                    if kind == "down":
                        if p == FIRST[kind, c]:
                            pe.wait_ge(hT_ready, e * NCH + c + 1)
                            if c == 0:
                                pe.wait_ge(y_scaled, e + 1)
                        kb = fblocks(c)[0][1]
                        first_of_all, last_of_all = c == 0 and b0 == 0, c == NCH - 1 and last_piece
                        pairs = [(hT_hi, hi), (hT_lo, hi)], [(hT_hi, lo)]
                        for part in range(2):
                            pe.wait_ge((hi_ready, lo_ready)[part], e * NP + p + 1)
                            for b in range(nb):
                                for half in range(2):
                                    for n, (h, w) in enumerate(pairs[part]):
                                        last = mm(ps[0:SLOTS, 4 + half, :], h[0:kb, c % 2, b0 + b, :],
                                                  w[0:kb, b * D + half * 512:b * D + (half + 1) * 512],
                                                  start=(first_of_all and part == 0 and b == 0 and n == 0),
                                                  stop=(last_of_all and part == 1 and b == nb - 1))
                    else:
                        bank, w0 = c % 2 + (2 if kind == "up" else 0), width(c)
                        if p == FIRST[kind, c]:
                            if c < 2:
                                pe.wait_ge(xe_ready, e + 1)
                            else:
                                pe.wait_ge(h_done, e * NCH + c - 1)
                        pairs = [(xe_hi, hi), (xe_lo, hi)], [(xe_hi, lo)]
                        for part in range(2):
                            pe.wait_ge((hi_ready, lo_ready)[part], e * NP + p + 1)
                            for b in range(nb):
                                for n, (h, w) in enumerate(pairs[part]):
                                    last = mm(ps[0:SLOTS, bank, 0:w0], h[:, b0 + b, :], w[:, b * w0:(b + 1) * w0],
                                              start=(b0 + b == 0 and part == 0 and n == 0),
                                              stop=(last_piece and part == 1 and b == nb - 1))
                    last.then_inc(pieces_used, 1)
                    if 0 <= p - SCATTER_AT < 2 * NT:
                        if p == SCATTER_AT:
                            pe.wait_ge(y_ready, e + 1)
                            pe.wait_ge(back_ready, e + 1)
                        scatter(e, p - SCATTER_AT)
                    if kind == "gate" and c >= 1 and last_piece:
                        turn_hidden(e, c - 1)
                    if (kind, c) == ("up", NCH - 1) and last_piece:
                        turn_gathered(e + 1)
                    if p == FIRST["down", NCH - 2]:
                        turn_hidden(e, NCH - 1)
            pe.wait_ge(y_ready, NE + 1)
            pe.wait_ge(back_ready, NE + 1)
            for i in range(2 * NT):
                scatter(NE, i, i % 4, 4)

        @block.scalar
        def _(act):
            A = nc.scalar.activation

            def load_rows(name, r, loaded):
                src = a[name][0]
                act.dma_start(rows[r:r + src.shape[0] // 128, :], src.rearrange("(k p) -> k p", p=128)
                              ).then_inc(loaded, 16)

            act.dma_start(keep[:, :], a["const_keep"]).then_inc(cond_loaded, 16)
            load_rows("c", 0, cond_loaded)
            for name, r in (("norm1_g", 16), ("norm2_g", 24), ("pool_scale", 32), ("b_ada", 40)):
                load_rows(name, r, rows_loaded)
            for i, name in enumerate(("q_norm_g", "k_norm_g")):
                for half in range(2):
                    act.dma_start(rows[88 + i:89 + i, half * DH:(half + 1) * DH], a[name]).then_inc(rows_loaded, 16)
            act.dma_start(misc[:, 4096:4544], a["const_mixer"]).then_inc(consts_loaded, 16)
            act.dma_start(kg_row, a["k_norm_g"].broadcast_to([128, DH])).then_inc(consts_loaded, 16)
            act.dma_start(rpb_pad[:, 16:16 + NR], rpb_flat).then_inc(pad_written, 16)
            act.dma_start(rpb_pad[:, 0:16], rpb_flat[:, 0:16]).then_inc(pad_written, 16)
            act.dma_start(rpb_pad[:, 16 + NR:32 + NR], rpb_flat[:, NR - 16:NR]).then_inc(pad_written, 16)

            def copy_modulation(m, bank):
                act.wait_ge(mod_done, m + 1)
                A(mod_row[0:2, m % 2, :], ps[0:2, bank, :], ACT.Copy).then_inc(mod_copied, 1)

            def copy_h(t):
                act.wait_ge(x_turned, t + 1)
                b = 2 * (t % 3)
                A(hT[:, :, t * 128:(t + 1) * 128].rearrange("p (a k) n -> p a k n", a=2),
                  ps[:, b:b + 2, :].rearrange("p a (k n) -> p a k n", n=128), ACT.Copy).then_inc(h_copied, 1)

            act.wait_ge(cond_turned, 1)
            A(sigT, ps[:, 7, 0:2 * KD], ACT.Sigmoid).then_inc(cond_sig, 1)
            copy_modulation(0, 6)
            for t in range(NT):
                act.wait_ge(x_loaded[t], 16)
                A(xn[t % 2], x[:, t, :], ACT.Square, accum_out=ss1[:, t:t + 1]).then_inc(squared1, 1)
                act.wait_ge(squared1, t + 1)
            act.wait_ge(ms1_ready, 1)
            A(rs1, ss1, ACT.Sqrt).then_inc(root1, 1)
            copy_modulation(1, 6)
            copy_h(0)
            copy_h(1)
            copy_modulation(2, 6)
            copy_h(2)
            copy_h(3)
            copy_modulation(3, 6)
            copy_h(4)
            for t in range(2):
                act.wait_ge(past_turned, t + 1)
                A(kT[:, :, TOK + t * 128:TOK + (t + 1) * 128],
                  ps[:, 6 * t, :].rearrange("p (k n) -> p k n", n=128), ACT.Copy).then_inc(past_ready, 1)


            def in_high_part(c, k):
                if k == 0:
                    act.wait_ge(*chunk_there(C_QKV + c))
                A(in_hi[k], chunk_slot(C_QKV + c)[:, k, :], ACT.Copy).then_inc(in_high, 1)

            for k in range(KD):
                in_high_part(0, k)
                act.wait_ge(h_lat_ready, k + 1)
                A(h_hi[:, k, :], hT[:, k, 0:LAT], ACT.Copy).then_inc(h_cut_high, 1)

            def turned_out(m):
                act.wait_ge(qk_turned, m + 1)
                t = TILES[m % NT]
                dst = (kT, qT)[m // NT][:, :, t * 128:(t + 1) * 128]
                A(dst, ps[:, 4 + m % 2, :].rearrange("p (k n) -> p k n", n=128), ACT.Copy,
                  scale=gT[:, 0, 1 - m // NT:2 - m // NT]).then_inc(qkT_ready, 1)

            for i in range(3 * NT):
                act.wait_ge(proj_done, i + 1)
                if i < 2 * NT:
                    if i >= 2:
                        act.wait_ge(qk_ms, i - 1)
                    A(squares[i % 2], ps[:, i % 4, :], ACT.Square).then_inc(qk_squared, 1)
                    act.wait_ge(qk_ms, i + 1)
                    A(rs_qk[i % 2], ss_qk[i % 2], ACT.Sqrt).then_inc(qk_root, 1)
                else:
                    A(v_tok[:, TILES[i - 2 * NT], :], ps[:, proj_bank(i), :], ACT.Copy).then_inc(v_copied, 1)
                if 1 <= i <= 2 * NT:
                    turned_out(i - 1)
                if i % NT == NT - 1 and i < 2 * NT:
                    for k in range(KD):
                        in_high_part(i // NT + 1, k)

            NU = UNITS + 2

            def block_high_part(i):
                c = C_GATES + i // 4
                if i % 4 == 0:
                    act.wait_ge(*chunk_there(c))
                A(block_hi[i % 2], chunk_slot(c)[:, :, i % 4 * 128:(i % 4 + 1) * 128], ACT.Copy).then_inc(block_high, 1)

            for u in range(NU + 1):
                if u < NU:
                    act.wait_ge(max_ready, u + 1)
                    if u >= 2:
                        act.wait_ge(probs_turned, u - 1)
                    if u < UNITS:
                        A(probs[u % 2], ps[:, u % 3, :], ACT.Exp, bias=negmax[:, u:u + 1],
                          accum_out=expsum[:, u:u + 1]).then_inc(probs_ready, 1)
                    else:
                        for i in range(4):
                            h = 2 * i + u - UNITS
                            last = A(probs[u % 2][:, i * 128:(i + 1) * 128], ps[:, u % 3, i * 128:(i + 1) * 128],
                                     ACT.Exp, bias=negmax_c[:, h:h + 1], accum_out=expsum_c[:, h:h + 1])
                        last.then_inc(probs_ready, 1)
                if u >= 1:
                    m = u - 1
                    act.wait_ge(probs_turned, m + 1)
                    if m >= 2:
                        act.wait_ge(pv_done, m - 1)
                    A(probsT[m % 2], ps[:, 3 + m % 2, :], ACT.Copy).then_inc(probsT_ready, 1)

            block_high_part(0)
            act.wait_ge(pv_done, NU)
            block_high_part(1)
            act.wait_ge(halo_ready, 2)
            act.wait_ge(attT_ready, 5)
            for i in range(20):
                act.wait_ge(gate_done, i + 1)
                if i < 18:
                    block_high_part(i + 2)
                if i >= 16:
                    k = i - 16
                    A(att_hi[k], attT[:, k, 0:LAT], ACT.Copy).then_inc(att_high, 1)
                lat, con = ps[:, i % 3, :], ps[:, 3 + i % 3, 0:CTX]
                if i < 4:
                    A(u_lat[:, i, POOL_HALO:POOL_HALO + LAT].rearrange("p (r c) -> p r c", c=GRID_W),
                      lat.rearrange("p (c r) -> p r c", r=GRID_R), ACT.Copy).then_inc(gate_copied, 1)
                    A(u_ctx[:, i, POOL_HALO:POOL_HALO + CTX], con, ACT.Copy).then_inc(gate_copied, 1)
                else:
                    g = (gaT if i < 12 else gbT)[:, (i - 4) % KD, :]
                    A(g[:, 0:LAT], lat, ACT.Sigmoid).then_inc(gate_copied, 1)
                    A(g[:, LAT:TOK], con, ACT.Sigmoid).then_inc(gate_copied, 1)
            for m in range(C_QKV, C_QKV + len(ADA2) + 1):
                if m < C_QKV + len(ADA2):
                    copy_modulation(m, (2, 5)[m % 2])
                i = m - GATE1_END - 1
                if 0 <= i < 4:
                    act.wait_ge(row_done, i + 1)
                    A(gate1_row[:, i // 2, i % 2 * 512:(i % 2 + 1) * 512], ps[:, 7, :], ACT.Copy
                      ).then_inc(row_copied, 1)

            def out_high_part(half):
                c = C_TAIL + 1 + half
                act.wait_ge(*chunk_there(c))
                for k in range(KD):
                    A(out_hi[half][:, k, :], chunk_slot(c)[:, k, :], ACT.Copy).then_inc(out_high, 1)

            def wa_high_part(n):
                cols = stream[SLOT_OF[C_TAIL]].rearrange("p (k n) -> p k n", n=D)[:, :, n * 128:(n + 1) * 128]
                A(wa_hi[n % 2], cols, ACT.Copy).then_inc(wa_high, 1)

            act.wait_ge(*chunk_there(C_TAIL))
            wa_high_part(0)
            wa_high_part(1)
            act.wait_ge(pooled_ready, 8)
            out_high_part(0)
            for n in range(KD):
                if n < KD - 2:
                    act.wait_ge(branches_done, n + 1)
                    wa_high_part(n + 2)
                act.wait_ge(merged, n + 1)
                A(merged_hi[:, n, :], gaT[:, n, :], ACT.Copy).then_inc(merged_high, 1)
            act.wait_ge(branches_done, KD)
            out_high_part(1)
            for t in range(NT + 1):
                if t >= 1:
                    m = t - 1
                    act.wait_ge(xn2_turned, m + 1)
                    if m:
                        act.wait_ge(logits_done, m)
                    for k in range(KD):
                        last = A(h2T[:, k, :], ps[:, 4 + k // 4, k % 4 * 128:(k % 4 + 1) * 128], ACT.Identity,
                                 scale=scale2[:, k, m // 4:m // 4 + 1], bias=modT[:, 24 + k, m // 4:m // 4 + 1])
                    last.then_inc(h2_ready, 1)
                if t < NT:
                    act.wait_ge(x2_ready, t + 1)
                    A(square_junk, x[:, t, :], ACT.Square, accum_out=ss2[:, t:t + 1]).then_inc(squared2, 1)
                    act.wait_ge(ms2_ready, t + 1)
                    A(rs2[:, t:t + 1], ss2[:, t:t + 1], ACT.Sqrt).then_inc(root2, 1)
                    act.wait_ge(xn2_ready, t + 1)
                    act.dma_start(xn_rows[t * 128:(t + 1) * 128, :], xn2[t % 2]
                                  ).then_inc(rows_saved[t % 2], 16)
            act.wait_ge(max2_ready, 1)
            A(aff, aff, ACT.Exp).then_inc(exp2_ready, 1)
            for half in range(2):
                copy_modulation(C_QKV + len(ADA2) + half, half)
            for half in range(2):
                act.wait_ge(row2_done, half + 1)
                A(gate2_row[:, half * 512:(half + 1) * 512], ps[0:SLOTS, 2 + half, :], ACT.Copy
                  ).then_inc(gate2_ready, 1)

            def high_columns(e):
                act.wait_ge(xe_mod, e + 1)
                A(xe_hi[:, :, :], xe_f, ACT.Copy).then_inc(xe_high, 1)

            def silu(e, c):
                act.wait_ge(pieces_used, WBUF + e * NP + LAST["gate", c] + 1)
                if c < 2:
                    act.wait_ge(h_turned, e * NCH + NCH)
                else:
                    act.wait_ge(h_turned, e * NCH + NCH + c - 1)
                A(hid[:, c % 2, 0:width(c)], ps[0:SLOTS, c % 2, 0:width(c)], ACT.Silu).then_inc(silu_ready, 1)

            def high_hidden(e, c):
                act.wait_ge(h_turned, e * NCH + NCH + c + 1)
                kb, nb = fblocks(c)[0][1], len(fblocks(c))
                A(hT_hi[0:kb, c % 2, 0:nb, :], ps[0:kb, 6, 0:nb * SLOTS].rearrange("p (b s) -> p b s", s=SLOTS),
                  ACT.Copy).then_inc(h_high, 1)

            def high_rows(e):
                act.wait_ge(y_scaled, e + 1)
                act.wait_ge(scattered, 2 * NT * (e + 1))
                A(y_hi[:, :], y_f[0:SLOTS, :], ACT.Copy).then_inc(y_high, 1)

            high_columns(0)
            with act.Fori(0, NE) as e:
                for p, (j, kind, c, b0, nb) in enumerate(PIECES):
                    if p == FIRST[kind, c]:
                        act.wait_ge(slot_loaded[j % RING], arrived(e, j))
                    act.wait_ge(pieces_used, e * NP + p + 1)
                    rows_, n = piece_shape(p)
                    A(w_hi[0:rows_, p % WBUF, 0:n], piece(p), ACT.Copy).then_inc(hi_ready, 1)
                    for cc in range(NCH):
                        if cc < NCH - 1 and p == LAST["up", cc + 1]:
                            high_hidden(e, cc)
                        if p == LAST["gate", cc] + 2:
                            silu(e, cc)
                    if p == SCALE_AT + 1:
                        high_rows(e)
                    if p == FIRST["down", NCH - 1]:
                        high_columns(e + 1)
                        high_hidden(e, NCH - 1)
            high_rows(NE)

        @block.vector
        def _(dve):
            V = nc.vector
            steps = [0]

            def then(ins):
                steps[0] += 1
                ins.then_inc(dve_step, 1)
                dve.wait_ge(dve_step, steps[0])

            dve.wait_ge(cond_sig, 1)
            V.tensor_tensor(condT.rearrange("p a k -> p (a k)"), sigT, ps[:, 7, 0:2 * KD], ALU.mult
                            ).then_inc(cond_ready, 1)
            dve.wait_ge(squared1, NT)
            V.tensor_scalar(ss1, ss1, 1.0 / D, EPS, ALU.mult, ALU.add).then_inc(ms1_ready, 1)
            dve.wait_ge(root1, 1)
            then(V.reciprocal(rs1, rs1))
            for t in range(NT):
                if t >= 2:
                    dve.wait_ge(x_turned, t - 1)
                V.tensor_scalar(xn[t % 2], x[:, t, :], rs1[:, t:t + 1], None, ALU.mult).then_inc(x_normed, 1)
            dve.wait_ge(vec_done, 1)
            V.tensor_copy(vecT[:, :], ps[:, 7, 128:218]).then_inc(vec_ready, 1)
            dve.wait_ge(vec_ready, 1)
            V.tensor_scalar(gT[:, 0, 0:1], vecT[:, 88:89], DH ** -0.5, None, ALU.mult)
            V.tensor_copy(gT[:, 0, 1:2], vecT[:, 89:90])
            b_ada = vecT[:, 40:88]
            dve.wait_ge(mod_turned, C_QKV)
            then(V.tensor_tensor(modT[:, 0:16, :], ps[:, 7, 32:64].rearrange("p (n c) -> p n c", c=2),
                                 b_ada[:, 0:16].unsqueeze(2).broadcast_to([128, 16, 2]), ALU.add))
            then(V.scalar_tensor_tensor(scale1[:, :, :], modT[:, 8:16, :], 1.0,
                                        vecT[:, 16:24].unsqueeze(2).broadcast_to([128, 8, 2]), ALU.add, ALU.mult))
            dve.wait_ge(h_copied, NT)
            for k in range(KD):
                V.tensor_scalar(hT[:, k, LAT:TOK], hT[:, k, LAT:TOK], scale1[:, k, 1:2], modT[:, k, 1:2],
                                ALU.mult, ALU.add).then_inc(h_ready, 1)
            for k in range(KD):
                V.tensor_scalar(hT[:, k, 0:LAT], hT[:, k, 0:LAT], scale1[:, k, 0:1], modT[:, k, 0:1], ALU.mult, ALU.add
                                ).then_inc(h_lat_ready, 1)
            for k in range(KD):
                dve.wait_ge(h_cut_high, k + 1)
                V.tensor_tensor(h_lo[:, k, :], hT[:, k, 0:LAT], h_hi[:, k, :].bitcast(f32), ALU.subtract
                                ).then_inc(h_cut, 1)

            def in_low_parts(c):
                dve.wait_ge(proj_done, NT * c + 1)
                for k in range(KD):
                    dve.wait_ge(in_high, c * KD + k + 1)
                    V.tensor_tensor(stream_r[SLOT_OF[C_QKV + c]][:, k, :], chunk_slot(C_QKV + c)[:, k, :],
                                    in_hi[k].bitcast(f32), ALU.subtract).then_inc(in_cut, 1)

            for i in range(2 * NT):
                if i % NT == 0:
                    in_low_parts(i // NT)
                dve.wait_ge(qk_squared, i + 1)
                then(V.tensor_reduce(ss_qk[i % 2], squares[i % 2].rearrange("p (h d) -> p h d", d=DH), AX, ALU.add))
                V.tensor_scalar(ss_qk[i % 2], ss_qk[i % 2], 1.0 / DH, EPS, ALU.mult, ALU.add).then_inc(qk_ms, 1)
                dve.wait_ge(qk_root, i + 1)
                then(V.reciprocal(rs_qk[i % 2], rs_qk[i % 2]))
                if i >= 2:
                    dve.wait_ge(qk_turned, i - 1)
                V.tensor_tensor(normed[i % 2].rearrange("p (h d) -> p h d", d=DH),
                                ps[:, i % 4, :].rearrange("p (h d) -> p h d", d=DH),
                                rs_qk[i % 2].unsqueeze(2).broadcast_to([128, H, DH]), ALU.mult).then_inc(qk_normed, 1)
                if i == 0:
                    dve.wait_ge(qk_normed, 1)
                    dve.wait_ge(consts_loaded, 32)
                    V.tensor_tensor(k_state, normed[i % 2].rearrange("p (h d) -> p h d", d=DH),
                                    kg_row.unsqueeze(1).broadcast_to([128, H, DH]), ALU.mult).then_inc(kstate_ready, 1)
            in_low_parts(2)
            NU = UNITS + 2
            dve.wait_ge(bias_ready, 3)

            def finish_tile(j):
                dve.wait_ge(pv_done, min(H * (j + 1), NU))
                sums = expsum[:, j * H:(j + 1) * H]
                then(V.reciprocal(inv_sum, sums))
                if j == 0:
                    dve.wait_ge(kstate_stored, 16)
                if j >= 2:
                    dve.wait_ge(att_turned, j - 1)
                V.tensor_tensor(att[j % 2].rearrange("p (h d) -> p h d", d=DH),
                                ps[:, 5 + j % 2, :].rearrange("p (h d) -> p h d", d=DH),
                                inv_sum.unsqueeze(2).broadcast_to([128, H, DH]), ALU.mult).then_inc(att_scaled, 1)

            def copy_turned(j):
                dve.wait_ge(att_turned, j + 1)
                V.tensor_copy(attT[:, :, j * 128:(j + 1) * 128],
                              ps[:, 7, :].rearrange("p (k n) -> p k n", n=128)).then_inc(attT_ready, 1)

            def block_low_part(i):
                dve.wait_ge(block_high, i + 1)
                V.tensor_tensor(block_lo[i % 2], chunk_slot(C_GATES + i // 4)[:, :, i % 4 * 128:(i % 4 + 1) * 128],
                                block_hi[i % 2].bitcast(f32), ALU.subtract).then_inc(block_cut, 1)

            for u in range(NU):
                dve.wait_ge(scores_done, u + 1)
                s = ps[:, u % 3, :]
                if u < UNITS:
                    j, h = divmod(u, H)
                    then(V.tensor_tensor(s[:, 0:256], s[:, 0:256],
                                         bias[:, BIAS_VARIANT[j] * H + h].rearrange("p c r -> p (c r)"), ALU.add))
                    V.tensor_reduce(negmax[:, u:u + 1], s, AX, ALU.max, negate=True).then_inc(max_ready, 1)
                else:
                    V.tensor_reduce(negmax_c[:, u - UNITS:H:2], s.rearrange("p (h n) -> p h n", n=128), AX, ALU.max,
                                    negate=True).then_inc(max_ready, 1)
                if u >= 10 and u % H == 2 and u < NU - 1:
                    finish_tile(u // H - 1)
                if u >= 12 and u % H == 5:
                    copy_turned(u // H - 1)
            finish_tile(3)
            copy_turned(3)
            finish_tile(4)
            block_low_part(0)
            copy_turned(4)
            block_low_part(1)

            V.memset(u_lat[:, :, :], 0.0).then_inc(halo_ready, 1)
            V.memset(u_ctx[:, :, :], 0.0).then_inc(halo_ready, 1)
            for g in range(4):
                block_low_part(g + 2)
                dve.wait_ge(gate_copied, 2 * (g + 1))
                for u_set, L, order in ((u_lat, LAT, True), (u_ctx, CTX, False)):
                    u, c = u_set[:, g, :], POOL_HALO
                    w, reach = 1, POOL_HALO - 1
                    then(V.tensor_tensor(win[0][:, 1:L + 2 * c], u[:, 0:L + 2 * c - 1], u[:, 1:L + 2 * c], ALU.add))
                    lo, hi, cur = 1, L + 2 * c, 0
                    for n in range(g):
                        sh = 1 << n
                        then(V.tensor_tensor(win[1 - cur][:, lo + sh:hi - sh], win[cur][:, lo:hi - 2 * sh],
                                             win[cur][:, lo + 2 * sh:hi], ALU.add))
                        lo, hi, cur = lo + sh, hi - sh, 1 - cur
                    f = win[cur]
                    then(V.tensor_tensor(f[:, c:c + 8], f[:, c:c + 8], pool_fix[:, g, 0, :], ALU.mult))
                    then(V.tensor_tensor(f[:, c + L - 8:c + L], f[:, c + L - 8:c + L], pool_fix[:, g, 1, :], ALU.mult))
                    if order:
                        dst = pooledT[:, g, 0:LAT].rearrange("p (c r) -> p r c", r=GRID_R)
                        fi = f[:, c:c + L].rearrange("p (r c) -> p r c", c=GRID_W)
                        ui = u[:, c:c + L].rearrange("p (r c) -> p r c", c=GRID_W)
                    else:
                        dst, fi, ui = pooledT[:, g, LAT:TOK], f[:, c:c + L], u[:, c:c + L]
                    V.scalar_tensor_tensor(dst, fi, 1.0 / (2 << g), ui, ALU.mult, ALU.subtract
                                           ).then_inc(pooled_ready, 1)
                    dve.wait_ge(pooled_ready, 2 * g + (1 if order else 2))
            for i in range(6, 20):
                block_low_part(i)
            dve.wait_ge(mod_turned, GATE1_END)
            then(V.tensor_tensor(modT[:, 16:24, :], ps[:, 0, 32:48].rearrange("p (n c) -> p n c", c=2),
                                 b_ada[:, 16:24].unsqueeze(2).broadcast_to([128, 8, 2]), ALU.add))
            for i in range(4):
                if i >= 2:
                    dve.wait_ge(row_done, i - 1)
                cols = modT[:, 16 + i % 2 * 4:20 + i % 2 * 4, i // 2:i // 2 + 1]
                V.tensor_tensor(diag[i % 2], ident.unsqueeze(1).broadcast_to([128, 4, 128]),
                                cols.broadcast_to([128, 4, 128]), ALU.mult).then_inc(diag_ready, 1)
            dve.wait_ge(mod_turned, C_QKV + len(ADA2))
            then(V.tensor_tensor(modT[:, 24:40, :], ps[:, 6, 48:80].rearrange("p (n c) -> p n c", c=2),
                                 b_ada[:, 24:40].unsqueeze(2).broadcast_to([128, 16, 2]), ALU.add))
            V.scalar_tensor_tensor(scale2[:, :, :], modT[:, 32:40, :], 1.0,
                                   vecT[:, 24:32].unsqueeze(2).broadcast_to([128, 8, 2]), ALU.add, ALU.mult
                                   ).then_inc(mod_ready, 1)

            def merged_low_part(n):
                dve.wait_ge(merged_high, n + 1)
                V.tensor_tensor(merged_lo[:, n, :], gaT[:, n, :], merged_hi[:, n, :].bitcast(f32), ALU.subtract
                                ).then_inc(merged_cut, 1)

            for n in range(KD):
                dve.wait_ge(branches_done, n + 1)
                b = n % 2 * 4
                for o, m, w in ((0, LAT, 0), (LAT, CTX, 1)):
                    V.tensor_tensor(gaT[:, n, o:o + m], gaT[:, n, o:o + m], ps[:, b + w, 0:m], ALU.mult)
                    then(V.scalar_tensor_tensor(gbT[:, n, o:o + m], ps[:, b + 2 + w, 0:m], vecT[:, 32 + n:33 + n],
                                                gbT[:, n, o:o + m], ALU.mult, ALU.mult))
                V.tensor_tensor(gaT[:, n, :], gaT[:, n, :], gbT[:, n, :], ALU.add).then_inc(merged, 1)
                if n:
                    merged_low_part(n - 1)
            merged_low_part(KD - 1)
            for k in range(KD):
                out_low_part(dve, V, 1, k)
            dve.wait_ge(row_copied, 4)
            for t in range(NT):
                for half in range(2):
                    dve.wait_ge(out_done, 2 * t + half + 1)
                    cols = slice(half * 512, (half + 1) * 512)
                    then(V.tensor_tensor(gated[:, cols], ps[:, t % 2 * 2 + half, :], gate1_row[:, int(t == 4), cols],
                                         ALU.mult))
                    last = V.tensor_tensor(x[:, t, cols], x[:, t, cols], gated[:, cols], ALU.add)
                last.then_inc(x2_ready, 1)
                dve.wait_ge(squared2, t + 1)
                V.tensor_scalar(ss2[:, t:t + 1], ss2[:, t:t + 1], 1.0 / D, EPS, ALU.mult, ALU.add
                                ).then_inc(ms2_ready, 1)
                dve.wait_ge(root2, t + 1)
                then(V.reciprocal(rs2[:, t:t + 1], rs2[:, t:t + 1]))
                if t >= 2:
                    dve.wait_ge(rows_saved[t % 2], 16 * (t // 2))
                    dve.wait_ge(xn2_turned, t - 1)
                V.tensor_scalar(xn2[t % 2], x[:, t, :], rs2[:, t:t + 1], None, ALU.mult).then_inc(xn2_ready, 1)
            dve.wait_ge(logits_done, NT)
            logits = ps[:, 6, 0:NT * NE].rearrange("p (t n) -> p t n", n=NE)
            then(V.tensor_reduce(rmax, logits, AX, ALU.max))
            V.tensor_tensor(aff, logits, rmax.unsqueeze(2).broadcast_to([128, NT, NE]), ALU.subtract
                            ).then_inc(max2_ready, 1)
            dve.wait_ge(exp2_ready, 1)
            then(V.tensor_reduce(rsum, aff, AX, ALU.add))
            then(V.reciprocal(rsum, rsum))
            V.tensor_tensor(aff, aff, rsum.unsqueeze(2).broadcast_to([128, NT, NE]), ALU.mult
                            ).then_inc(aff_ready, 1)
            dve.wait_ge(aff_turned, 1)
            V.tensor_copy(affN[:, 0:LAT].rearrange("p (r c) -> p r c", c=GRID_W),
                          ps[0:NE, 7, :].rearrange("p (c r) -> p r c", r=GRID_R))
            then(V.tensor_copy(affN[:, LAT:TOK], ps[0:NE, 4, 0:CTX]))
            for o, m, s0, cap in ((0, LAT, 0, CAP_L), (LAT, CTX, CAP_L, CAP_C)):
                src, dst = affN[:, o:o + m], left[:, o:o + m]
                for n in range(s0, s0 + cap, 8):
                    then(V.max(best[:, n:n + 8], src))
                    V.max_index(found[:, n:n + 8], best[:, n:n + 8], src)
                    then(V.match_replace(dst, best[:, n:n + 8], src, -1.0))
                    src = dst
            lat = found[:, 0:CAP_L]
            then(V.tensor_scalar(found_col[:, 0:CAP_L], lat, GRID_W - 1, 3, ALU.bitwise_and, ALU.logical_shift_left))
            then(V.tensor_scalar(lat, lat, 6, None, ALU.logical_shift_right))
            then(V.tensor_tensor(lat, lat, found_col[:, 0:CAP_L], ALU.bitwise_or))
            then(V.tensor_copy(best_place, found))
            V.tensor_scalar(best_place[:, CAP_L:SLOTS], best_place[:, CAP_L:SLOTS], float(LAT), None, ALU.add
                            ).then_inc(best_ready, 1)
            dve.wait_ge(best_turned, 1)
            V.tensor_copy(places[:, 0:NE], ps[0:SLOTS, 5, NE:2 * NE])
            then(V.memset(places[:, NE:NE + 2], 0.0))
            then(V.tensor_copy(places_int[:, :], places[:, :]))
            V.tensor_copy(place_now[:, :], places_int[:, 0:1]).then_inc(place_ready, 1)
            V.memset(gates[:, 0:1], 0.0)
            then(V.tensor_copy(gates[:, 1:NE + 1], ps[0:SLOTS, 5, 0:NE]))
            then(V.memset(ps[0:SLOTS, 4:6, :], 0.0))
            dve.wait_ge(rows_saved[0], 16 * 3)
            dve.wait_ge(rows_saved[1], 16 * 2)
            V.memset(back[:, :].bitcast(f32), 0.0).then_inc(back_ready, 1)
            dve.wait_ge(gate2_ready, 2)
            dve.sem_inc(pieces_used, WBUF)
            dve.sem_inc(scattered, 2 * NT)
            dve.sem_inc(added, 1)
            dve.sem_inc(h_turned, NCH)

            def fit_columns(e):
                dve.wait_ge(xe_turned, e + 1)
                X = ps[:, 0:3:2, 0:4 * SLOTS].rearrange("p a (k s) -> p a k s", s=SLOTS)
                xe4 = xe_f.rearrange("p (a k) s -> p a k s", a=2)
                for s, (o, m) in enumerate(((0, CAP_L), (CAP_L, CAP_C))):
                    last = V.tensor_tensor(xe4[:, :, :, o:o + m], X[:, :, :, o:o + m],
                                           scale2[:, :, s:s + 1].rearrange("p (a k) o -> p a k o", a=2)
                                           .broadcast_to([128, 2, 4, m]), ALU.mult)
                last.then_inc(xe_scaled, 1)
                dve.wait_ge(xe_scaled, e + 1)
                for s, (o, m) in enumerate(((0, CAP_L), (CAP_L, CAP_C))):
                    last = V.tensor_tensor(xe_f[:, :, o:o + m], xe_f[:, :, o:o + m],
                                           modT[:, 24:32, s:s + 1].broadcast_to([128, 8, m]), ALU.add)
                last.then_inc(xe_mod, 1)

            def hidden(e, c):
                dve.wait_ge(pieces_used, WBUF + e * NP + LAST["up", c] + 1)
                dve.wait_ge(silu_ready, e * NCH + c + 1)
                h = hid[:, c % 2, 0:width(c)]
                V.tensor_tensor(h, h, ps[0:SLOTS, 2 + c % 2, 0:width(c)], ALU.mult).then_inc(h_done, 1)

            def low_hidden(e, c):
                dve.wait_ge(h_high, e * NCH + c + 1)
                kb, nb = fblocks(c)[0][1], len(fblocks(c))
                V.tensor_tensor(hT_lo[0:kb, c % 2, 0:nb, :],
                                ps[0:kb, 6, 0:nb * SLOTS].rearrange("p (b s) -> p b s", s=SLOTS),
                                hT_hi[0:kb, c % 2, 0:nb, :].bitcast(f32), ALU.subtract).then_inc(hT_ready, 1)

            def scale_rows(e):
                dve.wait_ge(pieces_used, WBUF + e * NP)
                dve.wait_ge(xe_ready, e + 1)
                V.scalar_tensor_tensor(y_f[0:SLOTS, :].rearrange("p (a n) -> p a n", a=2), ps[0:SLOTS, 4:6, :],
                                       gates[:, ds(e, 1)], gate2_row[:, :].rearrange("p (a n) -> p a n", a=2),
                                       ALU.mult, ALU.mult).then_inc(y_scaled, 1)

            def add_back(e, i, bank=7):
                dve.wait_ge(scattered, 2 * NT + e * 2 * NT + i + 1)
                t, half = divmod(i, 2)
                xt = x[:, t, half * 512:(half + 1) * 512]
                V.tensor_tensor(xt, xt, ps[:, bank, :], ALU.add).then_inc(added, 1)

            fit_columns(0)
            dve.wait_ge(gathered, 16)
            V.tensor_copy(place_now[:, :], places_int[:, 1:2]).then_inc(place_ready, 1)
            with dve.Fori(0, NE) as e:
                for p, (j, kind, c, b0, nb) in enumerate(PIECES):
                    rows_, n = piece_shape(p)
                    dve.wait_ge(hi_ready, e * NP + p + 1)
                    V.tensor_tensor(w_lo[0:rows_, p % WBUF, 0:n], piece(p), w_hi[0:rows_, p % WBUF, 0:n].bitcast(f32),
                                    ALU.subtract).then_inc(lo_ready, 1)
                    if p == SCALE_AT:
                        scale_rows(e)
                    if 0 <= p - SCATTER_AT - 1 < 2 * NT:
                        add_back(e, p - SCATTER_AT - 1)
                    for cc in range(NCH):
                        if p == LAST["up", cc] + (2 if cc < NCH - 1 else 1):
                            hidden(e, cc)
                        if cc < NCH - 1 and p == LAST["up", cc + 1]:
                            low_hidden(e, cc)
                    if p == SCATTER_AT + 2 * NT + 2:
                        dve.wait_ge(iota_loaded, 16)
                        V.tensor_scalar(back[:, :], iota[:, :], places[:, ds(e, 1)], None, ALU.is_equal
                                        ).then_inc(back_ready, 1)
                        dve.wait_ge(gathered, 16 * (e + 2))
                        V.tensor_copy(place_now[:, :], places_int[:, ds(e + 2, 1)]).then_inc(place_ready, 1)
                    if p == FIRST["down", NCH - 2]:
                        fit_columns(e + 1)
                    if p == FIRST["down", NCH - 1]:
                        low_hidden(e, NCH - 1)
            scale_rows(NE)
            dve.wait_ge(y_high, NE + 1)
            V.tensor_tensor(y_lo[:, :], y_f[0:SLOTS, :], y_hi[:, :].bitcast(f32), ALU.subtract).then_inc(y_ready, 1)
            for i in range(2 * NT):
                add_back(NE, i, i % 4)

        @block.gpsimd
        def _(pool):
            pool.wait_ge(wide_loaded, 16 * GRID_R * H)
            pool.wait_ge(consts_loaded, 32)
            for v in range(3):
                for h in range(H):
                    last = nc.gpsimd.tensor_tensor(
                        bias[:, v * H + h], rpb_wide[:, h, :, 8 * v:32 + 8 * v][:, :, ::-1].rearrange("p r c -> p c r"),
                        mask[:, v, :].unsqueeze(2).broadcast_to([128, 32, GRID_R]), ALU.add)
                last.then_inc(bias_ready, 1)
            G = nc.gpsimd
            pool.wait_ge(qkT_ready, 2 * NT)
            pool.wait_ge(bias_ready, 3)
            G.memset(q_apart[DH:128, :, 0], 0.0).then_inc(pool_step, 1)
            pool.wait_ge(pool_step, 1)
            G.memset(q_apart[0:DH, :, 1], 0.0).then_inc(pool_step, 1)
            for j in range(NT):
                pool.wait_ge(pool_step, 2 + j)
                if j >= 2:
                    pool.wait_ge(scores_done, H * (j - 1))
                t = slice(j * 128, (j + 1) * 128)
                G.tensor_copy(q_apart[0:DH, j % 2, 0], qT[0:DH, :, t]).then_inc(pool_step, 1)
                pool.wait_ge(pool_step, 3 + j)
                G.tensor_copy(q_apart[DH:128, j % 2, 1], qT[DH:128, :, t]).then_inc(q_spread, 1)
                pool.wait_ge(q_spread, j + 1)
            for k in range(4):
                pool.wait_ge(att_high, k + 1)
                G.tensor_tensor(att_lo[:, k, :], attT[:, k, 0:LAT], att_hi[k].bitcast(f32), ALU.subtract
                                ).then_inc(att_cut, 1)
            for n in range(KD):
                pool.wait_ge(wa_high, n + 1)
                cols = stream[SLOT_OF[C_TAIL]].rearrange("p (k n) -> p k n", n=D)[:, :, n * 128:(n + 1) * 128]
                G.tensor_tensor(wa_lo[n % 2], cols, wa_hi[n % 2].bitcast(f32), ALU.subtract).then_inc(wa_cut, 1)
                out_low_part(pool, G, 0, n)
            pool.wait_ge(rows_saved[0], 16 * 3)
            pool.wait_ge(rows_saved[1], 16 * 2)

            def gather(e):
                pool.wait_ge(place_ready, e + 1)
                pool.sem_inc(gathers_begun, 1)
                nc.gpsimd.indirect_dma_start(
                    out=x_rows[:, :], out_offset=None, in_=xn_rows,
                    in_offset=bass.IndirectOffsetOnAxis(ap=place_now[:, 0:1], axis=0)).then_inc(gathered, 16)

            def low_columns(e):
                pool.wait_ge(xe_high, e + 1)
                G.tensor_tensor(xe_lo[:, :, :], xe_f, xe_hi[:, :, :].bitcast(f32), ALU.subtract).then_inc(xe_ready, 1)

            def low_rows(e):
                pool.wait_ge(y_high, e + 1)
                G.tensor_tensor(y_lo[:, :], y_f[0:SLOTS, :], y_hi[:, :].bitcast(f32), ALU.subtract
                                ).then_inc(y_ready, 1)

            gather(0)
            with pool.Fori(0, NE) as e:
                pool.wait_ge(xe_turned, e + 1)
                gather(e + 1)
                low_columns(e)
                low_rows(e)
            low_columns(NE)


def _constants():
    keep = np.eye(128, dtype=np.float32)
    mixer = np.zeros((128, 448), np.float32)
    for v, (j, base) in enumerate(((0, 0), (1, 8), (3, 32))):
        qc = 16 * j + np.arange(128)[:, None] // 8
        kc = base + np.arange(32)[None, :]
        start = np.clip(qc - 8, 0, 48)
        mixer[:, v * 32:(v + 1) * 32] = np.where((kc >= start) & (kc < start + 16), 0.0, -1e30)
    fix = np.ones((4, 2, 8), np.float64)
    for g in range(4):
        w = 2 << g
        for i in range(8):
            fix[g, 0, i] = w / (i + w - w // 2 - max(i - w // 2, 0))
            fix[g, 1, i] = w / (min(i - 8 + w - w // 2, 0) - (i - 8 - w // 2))
    mixer[:, 96:160] = fix.reshape(1, 64)
    mixer[:, 160:288] = 1.0
    mixer[0, 288:288 + CAP_L] = 1.0
    mixer[1, 288 + CAP_L:288 + SLOTS] = 1.0
    iota = np.tile(np.arange(TOK, dtype=np.float32), (SLOTS, 1))
    return {"const_keep": keep, "const_mixer": mixer, "const_iota": iota}


_OUTS = {"y_prompt": (1, CTX, D), "y_sample": (1, LAT, D), "state_k": (CTX, H * DH), "state_v": (CTX, H * DH)}


def kernel(**inputs):
    import concourse.bacc as bacc
    from concourse.bass_utils import run_bass_kernel_spmd

    nc = bacc.Bacc("TRN2", target_bir_lowering=False, num_devices=1)
    arrays, a, out = {}, {}, {}
    inputs = {**inputs, "rpb": np.asarray(inputs["rpb"])[..., ::-1]}
    for name, v in {**inputs, **_constants()}.items():
        v = np.ascontiguousarray(v)
        arrays[f"in_{name}"] = v
        a[name] = nc.dram_tensor(f"in_{name}", v.shape, mybir.dt.from_np(v.dtype), kind="ExternalInput").ap()
    for name, shape in _OUTS.items():
        out[name] = nc.dram_tensor(f"out_{name}", shape, mybir.dt.float32, kind="ExternalOutput").ap()
    step_kernel(nc, a, out)
    r = run_bass_kernel_spmd(nc, [arrays], core_ids=[0]).results[0]
    state = (1, 1, CTX, H, DH)
    return (r["out_y_prompt"], r["out_y_sample"], r["out_state_k"].reshape(state), r["out_state_v"].reshape(state))
```
